# Optimizing a Trainium2 kernel written in Bass

```python
import jax, jax.numpy as jnp
from jax import lax
import numpy as np

D_MODEL = 1024
BATCH = 1
SEQ = 256
DEPTH = 2

PLE_DIM = 256
D_FF = 2816
LN_EPS = 1e-5
RMS_EPS = 1e-6
DEEPNORM_ALPHA = (2 * DEPTH) ** 0.25
DEEPNORM_BETA = (8 * DEPTH) ** -0.25

GDN_HEADS = 8
GDN_DK = 64
GDN_DV = 64
GDN_CONV = 4
GDN_CHUNK = 64

SB_HEADS = 4
SB_DIM = 64

MLA_HEADS = 4
MLA_NOPE = 64
MLA_ROPE = 32
MLA_V = 64
MLA_Q_RANK = 256
MLA_KV_RANK = 128
ROPE_BASE = 10000.0

Q_BLOCK = 128

MIX_WIDTH = GDN_HEADS * GDN_DV + SB_HEADS * SB_DIM + MLA_HEADS * MLA_V
IN_WIDTHS = (
    GDN_HEADS * GDN_DK, GDN_HEADS * GDN_DK, GDN_HEADS * GDN_DV,
    GDN_HEADS * GDN_DV,
    GDN_HEADS, GDN_HEADS,
    SB_HEADS * SB_DIM, SB_HEADS * SB_DIM, SB_HEADS * SB_DIM,
    MLA_Q_RANK,
    MLA_KV_RANK + MLA_ROPE,
)
IN_TOTAL = int(sum(IN_WIDTHS))
IN_SPLITS = tuple(int(s) for s in np.cumsum(IN_WIDTHS)[:-1])
GDN_CONV_CH = 2 * GDN_HEADS * GDN_DK + GDN_HEADS * GDN_DV


def layer_norm(x, g, b):
    xf = x.astype(jnp.float32)
    mu = jnp.mean(xf, axis=-1, keepdims=True)
    var = jnp.mean(jnp.square(xf - mu), axis=-1, keepdims=True)
    y = (xf - mu) * lax.rsqrt(var + LN_EPS)
    return (y * g.astype(jnp.float32) + b.astype(jnp.float32)).astype(x.dtype)

def rms_norm(x, w):
    xf = x.astype(jnp.float32)
    y = xf * lax.rsqrt(jnp.mean(jnp.square(xf), axis=-1, keepdims=True) + RMS_EPS)
    return (y * w.astype(jnp.float32)).astype(x.dtype)

def l2_normalize(x):
    xf = x.astype(jnp.float32)
    return xf * lax.rsqrt(jnp.sum(jnp.square(xf), axis=-1, keepdims=True) + RMS_EPS)

def swiglu(h, w_in, w_out):
    gate, up = jnp.split(h @ w_in, 2, axis=-1)
    return (jax.nn.silu(gate) * up) @ w_out

def causal_depthwise_conv(x, w):
    k_width, ch = w.shape
    return lax.conv_general_dilated(
        x, w[:, None, :].astype(x.dtype), window_strides=(1,), padding=[(k_width - 1, 0)],
        dimension_numbers=("NWC", "WIO", "NWC"), feature_group_count=ch)

def rope_tables(positions):
    inv = 1.0 / (ROPE_BASE ** (jnp.arange(0, MLA_ROPE, 2, dtype=jnp.float32) / MLA_ROPE))
    ang = positions.astype(jnp.float32)[..., None] * inv
    return jnp.cos(ang), jnp.sin(ang)

def apply_rope(x, cos, sin):
    x1, x2 = jnp.split(x.astype(jnp.float32), 2, axis=-1)
    return jnp.concatenate([x1 * cos - x2 * sin, x2 * cos + x1 * sin], axis=-1).astype(x.dtype)

def chunk_gated_delta_rule(q, k, v, g, beta):
    B, S, H, DK = q.shape
    DV = v.shape[-1]
    C = GDN_CHUNK
    N = S // C
    f32 = jnp.float32

    def chunks(t):
        t = t.astype(f32).reshape((B, N, C) + t.shape[2:])
        return jnp.moveaxis(jnp.moveaxis(t, 3, 2), 1, 0)

    qc, kc, vc, gc, bc = (chunks(t) for t in (q, k, v, g, beta))
    gc = jnp.cumsum(gc, axis=-1)
    incl = jnp.tril(jnp.ones((C, C), dtype=bool))
    strict = jnp.tril(jnp.ones((C, C), dtype=bool), -1)
    diff = gc[..., :, None] - gc[..., None, :]
    decay = jnp.where(incl, jnp.exp(jnp.where(incl, diff, 0.0)), 0.0)
    kb = kc * bc[..., None]
    lhs = jnp.where(strict, jnp.einsum('nbhid,nbhjd->nbhij', kb, kc) * decay, 0.0) + jnp.eye(C, dtype=f32)
    u = lax.linalg.triangular_solve(lhs, vc * bc[..., None], left_side=True, lower=True, unit_diagonal=True)
    w = lax.linalg.triangular_solve(lhs, kb * jnp.exp(gc)[..., None], left_side=True, lower=True, unit_diagonal=True)
    qk = jnp.where(incl, jnp.einsum('nbhid,nbhjd->nbhij', qc, kc) * decay, 0.0)
    q_dec = qc * jnp.exp(gc)[..., None]
    k_dec = kc * jnp.exp(gc[..., -1:] - gc)[..., None]
    g_last = jnp.exp(gc[..., -1])

    def step(state, xs):
        u_n, w_n, qk_n, qd_n, kd_n, gl_n = xs
        v_new = u_n - jnp.einsum('bhck,bhkv->bhcv', w_n, state)
        o_n = jnp.einsum('bhck,bhkv->bhcv', qd_n, state) + jnp.einsum('bhij,bhjv->bhiv', qk_n, v_new)
        state = state * gl_n[..., None, None] + jnp.einsum('bhck,bhcv->bhkv', kd_n, v_new)
        return state, o_n

    s0 = jnp.zeros((B, H, DK, DV), f32)
    _, o = lax.scan(step, s0, (u, w, qk, q_dec, k_dec, g_last))
    return jnp.transpose(o, (1, 0, 3, 2, 4)).reshape(B, S, H, DV)

def gated_deltanet(gq, gk, gv, gz, ga, gb, conv_w, a_log, dt_bias, norm_w):
    B, S, _ = gq.shape
    f32 = jnp.float32
    qkv = jax.nn.silu(causal_depthwise_conv(jnp.concatenate([gq, gk, gv], axis=-1), conv_w))
    q, k, v = jnp.split(qkv, [GDN_HEADS * GDN_DK, 2 * GDN_HEADS * GDN_DK], axis=-1)
    q = l2_normalize(q.reshape(B, S, GDN_HEADS, GDN_DK)) * (GDN_DK ** -0.5)
    k = l2_normalize(k.reshape(B, S, GDN_HEADS, GDN_DK))
    v = v.reshape(B, S, GDN_HEADS, GDN_DV)
    beta = jax.nn.sigmoid(gb.astype(f32))
    g = -jnp.exp(a_log.astype(f32)) * jax.nn.softplus(ga.astype(f32) + dt_bias.astype(f32))
    o = chunk_gated_delta_rule(q, k, v, g, beta)
    o = rms_norm(o, norm_w) * jax.nn.silu(gz.reshape(B, S, GDN_HEADS, GDN_DV).astype(f32))
    return o.reshape(B, S, GDN_HEADS * GDN_DV).astype(gq.dtype)

def to_query_blocks(t):
    B, S = t.shape[:2]
    return jnp.swapaxes(t.reshape((B, S // Q_BLOCK, Q_BLOCK) + t.shape[2:]), 0, 1)

def from_query_blocks(t):
    t = jnp.swapaxes(t, 0, 1)
    return t.reshape((t.shape[0], t.shape[1] * t.shape[2]) + t.shape[3:])

def stick_breaking_attention(q, k, v):
    S = q.shape[1]
    scale = SB_DIM ** -0.5
    kpos = jnp.arange(S)

    def block(args):
        qb, i = args
        z = jnp.einsum('bqhd,bkhd->bhqk', qb, k).astype(jnp.float32) * scale
        qpos = i * Q_BLOCK + jnp.arange(Q_BLOCK)
        mask = kpos[None, :] < qpos[:, None]
        log_1m = jnp.where(mask, jax.nn.log_sigmoid(-z), 0.0)
        rest = lax.cumsum(log_1m, axis=3, reverse=True) - log_1m
        wts = jnp.where(mask, jnp.exp(jax.nn.log_sigmoid(z) + rest), 0.0)
        return jnp.einsum('bhqk,bkhd->bqhd', wts.astype(v.dtype), v)

    nb = S // Q_BLOCK
    out = lax.map(block, (to_query_blocks(q), jnp.arange(nb)))
    return from_query_blocks(out)

def mla_attention(q_nope, q_rope, k_nope, k_rope, v):
    S = q_nope.shape[1]
    scale = (MLA_NOPE + MLA_ROPE) ** -0.5
    kpos = jnp.arange(S)

    def block(args):
        qn, qr, i = args
        s = (jnp.einsum('bqhd,bkhd->bhqk', qn, k_nope) + jnp.einsum('bqhd,bkd->bhqk', qr, k_rope)).astype(jnp.float32) * scale
        qpos = i * Q_BLOCK + jnp.arange(Q_BLOCK)
        s = jnp.where(kpos[None, :] <= qpos[:, None], s, -jnp.inf)
        pr = jax.nn.softmax(s, axis=-1)
        return jnp.einsum('bhqk,bkhd->bqhd', pr.astype(v.dtype), v)

    nb = S // Q_BLOCK
    out = lax.map(block, (to_query_blocks(q_nope), to_query_blocks(q_rope), jnp.arange(nb)))
    return from_query_blocks(out)

def hybrid_mixer(h, cos, sin, w_in, conv_w, a_log, dt_bias, gdn_norm_w, q_norm_w, kv_norm_w, w_uq, w_ukv, w_o):
    B, S, _ = h.shape
    proj = h @ w_in
    gq, gk, gv, gz, ga, gb, sq, sk, sv, mq, mkv = jnp.split(proj, IN_SPLITS, axis=-1)
    o_gdn = gated_deltanet(gq, gk, gv, gz, ga, gb, conv_w, a_log, dt_bias, gdn_norm_w)
    shp = (B, S, SB_HEADS, SB_DIM)
    o_sb = stick_breaking_attention(sq.reshape(shp), sk.reshape(shp), sv.reshape(shp)).reshape(B, S, SB_HEADS * SB_DIM)
    qf = (rms_norm(mq, q_norm_w) @ w_uq).reshape(B, S, MLA_HEADS, MLA_NOPE + MLA_ROPE)
    q_nope, q_rope = jnp.split(qf, [MLA_NOPE], axis=-1)
    ckv, k_rope = jnp.split(mkv, [MLA_KV_RANK], axis=-1)
    kvf = (rms_norm(ckv, kv_norm_w) @ w_ukv).reshape(B, S, MLA_HEADS, MLA_NOPE + MLA_V)
    k_nope, v_mla = jnp.split(kvf, [MLA_NOPE], axis=-1)
    q_rope = apply_rope(q_rope, cos[:, :, None, :], sin[:, :, None, :])
    k_rope = apply_rope(k_rope, cos, sin)
    o_mla = mla_attention(q_nope, q_rope, k_nope, k_rope, v_mla).reshape(B, S, MLA_HEADS * MLA_V)
    return jnp.concatenate([o_gdn, o_sb, o_mla], axis=-1) @ w_o

def first_inputs(seed: int = 0) -> dict:
    key = jax.random.key(seed)
    ks = jax.random.split(key, 24)
    f32 = jnp.float32
    L = DEPTH

    def nrm(k, shape, scale):
        return jax.random.normal(k, shape, f32) * scale

    x = nrm(ks[0], (BATCH, SEQ, D_MODEL), 1.0)
    p = nrm(ks[1], (DEPTH, BATCH, SEQ, PLE_DIM), 1.0)
    positions = (jnp.arange(SEQ, dtype=jnp.int32)[None, :]
                 + jax.random.randint(ks[2], (BATCH, 1), 0, 1024, dtype=jnp.int32))
    a_init = jax.random.uniform(ks[7], (L, GDN_HEADS), f32, 1.0, 16.0)
    dt = jnp.exp(jax.random.uniform(ks[8], (L, GDN_HEADS), f32, np.log(1e-3), np.log(1e-1)))
    return {
        "x": x,
        "p": p,
        "positions": positions,
        "ffa_w_in": nrm(ks[3], (L, D_MODEL, 2 * D_FF), D_MODEL ** -0.5),
        "ffa_w_out": nrm(ks[4], (L, D_FF, D_MODEL), D_FF ** -0.5 * DEEPNORM_BETA),
        "mix_w_in": nrm(ks[5], (L, D_MODEL, IN_TOTAL), D_MODEL ** -0.5),
        "gdn_conv_w": nrm(ks[6], (L, GDN_CONV, GDN_CONV_CH), GDN_CONV ** -0.5),
        "gdn_a_log": jnp.log(a_init),
        "gdn_dt_bias": dt + jnp.log(-jnp.expm1(-dt)),
        "gdn_norm_w": 1.0 + nrm(ks[9], (L, GDN_DV), 0.02),
        "mla_q_norm_w": 1.0 + nrm(ks[10], (L, MLA_Q_RANK), 0.02),
        "mla_kv_norm_w": 1.0 + nrm(ks[11], (L, MLA_KV_RANK), 0.02),
        "mla_w_uq": nrm(ks[12], (L, MLA_Q_RANK, MLA_HEADS * (MLA_NOPE + MLA_ROPE)), MLA_Q_RANK ** -0.5),
        "mla_w_ukv": nrm(ks[13], (L, MLA_KV_RANK, MLA_HEADS * (MLA_NOPE + MLA_V)), MLA_KV_RANK ** -0.5),
        "mix_w_o": nrm(ks[14], (L, MIX_WIDTH, D_MODEL), MIX_WIDTH ** -0.5 * DEEPNORM_BETA),
        "ffb_w_in": nrm(ks[15], (L, D_MODEL, 2 * D_FF), D_MODEL ** -0.5),
        "ffb_w_out": nrm(ks[16], (L, D_FF, D_MODEL), D_FF ** -0.5 * DEEPNORM_BETA),
        "ln_g": 1.0 + nrm(ks[17], (L, 3, D_MODEL), 0.02),
        "ln_b": nrm(ks[18], (L, 3, D_MODEL), 0.02),
        "ple_w_gate": nrm(ks[19], (L, D_MODEL, D_MODEL), D_MODEL ** -0.5),
        "ple_w_proj": nrm(ks[20], (L, PLE_DIM, D_MODEL), PLE_DIM ** -0.5 * DEEPNORM_BETA),
    }

def first_block(x, p, positions, ffa_w_in, ffa_w_out, mix_w_in, gdn_conv_w, gdn_a_log, gdn_dt_bias,
              gdn_norm_w, mla_q_norm_w, mla_kv_norm_w, mla_w_uq, mla_w_ukv, mix_w_o,
              ffb_w_in, ffb_w_out, ln_g, ln_b, ple_w_gate, ple_w_proj):
    cos, sin = rope_tables(positions)
    h = x
    for i in range(DEPTH):
        h = layer_norm(DEEPNORM_ALPHA * h + 0.5 * swiglu(h, ffa_w_in[i], ffa_w_out[i]), ln_g[i, 0], ln_b[i, 0])
        mix = hybrid_mixer(h, cos, sin, mix_w_in[i], gdn_conv_w[i], gdn_a_log[i], gdn_dt_bias[i], gdn_norm_w[i],
                           mla_q_norm_w[i], mla_kv_norm_w[i], mla_w_uq[i], mla_w_ukv[i], mix_w_o[i])
        h = layer_norm(DEEPNORM_ALPHA * h + mix, ln_g[i, 1], ln_b[i, 1])
        h = layer_norm(DEEPNORM_ALPHA * h + 0.5 * swiglu(h, ffb_w_in[i], ffb_w_out[i]), ln_g[i, 2], ln_b[i, 2])
        h = h + jax.nn.sigmoid(h @ ple_w_gate[i]) * (p[i] @ ple_w_proj[i])
    return h


DEPTH_2 = 1

LRU_WIDTH = 1024
LRU_BLOCKS = 16
LRU_BLOCK_W = LRU_WIDTH // LRU_BLOCKS
CONV_WIDTH = 4
LRU_C = 8.0
HEAD_DIM = 64
N_Q_HEADS = 16
N_KV_HEADS = 4
Q_PER_KV = N_Q_HEADS // N_KV_HEADS
ATTN_WIDTH = N_Q_HEADS * HEAD_DIM
KV_WIDTH = N_KV_HEADS * HEAD_DIM
WINDOW = 128
BLOCK = 128
ROPE_THETA = 10000.0
MACARON_SCALE = 0.5
NORM_EPS = 1e-6
MASK_VALUE = -1e30
IN_WIDTH = 2 * LRU_WIDTH + ATTN_WIDTH + 2 * KV_WIDTH + 2 * D_MODEL
IN_SPLITS_2 = (
    LRU_WIDTH,
    2 * LRU_WIDTH,
    2 * LRU_WIDTH + ATTN_WIDTH,
    2 * LRU_WIDTH + ATTN_WIDTH + KV_WIDTH,
    2 * LRU_WIDTH + ATTN_WIDTH + 2 * KV_WIDTH,
    2 * LRU_WIDTH + ATTN_WIDTH + 2 * KV_WIDTH + D_MODEL,
)


def rms_norm_2(x, g):
    xf = x.astype(jnp.float32)
    y = xf * lax.rsqrt(jnp.mean(xf * xf, axis=-1, keepdims=True) + NORM_EPS)
    return (y * g.astype(jnp.float32)).astype(x.dtype)

def swiglu_2(x, w_gu, w_down):
    g, u = jnp.split(x @ w_gu, 2, axis=-1)
    return (jax.nn.silu(g) * u) @ w_down

def rope_tables_2(seq_len):
    half = HEAD_DIM // 2
    inv_freq = ROPE_THETA ** (-jnp.arange(half, dtype=jnp.float32) / half)
    ang = jnp.arange(seq_len, dtype=jnp.float32)[:, None] * inv_freq[None, :]
    return jnp.cos(ang), jnp.sin(ang)

def apply_rope_2(x, cos, sin):
    half = HEAD_DIM // 2
    xf = x.astype(jnp.float32)
    x1, x2 = xf[..., :half], xf[..., half:]
    c = cos[None, :, None, :]
    s = sin[None, :, None, :]
    return jnp.concatenate([x1 * c - x2 * s, x2 * c + x1 * s], axis=-1).astype(x.dtype)

def causal_depthwise_conv_2(x, w, b):
    s = x.shape[1]
    xp = jnp.pad(x, ((0, 0), (CONV_WIDTH - 1, 0), (0, 0)))
    y = xp[:, 0:s] * w[0]
    for k in range(1, CONV_WIDTH):
        y = y + xp[:, k:k + s] * w[k]
    return y + b

def block_diag_linear(x, w, b):
    bsz, s, _ = x.shape
    xb = x.reshape(bsz, s, LRU_BLOCKS, LRU_BLOCK_W)
    y = jnp.einsum('bsnc,ncd->bsnd', xb, w).reshape(bsz, s, LRU_WIDTH)
    return y + b

def rg_lru(x, w_a, b_a, w_x, b_x, lam):
    xf = x.astype(jnp.float32)
    r = jax.nn.sigmoid(block_diag_linear(x, w_a, b_a).astype(jnp.float32))
    i = jax.nn.sigmoid(block_diag_linear(x, w_x, b_x).astype(jnp.float32))
    log_a = -LRU_C * r * jax.nn.softplus(-lam.astype(jnp.float32))
    a = jnp.exp(log_a)
    mult = jnp.sqrt(jnp.maximum(-jnp.expm1(2.0 * log_a), 0.0))
    bterm = mult * (i * xf)

    def combine(left, right):
        a1, b1 = left
        a2, b2 = right
        return a1 * a2, a2 * b1 + b2

    _, h = lax.associative_scan(combine, (a, bterm), axis=1)
    return h.astype(x.dtype)

def band_blocks(t):
    bsz, s, h, d = t.shape
    tb = t.reshape(bsz, s // BLOCK, BLOCK, h, d)
    prev = jnp.pad(tb, ((0, 0), (1, 0), (0, 0), (0, 0), (0, 0)))[:, :-1]
    return jnp.concatenate([prev, tb], axis=2)

def sliding_window_attention_with_sinks(q, k, v, sinks):
    bsz, s = q.shape[0], q.shape[1]
    nb = s // BLOCK
    qb = q.reshape(bsz, nb, BLOCK, N_KV_HEADS, Q_PER_KV, HEAD_DIM)
    kb = band_blocks(k)
    vb = band_blocks(v)
    scores = jnp.einsum('bnqhgd,bnshd->bhgnqs', qb, kb).astype(jnp.float32) * (HEAD_DIM ** -0.5)
    qi = jnp.arange(BLOCK)[:, None]
    si = jnp.arange(2 * BLOCK)[None, :]
    diff = BLOCK + qi - si
    key_pos = (jnp.arange(nb)[:, None, None] - 1) * BLOCK + si[None]
    mask = ((diff >= 0) & (diff < WINDOW))[None] & (key_pos >= 0)
    scores = jnp.where(mask, scores, MASK_VALUE)
    sink = sinks.astype(jnp.float32).reshape(1, N_KV_HEADS, Q_PER_KV, 1, 1, 1)
    sink = jnp.broadcast_to(sink, scores.shape[:-1] + (1,))
    probs = jax.nn.softmax(jnp.concatenate([scores, sink], axis=-1), axis=-1)[..., :-1]
    out = jnp.einsum('bhgnqs,bnshd->bnqhgd', probs.astype(v.dtype), vb)
    return out.reshape(bsz, s, ATTN_WIDTH)

def hybrid_mixer_2(u, cos, sin, w_in, conv_w, conv_b, lru_w_a, lru_b_a, lru_w_x, lru_b_x,
                 lru_lambda, attn_sinks, w_proj_lru, w_proj_attn, w_out):
    bsz, s, _ = u.shape
    z = u @ w_in
    gate_br, x_br, q, k, v, g_lru, g_attn = jnp.split(z, IN_SPLITS_2, axis=-1)
    xc = causal_depthwise_conv_2(x_br, conv_w, conv_b)
    y_lru = rg_lru(xc, lru_w_a, lru_b_a, lru_w_x, lru_b_x, lru_lambda) * jax.nn.gelu(gate_br)
    q = apply_rope_2(q.reshape(bsz, s, N_Q_HEADS, HEAD_DIM), cos, sin)
    k = apply_rope_2(k.reshape(bsz, s, N_KV_HEADS, HEAD_DIM), cos, sin)
    v = v.reshape(bsz, s, N_KV_HEADS, HEAD_DIM)
    y_attn = sliding_window_attention_with_sinks(q, k, v, attn_sinks)
    merged = jax.nn.sigmoid(g_lru) * (y_lru @ w_proj_lru) + jax.nn.sigmoid(g_attn) * (y_attn @ w_proj_attn)
    return merged @ w_out

def second_inputs(seed: int = 0) -> dict:
    key = jax.random.key(seed)
    ks = jax.random.split(key, 24)

    def nrm(k, shape, scale):
        return jax.random.normal(k, shape, jnp.float32) * scale

    def gain(k, shape):
        return 1.0 + 0.05 * jax.random.normal(k, shape, jnp.float32)

    u = jax.random.uniform(ks[13], (DEPTH_2, LRU_WIDTH), jnp.float32, minval=0.9, maxval=0.999)
    a0 = u ** (1.0 / LRU_C)
    lam = jnp.log(a0) - jnp.log1p(-a0)
    return {
        "x": nrm(ks[0], (BATCH, SEQ, D_MODEL), 1.0),
        "ffn1_pre_g": gain(ks[1], (DEPTH_2, D_MODEL)),
        "ffn1_w_gu": nrm(ks[2], (DEPTH_2, D_MODEL, 2 * D_FF), D_MODEL ** -0.5),
        "ffn1_w_down": nrm(ks[3], (DEPTH_2, D_FF, D_MODEL), D_FF ** -0.5),
        "ffn1_post_g": gain(ks[4], (DEPTH_2, D_MODEL)),
        "mix_pre_g": gain(ks[5], (DEPTH_2, D_MODEL)),
        "w_in": nrm(ks[6], (DEPTH_2, D_MODEL, IN_WIDTH), D_MODEL ** -0.5),
        "conv_w": nrm(ks[7], (DEPTH_2, CONV_WIDTH, LRU_WIDTH), CONV_WIDTH ** -0.5),
        "conv_b": nrm(ks[8], (DEPTH_2, LRU_WIDTH), 0.01),
        "lru_w_a": nrm(ks[9], (DEPTH_2, LRU_BLOCKS, LRU_BLOCK_W, LRU_BLOCK_W), LRU_BLOCK_W ** -0.5),
        "lru_b_a": nrm(ks[10], (DEPTH_2, LRU_WIDTH), 0.01),
        "lru_w_x": nrm(ks[11], (DEPTH_2, LRU_BLOCKS, LRU_BLOCK_W, LRU_BLOCK_W), LRU_BLOCK_W ** -0.5),
        "lru_b_x": nrm(ks[12], (DEPTH_2, LRU_WIDTH), 0.01),
        "lru_lambda": lam,
        "attn_sinks": nrm(ks[14], (DEPTH_2, N_Q_HEADS), 0.5),
        "w_proj_lru": nrm(ks[15], (DEPTH_2, LRU_WIDTH, D_MODEL), LRU_WIDTH ** -0.5),
        "w_proj_attn": nrm(ks[16], (DEPTH_2, ATTN_WIDTH, D_MODEL), ATTN_WIDTH ** -0.5),
        "w_out": nrm(ks[17], (DEPTH_2, D_MODEL, D_MODEL), D_MODEL ** -0.5),
        "mix_post_g": gain(ks[18], (DEPTH_2, D_MODEL)),
        "ffn2_pre_g": gain(ks[19], (DEPTH_2, D_MODEL)),
        "ffn2_w_gu": nrm(ks[20], (DEPTH_2, D_MODEL, 2 * D_FF), D_MODEL ** -0.5),
        "ffn2_w_down": nrm(ks[21], (DEPTH_2, D_FF, D_MODEL), D_FF ** -0.5),
        "ffn2_post_g": gain(ks[22], (DEPTH_2, D_MODEL)),
    }

def second_block(x, ffn1_pre_g, ffn1_w_gu, ffn1_w_down, ffn1_post_g,
              mix_pre_g, w_in, conv_w, conv_b, lru_w_a, lru_b_a, lru_w_x, lru_b_x,
              lru_lambda, attn_sinks, w_proj_lru, w_proj_attn, w_out, mix_post_g,
              ffn2_pre_g, ffn2_w_gu, ffn2_w_down, ffn2_post_g):
    cos, sin = rope_tables_2(x.shape[1])
    h = x
    for l in range(DEPTH_2):
        f = swiglu_2(rms_norm_2(h, ffn1_pre_g[l]), ffn1_w_gu[l], ffn1_w_down[l])
        h = h + MACARON_SCALE * rms_norm_2(f, ffn1_post_g[l])
        m = hybrid_mixer_2(rms_norm_2(h, mix_pre_g[l]), cos, sin, w_in[l], conv_w[l], conv_b[l],
                         lru_w_a[l], lru_b_a[l], lru_w_x[l], lru_b_x[l], lru_lambda[l],
                         attn_sinks[l], w_proj_lru[l], w_proj_attn[l], w_out[l])
        h = h + rms_norm_2(m, mix_post_g[l])
        f = swiglu_2(rms_norm_2(h, ffn2_pre_g[l]), ffn2_w_gu[l], ffn2_w_down[l])
        h = h + MACARON_SCALE * rms_norm_2(f, ffn2_post_g[l])
    return h


def setup_inputs(seed=0):
    out = dict(first_inputs(seed))
    for name, value in second_inputs(seed + 1).items():
        if name != "x":
            out[name + "_2"] = value
    return out


def reference(
    x, p, positions, ffa_w_in, ffa_w_out, mix_w_in, gdn_conv_w, gdn_a_log, gdn_dt_bias,
    gdn_norm_w, mla_q_norm_w, mla_kv_norm_w, mla_w_uq, mla_w_ukv, mix_w_o, ffb_w_in, ffb_w_out,
    ln_g, ln_b, ple_w_gate, ple_w_proj, ffn1_pre_g_2, ffn1_w_gu_2, ffn1_w_down_2, ffn1_post_g_2,
    mix_pre_g_2, w_in_2, conv_w_2, conv_b_2, lru_w_a_2, lru_b_a_2, lru_w_x_2, lru_b_x_2,
    lru_lambda_2, attn_sinks_2, w_proj_lru_2, w_proj_attn_2, w_out_2, mix_post_g_2,
    ffn2_pre_g_2, ffn2_w_gu_2, ffn2_w_down_2, ffn2_post_g_2,
):
    x = first_block(
        x, p, positions, ffa_w_in, ffa_w_out, mix_w_in, gdn_conv_w, gdn_a_log, gdn_dt_bias,
        gdn_norm_w, mla_q_norm_w, mla_kv_norm_w, mla_w_uq, mla_w_ukv, mix_w_o, ffb_w_in,
        ffb_w_out, ln_g, ln_b, ple_w_gate, ple_w_proj,
    )
    return second_block(
        x, ffn1_pre_g_2, ffn1_w_gu_2, ffn1_w_down_2, ffn1_post_g_2, mix_pre_g_2, w_in_2,
        conv_w_2, conv_b_2, lru_w_a_2, lru_b_a_2, lru_w_x_2, lru_b_x_2, lru_lambda_2,
        attn_sinks_2, w_proj_lru_2, w_proj_attn_2, w_out_2, mix_post_g_2, ffn2_pre_g_2,
        ffn2_w_gu_2, ffn2_w_down_2, ffn2_post_g_2,
    )


_drawn_inputs = setup_inputs


def setup_inputs(seed=0):
    import zlib

    import numpy as np

    out = dict(_drawn_inputs(seed))
    spreads = {}
    factors = {'gdn_norm_w': 7.903,
     'mla_q_norm_w': 8.0,
     'mla_kv_norm_w': 8.0,
     'lru_b_a_2': 42.895,
     'lru_b_x_2': 8.0,
     'attn_sinks_2': 3.694,
     'ffn2_post_g_2': 3.785}
    for name, (base, spread) in spreads.items():
        noise = np.random.default_rng([zlib.crc32(name.encode()), seed]).standard_normal(out[name].shape)
        drawn = base * np.exp(spread * noise) if base else spread * noise
        out[name] = __import__('jax').numpy.asarray(drawn.astype(out[name].dtype))
    for name, factor in factors.items():
        out[name] = (out[name] * factor).astype(out[name].dtype)
    return out
```

```python
import math
from contextlib import ExitStack

import numpy as np

import concourse.bass as bass
from concourse import mybir

ALU = mybir.AluOpType
ACT = mybir.ActivationFunctionType
AX = mybir.AxisListType
F32 = mybir.dt.float32
F32R = mybir.dt.float32r
I32 = mybir.dt.int32

P = 128
SEQ = 256
TT = SEQ // P
D = 1024
KT = D // P
DEPTH = 2
D_FF = 2816
FFC = 256
FF_STEPS = D_FF // FFC
PLE = 256
ALPHA = (2 * DEPTH) ** 0.25
LN_EPS = 1e-5
RMS_EPS = 1e-6
ROPE_BASE = 10000.0

GH, GD = 8, 64
GW = GH * GD
CONV = 4
SBH, SBD = 4, 64
SBW = SBH * SBD
MH, MN, MR, MV = 4, 64, 32, 64
MQ, MKV = 256, 128
MD = MN + MR
IN1 = 4 * GW + 2 * GH + 3 * SBW + MQ + MKV + MR
C_Z = 3 * GW
C_G = 4 * GW
C_SQ = C_G + 2 * GH
C_SV = C_SQ + 2 * SBW
C_MQ = C_SV + SBW
MLW = MQ + MKV + MR
DW = 2 * GH + MLW

LRU = 1024
LT = LRU // P
LRU_C = 8.0
QH, KVH, HD = 16, 4, 64
QW, KVW = QH * HD, KVH * HD
IN2 = 2 * LRU + QW + 2 * KVW + 2 * D

SLAB = 2048
RING = 3
NEG = -1e30

LEVELS = [1 << n for n in range(7)]
C_ID, C_UI, C_SL, C_LI, C_ONE = 0, 128, 256, 384, 512
C_LV = 640
C_NS = C_LV + 128 * len(LEVELS)
C_NC = C_NS + 256
C_NW = C_NC + 256
C_INV = C_NW + 256
C_COS = C_INV + MR // 2
C_SIN = C_COS + TT * (HD // 2)
C_TOT = C_SIN + TT * (HD // 2)


def shape_tables():
    t = np.zeros((P, C_TOT), np.float32)
    a, b = np.arange(P)[:, None], np.arange(P)[None, :]
    t[:, C_ID:C_ID + P] = a == b
    t[:, C_UI:C_UI + P] = a <= b
    t[:, C_SL:C_SL + P] = a > b
    t[:, C_LI:C_LI + P] = a >= b
    t[:, C_ONE:C_ONE + P] = 1
    for n, w in enumerate(LEVELS):
        same = a // (2 * w) == b // (2 * w)
        t[:, C_LV + n * P:C_LV + (n + 1) * P] = same & (a // w % 2 == 0) & (b // w % 2 == 1)
    t[:, C_NS:C_NS + P] = np.where(a < b, 0, NEG)
    t[:, C_NC + P:C_NC + 2 * P] = np.where(b <= a, 0, NEG)
    t[:, C_NW:C_NW + P] = np.where(b > a, 0, NEG)
    t[:, C_NW + P:C_NW + 2 * P] = np.where(b <= a, 0, NEG)
    t[:, C_INV:C_INV + MR // 2] = np.float32(1) / np.float32(ROPE_BASE) ** (
        np.arange(0, MR, 2, dtype=np.float32) / np.float32(MR))
    half = HD // 2
    inv = np.float32(ROPE_BASE) ** (-np.arange(half, dtype=np.float32) / np.float32(half))
    ang = np.arange(SEQ, dtype=np.float32)[:, None] * inv[None, :]
    for n, f in ((C_COS, np.cos), (C_SIN, np.sin)):
        t[:, n:n + TT * half] = f(ang).astype(np.float32).reshape(TT, P, half).transpose(1, 0, 2).reshape(P, -1)
    return t


class Steps:

    def __init__(self, known):
        self.known, self.found, self.sems, self.count, self.part = known, {}, {}, {}, ""

    def start(self, part):
        self.part = part
        self.count = dict.fromkeys(self.sems, 0)

    def mark(self, who, name):
        self.count[who] += 1
        assert (self.part, name) not in self.found, name
        self.found[self.part, name] = (who, self.count[who])
        return self.sems[who], 1

    def after(self, name):
        who, value = self.known.get((self.part, name), (None, 1))
        if who is None:
            assert not self.known, (self.part, name)
            who = next(iter(self.sems))
        return self.sems[who], value


def build_program(nc, A, out, known, stop=99, dbg=None):
    ctx = ExitStack()
    with ctx:
        def sb(name, shape, dt=F32):
            return ctx.enter_context(nc.sbuf_tensor(name, shape, dt))

        def sem(name):
            return ctx.enter_context(nc.semaphore(name))

        raw = sb("raw", [P, RING, SLAB])
        whi = sb("whi", [P, RING, SLAB], F32R)
        wlo = sb("wlo", [P, RING, SLAB], F32R)
        h = sb("h", [P, TT, D])
        xhi = sb("xhi", [P, KT, SEQ], F32R)
        xlo = sb("xlo", [P, KT, SEQ], F32R)
        gated = sb("gated", [P, 2, TT, FFC])
        ahi = sb("ahi", [P, 2, SEQ], F32R)
        alo = sb("alo", [P, 2, SEQ], F32R)
        normw = sb("normw", [P, 2, D])
        tab = sb("tab", [P, C_TOT])
        pv = sb("pv", [P, 512])
        small = sb("small", [P, 512])
        arena = sb("arena", [P, 20992])
        bank = [ctx.enter_context(nc.psum_tensor(f"bank{n}", [P, 512], F32)) for n in range(8)]
        acc = [[bank[2 * t + n] for n in range(2)] for t in range(TT)]

        ident = tab[:, C_ID:C_ID + P]

        def flat(x):
            return x[:, :, :].rearrange("p a b -> p (a b)")

        def tokens(t):
            return slice(P * t, P * t + P)

        rope1 = sb("rope1", [P, 2, TT, MR // 2])

        arrived = [sem(f"slab_arrived{n}") for n in range(RING)]
        hi_made = sem("slab_hi_made")
        lo_dve = sem("slab_lo_made_by_vector")
        lo_pool = sem("slab_lo_made_by_gpsimd")
        slab_used = sem("slab_used")
        ff_first = sem("gate_up_products_of_first_tile")
        ff_silu = sem("silu_of_gate")
        ff_gated = sem("gated_ready")
        ff_turned = sem("gated_turned")
        ff_hi = sem("gated_hi")
        ff_lo = sem("gated_lo")
        st = Steps(known)
        st.sems = {w: sem(f"steps_of_{w}") for w in ("tensor", "vector", "scalar", "gpsimd")}
        params = [sem(f"parameters{n}") for n in range(8)]
        stored = sem("stored")
        every = arrived + [hi_made, lo_dve, lo_pool, slab_used, ff_first, ff_silu, ff_gated, ff_turned,
                           ff_hi, ff_lo, *st.sems.values(), *params]
        after = st.after
        T, V, S, G = (lambda n, w=w: st.mark(w, n) for w in ("tensor", "vector", "scalar", "gpsimd"))

        DVE_PART = [1408]

        def load_slab(sp, g, i, parts):
            if not (isinstance(i, int) and g + 3 * i < RING):
                sp.wait_ge(lo_dve, g + 3 * i - RING + 1)
                sp.wait_ge(lo_pool, g + 3 * i - RING + 1)
            for n, (view, src) in enumerate(parts):
                nc.sync.dma_start(view(raw[:, g % RING, :]), src).then_inc(arrived[g % RING], 16)

        def make_hi(act, g, i=0):
            act.wait_ge(arrived[g % RING], 32 * (g // RING + 1 + i))
            if not (isinstance(i, int) and g < RING):
                act.wait_ge(slab_used, g + 3 * i - RING + 1)
            nc.scalar.activation(whi[:, g % RING, :], raw[:, g % RING, :], ACT.Copy).then_inc(hi_made, 1)

        def make_lo(eng, which, g, i=0):
            cut = DVE_PART[0]
            part = slice(0, cut) if which is lo_dve else slice(cut, SLAB)
            eng.wait_ge(hi_made, g + 3 * i + 1)
            eng.tensor_tensor(wlo[:, g % RING, part], raw[:, g % RING, part],
                              whi[:, g % RING, part].bitcast(F32), ALU.subtract).then_inc(which, 1)

        def await_slab(pe, g, i=0):
            pe.wait_ge(hi_made, g + 3 * i + 1)
            pe.wait_ge(lo_dve, g + 3 * i + 1)
            pe.wait_ge(lo_pool, g + 3 * i + 1)

        def product(o, left, right, first, last, skip=False):
            (lh, ll), (rh, rl) = left, right
            nc.tensor.matmul(o, lh, rh, start=first, stop=False, skip_group_check=skip)
            nc.tensor.matmul(o, ll, rh, start=False, stop=False, skip_group_check=skip)
            return nc.tensor.matmul(o, lh, rl, start=False, stop=last, skip_group_check=skip)

        def slab(g, k, w):
            return tuple(x[:, g % RING, :k * w].rearrange("p (k n) -> p k n", k=k) for x in (whi, wlo))

        def wide_slab(g, left, k0, first, last, done=None):
            wh, wl = slab(g, 2, D)
            lh, ll = left
            for t in range(TT):
                for k in range(2):
                    for n in range(2):
                        c = slice(512 * n, 512 * n + 512)
                        u = tokens(t)
                        m = product(acc[t][n][:, :], (lh[:, k0 + k, u], ll[:, k0 + k, u]),
                                    (wh[:, k, c], wl[:, k, c]), first and k == 0, last and k == 1)
                if last and t == 0:
                    m.then_inc(*T(done))
            return m

        def token_slab(g, k0, nk, w, outs):
            wh, wl = slab(g, nk, w)
            for t in range(TT):
                for k in range(nk):
                    u = tokens(t)
                    m = product(outs[t], (xhi[:, k0 + k, u], xlo[:, k0 + k, u]), (wh[:, k, :], wl[:, k, :]),
                                k0 + k == 0, k0 + k == KT - 1)
            return m

        def channel_slab(g, k0, outs):
            wh, wl = slab(g, 4, 512)
            for c in range(4):
                for k in range(4):
                    u = slice(P * c, P * c + P)
                    m = product(outs[c // 2][:, 256 * (c % 2):256 * (c % 2) + 256],
                                (wh[:, k, u], wl[:, k, u]), (xhi[:, k0 + k, :], xlo[:, k0 + k, :]),
                                k0 + k == 0 and c % 2 == 0, k0 + k == KT - 1, skip=True)
            return m

        def rows(W, r, n):
            return W[bass.ds(r, n), :]

        def in_parts(W, r0, half, j):
            def view(which):
                return lambda x: x.rearrange("p (k b n) -> p k b n", k=4, b=2)[:, :, which, :]
            return [(view(b), W[bass.ds(r0 + 512 * half, 512), bass.ds(b * D_FF + FFC * j, FFC)]
                     .rearrange("(k p) n -> p k n", p=P)) for b in range(2)]

        def wide_parts(W, r):
            return [((lambda x, k=k: x[:, D * k:D * k + D]), W[bass.ds(r + P * k, P), :]) for k in range(2)]

        def col_parts(W, r0, k0, nk, pieces):
            w = sum(n for _, n in pieces)
            if len(pieces) == 1:
                c = pieces[0][0]
                m = nk // 2
                return [((lambda x, b=b: x[:, :nk * w].rearrange("p (k n) -> p k n", k=nk)[:, b * m:b * m + m, :]),
                         W[bass.ds(r0 + P * (k0 + b * m), P * m), c:c + w].rearrange("(k p) n -> p k n", p=P))
                        for b in range(2)]
            out, at = [], 0
            for c, n in pieces:
                out.append(((lambda x, at=at, n=n: x[:, :nk * w].rearrange("p (k n) -> p k n", k=nk)[:, :, at:at + n]),
                            W[bass.ds(r0 + P * k0, P * nk), c:c + n].rearrange("(k p) n -> p k n", p=P)))
                at += n
            return out

        def ff_load(sp, g0, W1, r1, W2, r2):
            def step(g, i, j):
                load_slab(sp, g, i, in_parts(W1, r1, 0, j))
                load_slab(sp, g + 1, i, in_parts(W1, r1, 1, j))

            def step_and_out(i):
                step(g0 + 2, i, i + 1)
                load_slab(sp, g0 + 4, i, wide_parts(W2, r2 + FFC * i))

            step(g0, 0, 0)
            step_and_out(0)
            with sp.Fori(1, FF_STEPS - 1) as i:
                step_and_out(i)
            load_slab(sp, g0 + 32, 0, wide_parts(W2, r2 + FFC * (FF_STEPS - 1)))

        ff_bank = [bank[4], bank[5]]

        def ff_tensor(pe, g0, f, name):
            j0 = FF_STEPS * f

            def gate_up(g, i, half):
                wh, wl = slab(g, 4, 2 * FFC)
                await_slab(pe, g, i)
                for t in range(TT):
                    for k in range(4):
                        u, kk = tokens(t), 4 * half + k
                        m = product(ff_bank[t][:, :], (xhi[:, kk, u], xlo[:, kk, u]), (wh[:, k, :], wl[:, k, :]),
                                    kk == 0, kk == KT - 1)
                    if half and t == 0:
                        m.then_inc(ff_first, 1)
                m.then_inc(slab_used, 1)

            def turn_gated(j):
                pe.wait_ge(ff_gated, 2 * j + 2)
                if not (isinstance(j, int) and j == 0):
                    pe.wait_ge(ff_lo, j)
                for k in range(2):
                    for t in range(TT):
                        m = nc.tensor.transpose(bank[6][:, 256 * k + P * t:256 * k + P * t + P],
                                                gated[:, 1, t, P * k:P * k + P], ident)
                m.then_inc(ff_turned, 1)

            def step_in(g, i, j, turn):
                if not (isinstance(j, int) and j == 0):
                    pe.wait_ge(ff_gated, 2 * j)
                gate_up(g, i, 0)
                if turn:
                    turn_gated(j - 1)
                gate_up(g + 1, i, 1)

            def step_out(g, i, j, first, last):
                await_slab(pe, g, i)
                pe.wait_ge(ff_lo, j + 1)
                wide_slab(g, (ahi, alo), 0, first, last, name).then_inc(slab_used, 1)

            step_in(g0, 0, j0, False)
            step_in(g0 + 2, 0, j0 + 1, True)
            step_out(g0 + 4, 0, j0, True, False)
            with pe.Fori(1, FF_STEPS - 1) as i:
                step_in(g0 + 2, i, j0 + 1 + i, True)
                step_out(g0 + 4, i, j0 + i, False, False)
            turn_gated(j0 + FF_STEPS - 1)
            step_out(g0 + 32, 0, j0 + FF_STEPS - 1, False, True)

        def ff_scalar(act, g0, f, more):
            j0 = FF_STEPS * f

            def silus(j, g, i):
                for t in range(TT):
                    if t == 0:
                        act.wait_ge(ff_first, j + 1)
                    else:
                        act.wait_ge(slab_used, g + 3 * i + 1)
                    if not (isinstance(j, int) and j == 0):
                        act.wait_ge(ff_gated, 2 * j + t - 1)
                    nc.scalar.activation(gated[:, 0, t, :], ff_bank[t][:, 0:FFC], ACT.Silu).then_inc(ff_silu, 1)

            def hi(j):
                act.wait_ge(ff_turned, j + 1)
                nc.scalar.activation(flat(ahi), bank[6][:, :], ACT.Copy).then_inc(ff_hi, 1)

            def step(i, slabs):
                hi(j0 + i)
                if slabs > 0:
                    make_hi(act, g0 + 5, i)
                silus(j0 + 1 + i, g0 + 3, i)
                for n in range(1, slabs):
                    make_hi(act, g0 + 5 + n, i)

            make_hi(act, g0 + 3)
            silus(j0, g0 + 1, 0)
            make_hi(act, g0 + 4)
            with act.Fori(0, FF_STEPS - 2) as i:
                step(i, 3)
            step(FF_STEPS - 2, 3 if more else 1)
            hi(j0 + FF_STEPS - 1)
            if more:
                make_hi(act, g0 + 35)

        def ff_vector(dve, g0, f, more):
            j0 = FF_STEPS * f

            def gate(j):
                for t in range(TT):
                    dve.wait_ge(ff_silu, 2 * j + t + 1)
                    if not (isinstance(j, int) and j == 0):
                        dve.wait_ge(ff_turned, j)
                    nc.vector.tensor_tensor(gated[:, 1, t, :], gated[:, 0, t, :], ff_bank[t][:, FFC:2 * FFC],
                                            ALU.mult).then_inc(ff_gated, 1)

            def lo(j):
                dve.wait_ge(ff_hi, j + 1)
                nc.vector.tensor_tensor(flat(alo), bank[6][:, :], flat(ahi).bitcast(F32),
                                        ALU.subtract).then_inc(ff_lo, 1)

            def step(i, slabs):
                lo(j0 + i)
                if slabs > 0:
                    make_lo(dve, lo_dve, g0 + 5, i)
                gate(j0 + 1 + i)
                for n in range(1, slabs):
                    make_lo(dve, lo_dve, g0 + 5 + n, i)

            make_lo(dve, lo_dve, g0 + 3)
            gate(j0)
            make_lo(dve, lo_dve, g0 + 4)
            with dve.Fori(0, FF_STEPS - 2) as i:
                step(i, 3)
            step(FF_STEPS - 2, 3 if more else 1)
            lo(j0 + FF_STEPS - 1)
            if more:
                make_lo(dve, lo_dve, g0 + 35)

        def ff_gpsimd(pool, g0, more):
            with pool.Fori(0, FF_STEPS - (0 if more else 1)) as i:
                for n in range(3):
                    make_lo(pool, lo_pool, g0 + 3 + n, i)

        def rsqrt(dve, name, y, v, eps, scale=1.0):
            n = v.shape[-1]
            x, yy, z = y[:, 1, 0:n], y[:, 0, 0:n], y[:, 2, 0:n]
            k = [0]

            def link(ins):
                k[0] += 1
                ins.then_inc(*V(f"{name} {k[0]}"))
                dve.wait_ge(*after(f"{name} {k[0]}"))

            link(nc.vector.tensor_scalar(x, v, scale, eps, ALU.mult, ALU.add))
            link(nc.vector.tensor_scalar(z.bitcast(I32), x.bitcast(I32), 1, None, ALU.logical_shift_right))
            link(nc.vector.tensor_scalar(yy.bitcast(I32), z.bitcast(I32), -1.0, float(0x5F3759DF), ALU.mult, ALU.add))
            for step in range(3):
                link(nc.vector.scalar_tensor_tensor(z, x, -0.5, yy, ALU.mult, ALU.mult))
                link(nc.vector.tensor_tensor(z, z, yy, ALU.mult))
                ins = nc.vector.scalar_tensor_tensor(yy, z, 1.5, yy, ALU.add, ALU.mult)
                if step < 2:
                    link(ins)
            ins.then_inc(*V(name))

        def norm_vector(dve, name, c, ready, nth):
            stats = small[:, 0:24].rearrange("p (t n s) -> p t n s", t=2, n=2)
            mv = small[:, 24:28].rearrange("p (t s) -> p t s", t=2)
            rs = small[:, 28:34].rearrange("p (t s n) -> p t s n", t=2, s=3)
            for t in range(TT):
                dve.wait_ge(*ready(t))
                for n in range(2):
                    c5 = slice(512 * n, 512 * n + 512)
                    nc.vector.scalar_tensor_tensor(h[:, t, c5], acc[t][n][:, :], c, h[:, t, c5],
                                                   ALU.mult, ALU.add).then_inc(*V(f"{name} sum {t}{n}"))
                for n in range(2):
                    dve.wait_ge(*after(f"{name} sum {t}{n}"))
                    nc.vector.bn_stats(stats[:, t, n, :], h[:, t, 512 * n:512 * n + 512]).then_inc(*V(f"{name} stats {t}{n}"))
                dve.wait_ge(*after(f"{name} stats {t}1"))
                nc.vector.bn_aggr(mv[:, t, :], stats[:, t, :, :].rearrange("p n s -> p (n s)")).then_inc(*V(f"{name} mean {t}"))
                dve.wait_ge(*after(f"{name} mean {t}"))
                rsqrt(dve, f"{name} rstd {t}", rs[:, t], mv[:, t, 1:2], LN_EPS / ALPHA ** 2)
                dve.wait_ge(*after(f"{name} rstd {t}"))
                nc.vector.tensor_scalar(h[:, t, :], h[:, t, :], mv[:, t, 0:1], rs[:, t, 0, 0:1],
                                        ALU.subtract, ALU.mult).then_inc(*V(f"{name} unit {t}"))
                dve.wait_ge(*after(f"{name} unit {t}"))
                dve.wait_ge(params[0], 32 * (nth + 1))
                nc.vector.tensor_tensor(h[:, t, :], h[:, t, :], normw[:, 0, :], ALU.mult).then_inc(*V(f"{name} gained {t}"))
                dve.wait_ge(*after(f"{name} gained {t}"))
                nc.vector.tensor_tensor(h[:, t, :], h[:, t, :], normw[:, 1, :], ALU.add).then_inc(*V(f"{name} done {t}"))

        def load_norm(sp, nth, g, b, free):
            if free:
                sp.wait_ge(*after(free))
            nc.sync.dma_start(normw[:, 0, :], g.partition_broadcast(P)).then_inc(params[0], 16)
            nc.sync.dma_start(normw[:, 1, :], b.partition_broadcast(P)).then_inc(params[0], 16)

        def turn_tensor(pe, name, src, ready, free=None):
            if free:
                pe.wait_ge(*free)
            for t in range(TT):
                if ready:
                    pe.wait_ge(*ready(t))
                for half in range(2):
                    n = 2 * t + half
                    if n >= 2:
                        pe.wait_ge(*after(f"{name} lo {n - 2}"))
                    for q in range(4):
                        m = nc.tensor.transpose(bank[6 + half][:, P * q:P * q + P],
                                                src[:, t, P * (4 * half + q):P * (4 * half + q) + P], ident)
                    m.then_inc(*T(f"{name} turned {n}"))

        def turn_scalar(act, name):
            for n in range(4):
                t, half = n // 2, n % 2
                act.wait_ge(*after(f"{name} turned {n}"))
                nc.scalar.activation(xhi[:, 4 * half:4 * half + 4, tokens(t)],
                                     bank[6 + half][:, :].rearrange("p (k n) -> p k n", k=4),
                                     ACT.Copy).then_inc(*S(f"{name} hi {n}"))

        def turn_vector(dve, name):
            for n in range(4):
                t, half = n // 2, n % 2
                dve.wait_ge(*after(f"{name} hi {n}"))
                nc.vector.tensor_tensor(xlo[:, 4 * half:4 * half + 4, tokens(t)],
                                        bank[6 + half][:, :].rearrange("p (k n) -> p k n", k=4),
                                        xhi[:, 4 * half:4 * half + 4, tokens(t)].bitcast(F32),
                                        ALU.subtract).then_inc(*V(f"{name} lo {n}"))

        at = {}

        def place(name, start, *shape):
            n = int(np.prod(shape))
            v = arena[:, start:start + n]
            if len(shape) == 2:
                v = v.rearrange("p (a b) -> p a b", a=shape[0])
            if len(shape) == 3:
                v = v.rearrange("p (a b c) -> p a b c", a=shape[0], b=shape[1])
            at[name] = v
            return v

        PR = TT * GH
        conv_in = place("conv_in", 0, 12, SEQ + 4)
        conv_out = place("conv_out", 3120, 12, SEQ)
        A_T = place("A_T", 0, PR, P)
        QK_T = place("QK_T", 2048, PR, P)
        B_T = place("B_T", 4096, 2, 4, P)
        Y_g = place("Y_g", 5120, 2, 4, P)
        T_inv = place("T_inv", 6192, PR, P)
        T_invT = place("T_invT", 8240, PR, P)
        q_tok = place("q_tok", 6192, TT, GW)
        kb_tok = place("kb_tok", 7216, TT, GW)
        k_tok = place("k_tok", 10288, TT, GW)
        v_new = place("v_new", 10288, TT, GW)
        vb_tok = place("vb_tok", 11312, TT, GW)
        kT = place("kT", 12336, TT, 4, P)
        qkbT = arena[:, 13360:15408].rearrange("p (t r b n) -> p t r b n", t=TT, r=4, b=2)
        g_upto = place("g_upto", 15408, 2, 4, P)
        decay = place("decay", 16432, 2, 4, P)
        squares = place("squares", 15408, 4, GW)
        k_dec = place("k_dec", 17456, GW)
        state = place("state", 17968, 4, GD)
        silu_z = place("silu_z", 18224, TT, GW)
        sqT = place("sqT", 19248, 2, SEQ)
        skT = place("skT", 19760, 2, SEQ)
        s_val = place("s_val", 20272, TT, SBW)
        conv_rows = arena[0:4 * 12, 6192:6192 + P]
        latent = gated[:, :, :, :].rearrange("p a b c -> p (a b c)")[:, 0:TT * DW].rearrange("p (t n) -> p t n", t=TT)
        mixed = normw
        pv_conv = pv[:, 0:48]
        pv_alog, pv_dt = pv[:, 48:56], pv[:, 56:64]
        pv_gnorm = pv[:, 64:128]
        pv_qn = pv[:, 128:128 + MQ + MKV]

        def sm(start, n):
            return small[:, start:start + n]

        def small_loads(sp, l):
            one = lambda name, n: A[name][bass.ds(l, 1), :].partition_broadcast(P).rearrange("p a n -> p (a n)")
            nc.sync.dma_start(conv_rows, A["gdn_conv_w"].rearrange("l k (c p) -> (l k c) p", p=P)[bass.ds(l * 48, 48), :])\
              .then_inc(params[1], 16)
            nc.sync.dma_start(pv_alog, one("gdn_a_log", 8)).then_inc(params[2], 16)
            nc.sync.dma_start(pv_dt, one("gdn_dt_bias", 8)).then_inc(params[2], 16)
            nc.sync.dma_start(pv_gnorm, one("gdn_norm_w", 64)).then_inc(params[2], 16)
            nc.sync.dma_start(pv_qn[:, 0:MQ], one("mla_q_norm_w", MQ)).then_inc(params[2], 16)
            nc.sync.dma_start(pv_qn[:, MQ:MQ + MKV], one("mla_kv_norm_w", MKV)).then_inc(params[2], 16)

        def mixer_load(sp, g0, l):
            W = A["mix_w_in"].rearrange("l k n -> (l k) n")
            r = l * D
            g = g0
            for c in (0, GW, 2 * GW, C_Z):
                for half in range(2):
                    load_slab(sp, g, 0, col_parts(W, r, 4 * half, 4, [(c, 512)]))
                    g += 1
            for half in range(2):
                load_slab(sp, g, 0, col_parts(W, r, 4 * half, 4, [(C_G, 2 * GH), (C_MQ, MLW)]))
                g += 1
            for half in range(2):
                load_slab(sp, g, 0, col_parts(W, r, 4 * half, 4, [(C_SQ, 512)]))
                g += 1
            load_slab(sp, g, 0, col_parts(W, r, 0, 8, [(C_SV, SBW)]))
            wo = A["mix_w_o"].rearrange("l k n -> (l k) n")
            for n in range(4):
                load_slab(sp, g0 + 13 + n, 0, wide_parts(wo, l * D + 2 * P * n))

        def mixer_tensor(pe, g0):
            def used(m):
                m.then_inc(slab_used, 1)

            def chan(g, banks, free=None):
                for half in range(2):
                    if free and half == 0:
                        pe.wait_ge(*after(free))
                    await_slab(pe, g + half)
                    used(channel_slab(g + half, 4 * half, banks))

            def tok(g, nk, w, outs, free=None):
                for half in range(KT // nk):
                    if free and half == 0:
                        pe.wait_ge(*after(free))
                    await_slab(pe, g + half)
                    used(token_slab(g + half, nk * half, nk, w, outs))

            def to_tokens(grp, t, b):
                for c in range(4):
                    m = nc.tensor.transpose(b[:, P * c:P * c + P], conv_out[:, 4 * grp + c, tokens(t)], ident)
                return m

            pe.wait_ge(params[1], 16)
            nc.tensor.transpose(bank[0][:, 0:48], conv_rows, ident[0:48, 0:48]).then_inc(*T("taps"))
            chan(g0, bank[0:2], "taps in place")
            chan(g0 + 2, bank[2:4])
            chan(g0 + 4, bank[0:2], "evacuated 0 1")
            tok(g0 + 6, 4, 512, [bank[2][:, :], bank[3][:, :]], "evacuated 1 1")
            for grp in range(2):
                pe.wait_ge(*after(f"conv silu {grp} 1"))
                for t in range(TT):
                    to_tokens(grp, t, bank[4 + 2 * grp + t]).then_inc(*T(f"qk tokens {grp} {t}"))
            tok(g0 + 8, 4, DW, [bank[0][:, 0:DW], bank[1][:, 0:DW]], "evacuated 2 1")
            pe.wait_ge(*after("conv silu 2 1"))
            pe.wait_ge(*after("silu z 1"))
            for t in range(TT):
                to_tokens(2, t, bank[2 + t]).then_inc(*T(f"v tokens {t}"))
            chan(g0 + 10, bank[0:2], "latent 1")
            srcs = [("k", 0), ("q", 0), ("kb", 0), ("k", 1), ("q", 1), ("kb", 1)]
            for n, (what, t) in enumerate(srcs):
                src = {"k": k_tok, "q": q_tok, "kb": kb_tok}[what]
                pe.wait_ge(*after(f"{what} tok {t}"))
                if n == 0:
                    pe.wait_ge(*after("q tok 1"))
                    pe.wait_ge(*after("k tok 1"))
                if n >= 4:
                    pe.wait_ge(*after(f"turned in place {n - 4}"))
                for r in range(4):
                    m = nc.tensor.transpose(bank[4 + n % 4][:, P * r:P * r + P], src[:, t, P * r:P * r + P], ident)
                m.then_inc(*T(f"turned {n}"))
            tok(g0 + 12, 8, SBW, [bank[2][:, 0:SBW], bank[3][:, 0:SBW]], "vb tok 1")
            pe.wait_ge(*after("g"))
            pe.wait_ge(*after("turned in place 2"))
            nc.tensor.matmul(bank[6][:, 0:16], tab[:, C_UI:C_UI + P], sm(304, 16), start=True, stop=True)
            nc.tensor.matmul(bank[6][:, 16:32], tab[:, C_SL:C_SL + P], sm(304, 16), start=True, stop=True)\
                .then_inc(*T("g sums"))
            for q in range(4):
                pe.wait_ge(*after(f"g upto {q}"))
                if q == 0:
                    pe.wait_ge(*after("turned in place 3"))
                if q == 1:
                    pe.wait_ge(*after("eg"))
                if q >= 2:
                    pe.wait_ge(*after(f"decay exp {q - 2}"))
                nc.tensor.matmul(bank[7 - q % 2][:, :], tab[:, C_SL:C_SL + P], g_upto[:, q % 2, :, :],
                                 start=True, stop=True).then_inc(*T(f"decay sums {q}"))
                pe.wait_ge(*after("turned in place 5"))
                if q >= 1:
                    pe.wait_ge(*after(f"A_T {q - 1} 1"))
                t = q // 2
                for b in range(2):
                    for x in range(2):
                        hh = 4 * (q % 2) + 2 * x + b
                        u = slice(64 * (hh % 2), 64 * (hh % 2) + 64)
                        m = nc.tensor.matmul(bank[4 + b][:, 256 * x:256 * x + 256], kT[u, t, hh // 2, :],
                                             qkbT[u, t, hh // 2, :, :], start=True, stop=True)
                    m.then_inc(*T(f"kk {q} {b}"))
            for n in range(len(LEVELS)):
                for q in range(4):
                    y = bank[4 + q]
                    pe.wait_ge(*after(f"B_T {n} {q}"))
                    if n == 0:
                        if q == 0:
                            pe.wait_ge(*after("A_T 3 1"))
                        if q >= 2:
                            pe.wait_ge(*after("decay exp 3"))
                        for x in range(4):
                            m = nc.tensor.transpose(y[:, P * x:P * x + P], B_T[:, q % 2, x, :], ident)
                        m.then_inc(*T(f"Y {n} {q}"))
                        continue
                    pe.wait_ge(*after(f"T_invT {n - 1} {q}"))
                    for x in range(4):
                        m = nc.tensor.matmul(y[:, P * x:P * x + P], B_T[:, q % 2, x, :], T_inv[:, 4 * q + x, :],
                                             start=True, stop=True)
                    m.then_inc(*T(f"Y {n} {q}"))
                    pe.wait_ge(*after(f"Y_g {n} {q}"))
                    if n < len(LEVELS) - 1:
                        for x in range(4):
                            m = nc.tensor.matmul(y[:, P * x:P * x + P], T_invT[:, 4 * q + x, :], Y_g[:, q % 2, x, :],
                                                 start=True, stop=True)
                        m.then_inc(*T(f"dT {n} {q}"))
                    if n == 1 and q == 0:
                        pe.wait_ge(*after("sk"))
                        pe.wait_ge(*after("s_val"))
                    for x in range(4):
                        m = nc.tensor.matmul(bank[q][:, P * x:P * x + P], Y_g[:, q % 2, x, :], T_invT[:, 4 * q + x, :],
                                             start=True, stop=True)
                    m.then_inc(*T(f"dTT {n} {q}"))
            last = len(LEVELS) - 1

            def heads(o, left, right, name, pairs=False):
                for hh in range(GH):
                    m = nc.tensor.matmul(o(hh), left(hh), right(hh), start=True, stop=True)
                m.then_inc(*T(name))

            half = lambda hh: slice(64 * (hh % 2), 64 * (hh % 2) + 64)
            col = lambda hh: slice(64 * hh, 64 * hh + 64)
            pe.wait_ge(*after(f"T_invT {last} 3"))
            heads(lambda x: bank[4][:, col(x)], lambda x: T_invT[:, x, :], lambda x: vb_tok[:, 0, col(x)], "v_new 0")
            pe.wait_ge(*after("v_new in place 0"))
            pe.wait_ge(*after("k_dec"))
            heads(lambda x: bank[6][half(x), col(x // 2)], lambda x: k_dec[:, col(x)],
                  lambda x: v_new[:, 0, col(x)], "state")
            heads(lambda x: bank[5][:, col(x)], lambda x: QK_T[:, x, :], lambda x: v_new[:, 0, col(x)], "o 0")
            pe.wait_ge(*after("state in place"))
            heads(lambda x: bank[3 if x % 2 else 0][:, col(x // 2)], lambda x: kT[half(x), 1, x // 2, :],
                  lambda x: state[half(x), x // 2, :], "k state")
            heads(lambda x: bank[4 if x % 2 else 7][:, col(x // 2)], lambda x: qkbT[half(x), 1, x // 2, 0, :],
                  lambda x: state[half(x), x // 2, :], "q state")
            pe.wait_ge(*after("rhs 1"))
            heads(lambda x: bank[1][:, col(x)], lambda x: T_invT[:, GH + x, :], lambda x: vb_tok[:, 1, col(x)], "v_new 1")
            pe.wait_ge(*after("v_new in place 1"))
            heads(lambda x: bank[2][:, col(x)], lambda x: QK_T[:, GH + x, :], lambda x: v_new[:, 1, col(x)], "o 1")

        def mixer_scalar(act, g0):
            copy = lambda o, i: nc.scalar.activation(o, i, ACT.Copy)
            two = lambda b: b[:, :].rearrange("p (c n) -> p c n", c=2)

            def evacuate(grp, banks):
                for b in range(2):
                    act.wait_ge(slab_used, g0 + 2 * grp + 2)
                    c = 4 * grp + 2 * b
                    copy(conv_in[:, c:c + 2, 3:3 + SEQ], two(banks[b])).then_inc(*S(f"evacuated {grp} {b}"))

            def silu(grp):
                for b in range(2):
                    c = 4 * grp + 2 * b
                    act.wait_ge(*after(f"conv {c + 1} 3"))
                    nc.scalar.activation(conv_out[:, c:c + 2, :], conv_out[:, c:c + 2, :], ACT.Silu)\
                        .then_inc(*S(f"conv silu {grp} {b}"))

            act.wait_ge(*after("taps"))
            copy(pv_conv, bank[0][:, 0:48]).then_inc(*S("taps in place"))
            make_hi(act, g0 + 3)
            evacuate(0, bank[0:2])
            make_hi(act, g0 + 4)
            make_hi(act, g0 + 5)
            evacuate(1, bank[2:4])
            make_hi(act, g0 + 6)
            silu(0)
            make_hi(act, g0 + 7)
            evacuate(2, bank[0:2])
            make_hi(act, g0 + 8)
            silu(1)
            make_hi(act, g0 + 9)
            make_hi(act, g0 + 10)
            for t in range(TT):
                act.wait_ge(slab_used, g0 + 8)
                nc.scalar.activation(silu_z[:, t, :], bank[2 + t][:, :], ACT.Silu).then_inc(*S(f"silu z {t}"))
            silu(2)
            for n in range(4):
                act.wait_ge(*after(f"qk tokens {n // 2} {n % 2}"))
                nc.scalar.activation(squares[:, n, :], bank[4 + n][:, :], ACT.Square).then_inc(*S(f"squares {n}"))
            make_hi(act, g0 + 11)
            for t in range(TT):
                act.wait_ge(slab_used, g0 + 10)
                copy(latent[:, t, :], bank[t][:, 0:DW]).then_inc(*S(f"latent {t}"))
            make_hi(act, g0 + 12)
            act.wait_ge(params[2], 80)
            nc.scalar.activation(sm(352, 8), pv_alog, ACT.Exp).then_inc(*S("exp a"))
            act.wait_ge(*after("x gates"))
            nc.scalar.activation(sm(256, 32), sm(192, 32), ACT.Abs).then_inc(*S("abs gates"))
            act.wait_ge(*after("abs gates"))
            nc.scalar.activation(sm(224, 32), sm(256, 32), ACT.Exp, scale=-1.0).then_inc(*S("exp gates"))
            act.wait_ge(*after("exp gates"))
            nc.scalar.activation(sm(288, 16), sm(224, 16), ACT.Ln, bias=1.0).then_inc(*S("ln gates"))
            make_hi(act, g0 + 13)
            make_hi(act, g0 + 14)
            for n in range(6):
                act.wait_ge(*after(f"turned {n}"))
                src = bank[4 + n % 4][:, :].rearrange("p (r n) -> p r n", r=4)
                t = n // 3
                dst = kT[:, t, :, :] if n % 3 == 0 else qkbT[:, t, :, n % 3 - 1, :]
                copy(dst, src).then_inc(*S(f"turned in place {n}"))
            for w, o in (("sq", sqT), ("sk", skT)):
                b = bank[0 if w == "sq" else 1]
                act.wait_ge(slab_used, g0 + 12)
                copy(o[:, :, :], two(b)).then_inc(*S(w))
            make_hi(act, g0 + 15)
            act.wait_ge(*after("g sums"))
            nc.scalar.activation(sm(368, 32), bank[6][:, 0:32], ACT.Exp).then_inc(*S("eg"))
            for q in range(4):
                act.wait_ge(*after(f"decay sums {q}"))
                if q >= 2:
                    act.wait_ge(*after(f"A_T {q - 2} 1"))
                nc.scalar.activation(decay[:, q % 2, :, :], bank[7 - q % 2][:, :].rearrange("p (x n) -> p x n", x=4),
                                     ACT.Exp).then_inc(*S(f"decay exp {q}"))
            for t in range(TT):
                act.wait_ge(slab_used, g0 + 13)
                copy(s_val[:, t, :], bank[2 + t][:, 0:SBW]).then_inc(*S("s_val" if t else "s_val 0"))
            for n in range(1, len(LEVELS)):
                for q in range(4):
                    act.wait_ge(*after(f"Y {n} {q}"))
                    if q >= 2:
                        act.wait_ge(*after(f"dTT {n} {q - 2}"))
                    elif n >= 2:
                        act.wait_ge(*after(f"dTT {n - 1} {q + 2}"))
                    copy(Y_g[:, q % 2, :, :], bank[4 + q][:, :].rearrange("p (x n) -> p x n", x=4))\
                        .then_inc(*S(f"Y_g {n} {q}"))
            act.wait_ge(*after("v_new 0"))
            act.wait_ge(*after("k_dec"))
            copy(v_new[:, 0, :], bank[4][:, :]).then_inc(*S("v_new in place 0"))
            act.wait_ge(*after("state"))
            copy(state, bank[6][:, 0:256].rearrange("p (r n) -> p r n", r=4)).then_inc(*S("state in place"))
            act.wait_ge(*after("v_new 1"))
            copy(v_new[:, 1, :], bank[1][:, :]).then_inc(*S("v_new in place 1"))

        def mixer_vector(dve, g0):
            TTn, TS, STT = nc.vector.tensor_tensor, nc.vector.tensor_scalar, nc.vector.scalar_tensor_tensor
            lo = lambda n: make_lo(dve, lo_dve, g0 + n)
            per_head = lambda x: x.rearrange("p (h n) -> p h n", n=GD)

            def spread(x, n=GD):
                return x.unsqueeze(2).to_broadcast([P, x.shape[1], n])

            def conv(grp):
                for b in range(2):
                    dve.wait_ge(*after(f"evacuated {grp} {b}"))
                    for k in range(CONV):
                        for c in (4 * grp + 2 * b, 4 * grp + 2 * b + 1):
                            tap = pv_conv[:, 12 * k + c:12 * k + c + 1]
                            src = conv_in[:, c, k:k + SEQ]
                            if k == 0:
                                ins = TS(conv_out[:, c, :], src, tap, None, ALU.mult)
                            else:
                                dve.wait_ge(*after(f"conv {c} {k - 1}"))
                                ins = STT(conv_out[:, c, :], src, tap, conv_out[:, c, :], ALU.mult, ALU.add)
                            ins.then_inc(*V(f"conv {c} {k}"))

            dve.wait_ge(*after("pads"))
            dve.wait_ge(*after("taps in place"))
            lo(3)
            lo(4)
            conv(0)
            lo(5)
            lo(6)
            conv(1)
            lo(7)
            lo(8)
            conv(2)
            lo(9)
            lo(10)
            for n in range(4):
                dve.wait_ge(*after(f"squares {n}"))
                nc.vector.tensor_reduce(sm(64 + 8 * n, 8), per_head(squares[:, n, :]), AX.X, ALU.add)\
                    .then_inc(*V(f"square sums {n}"))
            dve.wait_ge(*after("square sums 3"))
            rn = small[:, 96:192].rearrange("p (s n) -> p s n", s=3)
            rsqrt(dve, "unit", rn, sm(64, 32), RMS_EPS)
            dve.wait_ge(*after("unit"))
            TS(rn[:, 0, 0:16], rn[:, 0, 0:16], GD ** -0.5, None, ALU.mult).then_inc(*V("unit q"))
            dve.wait_ge(*after("unit q"))
            for t in range(TT):
                TTn(per_head(q_tok[:, t, :]), per_head(bank[4 + t][:, :]), spread(rn[:, 0, 8 * t:8 * t + 8]), ALU.mult)\
                    .then_inc(*V(f"q tok {t}"))
                TTn(per_head(k_tok[:, t, :]), per_head(bank[6 + t][:, :]), spread(rn[:, 0, 16 + 8 * t:24 + 8 * t]),
                    ALU.mult).then_inc(*V(f"k tok {t}"))
            lo(11)
            x, e, l, g, be, den, ea = sm(192, 32), sm(224, 32), sm(288, 16), sm(304, 16), sm(320, 16), sm(336, 16), sm(352, 8)
            th = lambda v: v.rearrange("p (t h) -> p t h", t=TT)
            over_t = lambda v: v.unsqueeze(1).to_broadcast([P, TT, GH])
            dve.wait_ge(params[2], 80)
            dve.wait_ge(*after("latent 1"))
            TTn(th(x[:, 0:16]), latent[:, :, 0:8], over_t(pv_dt), ALU.add).then_inc(*V("x decay"))
            nc.vector.tensor_copy(th(x[:, 16:32]), latent[:, :, 8:16]).then_inc(*V("x gates"))
            dve.wait_ge(*after("exp gates"))
            TS(den, e[:, 16:32], 1.0, None, ALU.add).then_inc(*V("beta den"))
            STT(be, x[:, 16:32], 0.0, e[:, 16:32], ALU.is_ge, ALU.max).then_inc(*V("beta num"))
            dve.wait_ge(*after("beta den"))
            nc.vector.reciprocal(den, den).then_inc(*V("beta rec"))
            dve.wait_ge(*after("beta rec"))
            dve.wait_ge(*after("beta num"))
            TTn(be, be, den, ALU.mult).then_inc(*V("beta"))
            dve.wait_ge(*after("ln gates"))
            STT(l, x[:, 0:16], 0.0, l, ALU.max, ALU.add).then_inc(*V("softplus"))
            dve.wait_ge(*after("softplus"))
            dve.wait_ge(*after("exp a"))
            STT(th(g), th(l), -1.0, over_t(ea), ALU.mult, ALU.mult).then_inc(*V("g"))
            dve.wait_ge(*after("beta"))
            for t in range(TT):
                TTn(per_head(kb_tok[:, t, :]), per_head(k_tok[:, t, :]), spread(be[:, 8 * t:8 * t + 8]), ALU.mult)\
                    .then_inc(*V(f"kb tok {t}"))
            for t in range(TT):
                dve.wait_ge(*after(f"v tokens {t}"))
                TTn(per_head(vb_tok[:, t, :]), per_head(bank[2 + t][:, :]), spread(be[:, 8 * t:8 * t + 8]), ALU.mult)\
                    .then_inc(*V(f"vb tok {t}"))
            lo(12)
            lo(13)
            lo(14)
            lo(15)
            dve.wait_ge(*after("g"))
            four = lambda c: tab[:, c:c + P].unsqueeze(1).to_broadcast([P, 4, P])

            def g_upto_of(q):
                if q >= 2:
                    dve.wait_ge(*after(f"decay sums {q - 2}"))
                TTn(g_upto[:, q % 2, :, :], four(C_UI), spread(g[:, 4 * q:4 * q + 4], P), ALU.mult)\
                    .then_inc(*V(f"g upto {q}"))

            g_upto_of(0)
            g_upto_of(1)
            for q in range(4):
                dve.wait_ge(*after(f"decay exp {q}"))
                TTn(decay[:, q % 2, :, :], decay[:, q % 2, :, :], four(C_UI), ALU.mult).then_inc(*V(f"decay {q}"))
                if q < 2:
                    g_upto_of(q + 2)
                dve.wait_ge(*after(f"decay {q}"))
                for b in range(2):
                    dve.wait_ge(*after(f"kk {q} {b}"))
                    src = bank[4 + b][:, :].rearrange("p (x w n) -> p x w n", x=2, w=2)
                    pr = slice(4 * q + b, 4 * q + 4, 2)
                    TTn(QK_T[:, pr, :], src[:, :, 0, :], decay[:, q % 2, b::2, :], ALU.mult)\
                        .then_inc(*V(f"QK_T {q} {b}"))
                    TTn(A_T[:, pr, :], src[:, :, 1, :], decay[:, q % 2, b::2, :], ALU.mult)\
                        .then_inc(*V(f"A_T {q} {b}"))
            dve.wait_ge(*after("eg"))
            TTn(sm(400, 16), be, sm(368, 16), ALU.mult).then_inc(*V("beta eg"))
            TTn(per_head(k_dec), per_head(k_tok[:, 0, :]), spread(sm(384, 8)), ALU.mult).then_inc(*V("k_dec"))
            for n in range(len(LEVELS)):
                for q in range(4):
                    pr = slice(4 * q, 4 * q + 4)
                    y = bank[4 + q][:, :].rearrange("p (x n) -> p x n", x=4)
                    yt = bank[q][:, :].rearrange("p (x n) -> p x n", x=4)
                    if n == 0:
                        dve.wait_ge(*after(f"B_T {n} {q}"))
                        if q == 0:
                            dve.wait_ge(*after("turned 5"))
                        TTn(T_invT[:, pr, :], four(C_ID), B_T[:, q % 2, :, :], ALU.subtract).then_inc(*V(f"TT0 {q}"))
                        dve.wait_ge(*after(f"Y {n} {q}"))
                        TTn(T_inv[:, pr, :], four(C_ID), y, ALU.subtract).then_inc(*V(f"T_invT 0 {q}"))
                        continue
                    if n < len(LEVELS) - 1:
                        dve.wait_ge(*after(f"dT {n} {q}"))
                        TTn(T_inv[:, pr, :], T_inv[:, pr, :], y, ALU.subtract).then_inc(*V(f"T_inv {n} {q}"))
                    dve.wait_ge(*after(f"dTT {n} {q}"))
                    TTn(T_invT[:, pr, :], T_invT[:, pr, :], yt, ALU.subtract).then_inc(*V(f"T_invT {n} {q}"))
            dve.wait_ge(*after("k state"))
            for b in range(2):
                TTn(per_head(k_dec)[:, b::2, :], per_head(bank[3 if b else 0][:, 0:256]), spread(sm(408, 8)[:, b::2]),
                    ALU.mult).then_inc(*V("k state beta" if b else "k state beta 0"))
            dve.wait_ge(*after("k state beta"))
            TTn(vb_tok[:, 1, :], vb_tok[:, 1, :], k_dec, ALU.subtract).then_inc(*V("rhs 1"))
            o0, o1 = mixed[:, 0, 0:GW], mixed[:, 1, 0:GW]
            dve.wait_ge(*after("o 0"))
            nc.vector.tensor_copy(o0, bank[5][:, :]).then_inc(*V("o in place 0"))
            dve.wait_ge(*after("q state"))
            for b in range(2):
                TTn(per_head(o1)[:, b::2, :], per_head(bank[4 if b else 7][:, 0:256]), spread(sm(376, 8)[:, b::2]),
                    ALU.mult).then_inc(*V("o old 1" if b else "o old even"))
            dve.wait_ge(*after("o 1"))
            dve.wait_ge(*after("o old 1"))
            TTn(o1, o1, bank[2][:, :], ALU.add).then_inc(*V("o in place 1"))
            for t in range(TT):
                dve.wait_ge(*after(f"o in place {t}"))
                TTn(squares[:, t, :], mixed[:, t, 0:GW], mixed[:, t, 0:GW], ALU.mult).then_inc(*V(f"o squares {t}"))
                dve.wait_ge(*after(f"o squares {t}"))
                nc.vector.tensor_reduce(sm(416 + 8 * t, 8), per_head(squares[:, t, :]), AX.X, ALU.add)\
                    .then_inc(*V(f"o square sums {t}"))
            rn2 = small[:, 432:480].rearrange("p (s n) -> p s n", s=3)
            dve.wait_ge(*after("o square sums 1"))
            rsqrt(dve, "o unit", rn2, sm(416, 16), RMS_EPS, 1.0 / GD)
            dve.wait_ge(*after("o unit"))
            for t in range(TT):
                o = per_head(mixed[:, t, 0:GW])
                TTn(o, o, spread(rn2[:, 0, 8 * t:8 * t + 8]), ALU.mult).then_inc(*V(f"o a {t}"))
                dve.wait_ge(*after(f"o a {t}"))
                TTn(o, o, pv_gnorm.unsqueeze(1).to_broadcast([P, GH, GD]), ALU.mult).then_inc(*V(f"o b {t}"))
                dve.wait_ge(*after(f"o b {t}"))
                TTn(mixed[:, t, 0:GW], mixed[:, t, 0:GW], silu_z[:, t, :], ALU.mult).then_inc(*V(f"gdn {t}"))

        def mixer_gpsimd(pool, g0):
            lo = lambda n: make_lo(pool, lo_pool, g0 + n)
            nc.gpsimd.memset(conv_in[:, :, 0:3], 0.0).then_inc(*G("pads"))
            for n in range(3, 16):
                lo(n)
            four = lambda n: tab[:, C_LV + P * n:C_LV + P * n + P].unsqueeze(1).to_broadcast([P, 4, P])
            for n in range(len(LEVELS)):
                for q in range(4):
                    if n == 0:
                        pool.wait_ge(*after(f"A_T {q} 1"))
                        if q == 0:
                            pool.wait_ge(*after("v tokens 1"))
                    if q >= 2:
                        pool.wait_ge(*after(f"Y {n} {q - 2}"))
                        if n == 0:
                            pool.wait_ge(*after(f"TT0 {q - 2}"))
                    elif n >= 1:
                        pool.wait_ge(*after(f"Y {n - 1} {q + 2}"))
                        if n == 1:
                            pool.wait_ge(*after(f"TT0 {q + 2}"))
                    nc.gpsimd.tensor_tensor(B_T[:, q % 2, :, :], A_T[:, 4 * q:4 * q + 4, :], four(n), ALU.mult)\
                        .then_inc(*G(f"B_T {n} {q}"))

        sb_z = place("sb_z", 0, 3, 512)
        sb_e = place("sb_e", 4096, 3, 512)
        sb_sp = place("sb_sp", 6192, 3, 512)
        SB_GROUPS = [(0, 0), (0, 1), (1, 1)]
        w_uq = place("w_uq", 13360, 2, MH * MD)
        w_ukv = arena[:, 14128:14128 + MH * (MN + MV)]
        l_unit = place("l_unit", 2048, TT, MQ + MKV)
        l_T = place("l_T", 2816, 3, SEQ)
        l_val = place("l_val", 3584, TT, MH, MV)
        l_q = place("l_q", 8240, TT, MH, MD)
        l_k = place("l_k", 9008, TT, MH, MD)
        rot = arena[:, 9776:10288].rearrange("p (m t h n) -> p m t h n", m=4, t=TT, h=MH)
        rotk = arena[:, 12848:12976].rearrange("p (m t n) -> p m t n", m=4, t=TT)
        l_qT = arena[0:MD, 10288:11312].rearrange("p (h n) -> p h n", h=MH)
        l_kT = arena[0:MD, 11312:12336].rearrange("p (h n) -> p h n", h=MH)
        l_s = [place("l_s0", 12336, MH, P), place("l_s1", 16432, MH, SEQ)]
        l_pT = place("l_pT", 17456, 12, P)

        def head_half(x):
            return slice(64 * (x % 2), 64 * (x % 2) + 64)

        def sb_bank(n, x):
            b = bank[(3, 4, 0, 1)[2 * (n // 2) + x % 2]]
            c = 256 * (n % 2) + P * (x // 2)
            return b[:, c:c + P]

        def attention_load(sp, l):
            sp.wait_ge(*after("q state"))
            nc.sync.dma_start(w_uq[:, :, :], A["mla_w_uq"].rearrange("l (k p) n -> p (l k) n", p=P)[:, bass.ds(l * 2, 2), :])\
              .then_inc(params[3], 16)
            nc.sync.dma_start(w_ukv, A["mla_w_ukv"].rearrange("l k n -> (l k) n")[bass.ds(l * MKV, MKV), :])\
              .then_inc(params[3], 16)

        def attention_tensor(pe):
            cb = [bank[6], bank[7], bank[5]]
            pe.wait_ge(*after("o old 1"))
            for n, (kt, qt) in enumerate(SB_GROUPS):
                for x in range(SBH):
                    m = nc.tensor.matmul(sb_bank(n, x), skT[head_half(x), x // 2, tokens(kt)],
                                         sqT[head_half(x), x // 2, tokens(qt)], start=True, stop=True)
                m.then_inc(*T(f"sb z {n}"))
            for n in range(3):
                pe.wait_ge(*after(f"sb sp {n}"))
                if n == 0:
                    pe.wait_ge(*after("o in place 0"))
                if n == 1:
                    pe.wait_ge(*after("sb sp 2"))
                    nc.tensor.matmul(cb[n][:, :], tab[:, C_ONE:C_ONE + P], sb_sp[:, 2, :], start=True, stop=False)
                nc.tensor.matmul(cb[n][:, :], tab[:, C_LI:C_LI + P], sb_sp[:, n, :], start=n != 1, stop=True)\
                    .then_inc(*T(f"sb rest {n}"))
            for k in range(3):
                for t in range(TT):
                    pe.wait_ge(*after(f"l unit {t} {0 if k < 2 else 1}"))
                    if k == 0 and t == 0:
                        pe.wait_ge(*after("o in place 1"))
                        pe.wait_ge(*after("sb zp 2"))
                    o = bank[2 if k < 2 else 4]
                    m = nc.tensor.transpose(o[:, 256 * (k % 2) + P * t:256 * (k % 2) + P * t + P],
                                            l_unit[:, t, P * k:P * k + P], ident)
                if k >= 1:
                    m.then_inc(*T(f"l turned {k - 1}"))
            for n in range(3):
                pe.wait_ge(*after(f"sb w {n}"))
            for t in range(TT):
                for x in range(SBH):
                    o = bank[3][:, 256 * t + 64 * x:256 * t + 64 * x + 64]
                    gs = [(0, 0)] if t == 0 else [(1, 0), (2, 1)]
                    for i, (n, kt) in enumerate(gs):
                        m = nc.tensor.matmul(o, sb_e[:, n, P * x:P * x + P], s_val[:, kt, 64 * x:64 * x + 64],
                                             start=i == 0, stop=i == len(gs) - 1)
            m.then_inc(*T("sb out"))
            pe.wait_ge(params[3], 32)
            pe.wait_ge(*after("l T 1"))
            pe.wait_ge(*after("sb d 2"))
            pe.wait_ge(*after("o in place 0"))
            for t in range(TT):
                for k in range(2):
                    m = nc.tensor.matmul(bank[4 + t if t else 1][:, 0:MH * MD], l_T[:, k, tokens(t)], w_uq[:, k, :],
                                         start=k == 0, stop=k == 1)
                m.then_inc(*T(f"l q {t}"))
                nc.tensor.matmul(bank[6 + t][:, :], l_T[:, 2, tokens(t)], w_ukv, start=True, stop=True)\
                    .then_inc(*T(f"l kv {t}"))
            kb = [bank[0], bank[2], bank[4], bank[3]]
            pe.wait_ge(*after("sb out in place"))
            for i, (w, src) in enumerate((("q", l_q), ("k", l_k))):
                for t in range(TT):
                    pe.wait_ge(*after(f"l {w} whole"))
                    for x in range(MH):
                        m = nc.tensor.transpose(kb[2 * i + t][0:MD, P * x:P * x + P], src[:, t, x, :], ident)
                    m.then_inc(*T(f"l {w}T {t}"))
            for w in "qk":
                for t in range(TT):
                    pe.wait_ge(*after(f"l {w}T in place {t}"))
            sbk = [bank[5], bank[6], bank[7]]
            for x in range(MH):
                m = nc.tensor.matmul(sbk[0][:, P * x:P * x + P], l_qT[:, x, 0:P], l_kT[:, x, 0:P], start=True, stop=True)
            m.then_inc(*T("l s 0"))
            for x in range(MH):
                m = nc.tensor.matmul(sbk[1 + x // 2][:, 256 * (x % 2):256 * (x % 2) + 256], l_qT[:, x, P:2 * P],
                                     l_kT[:, x, :], start=True, stop=True)
                if x % 2:
                    m.then_inc(*T(f"l s {1 + x // 2}"))
            pb = [bank[1], bank[0], bank[2]]
            for n in range(3):
                for b in range(4):
                    if n == 0:
                        src = l_s[0][:, b, :]
                    else:
                        x, kt = 2 * (n - 1) + b // 2, b % 2
                        src = l_s[1][:, x, tokens(kt)]
                    pe.wait_ge(*after(f"l p {0 if n == 0 else 1} {b if n == 0 else x}"))
                    m = nc.tensor.transpose(pb[n][:, P * b:P * b + P], src, ident)
                m.then_inc(*T(f"l pT {n}"))
            for n in range(3):
                pe.wait_ge(*after(f"l pT in place {n}"))
            for t in range(TT):
                for x in range(MH):
                    o = bank[3][:, 256 * t + 64 * x:256 * t + 64 * x + 64]
                    blocks = [(x, 0)] if t == 0 else [(4 + 2 * x, 0), (5 + 2 * x, 1)]
                    for i, (b, kt) in enumerate(blocks):
                        m = nc.tensor.matmul(o, l_pT[:, b, :], l_val[:, kt, x, :], start=i == 0,
                                             stop=i == len(blocks) - 1)
            m.then_inc(*T("l out"))

        def attention_scalar(act):
            copy = lambda o, i: nc.scalar.activation(o, i, ACT.Copy)
            for n in range(3):
                act.wait_ge(*after(f"sb zp {n}"))
                if n == 0:
                    act.wait_ge(*after(f"dTT {len(LEVELS) - 1} 3"))
                nc.scalar.activation(sb_e[:, n, :], sb_z[:, n, :], ACT.Abs).then_inc(*S(f"sb abs {n}"))
                act.wait_ge(*after(f"sb abs {n}"))
                nc.scalar.activation(sb_e[:, n, :], sb_e[:, n, :], ACT.Exp, scale=-1.0).then_inc(*S(f"sb exp {n}"))
                act.wait_ge(*after(f"sb exp {n}"))
                nc.scalar.activation(sb_e[:, n, :], sb_e[:, n, :], ACT.Ln, bias=1.0).then_inc(*S(f"sb ln {n}"))
            act.wait_ge(*after("l turned 0"))
            copy(l_T[:, 0:2, :], bank[2][:, :].rearrange("p (k n) -> p k n", k=2)).then_inc(*S("l T 0"))
            act.wait_ge(*after("l turned 1"))
            copy(l_T[:, 2, :], bank[4][:, 0:SEQ]).then_inc(*S("l T 1"))
            for n in range(3):
                act.wait_ge(*after(f"sb d {n}"))
                nc.scalar.activation(sb_e[:, n, :], sb_e[:, n, :], ACT.Exp).then_inc(*S(f"sb w {n}"))
            act.wait_ge(*after("sb out"))
            copy(mixed[:, :, GW:GW + SBW], bank[3][:, :].rearrange("p (t n) -> p t n", t=TT)).then_inc(*S("sb out in place"))
            for t in range(TT):
                act.wait_ge(*after(f"l q {t}"))
                copy(l_q[:, t, :, :], bank[4 + t if t else 1][:, 0:MH * MD].rearrange("p (h n) -> p h n", h=MH))\
                    .then_inc(*S(f"l q in place {t}"))
                act.wait_ge(*after(f"l kv {t}"))
                kv = bank[6 + t][:, :].rearrange("p (h n) -> p h n", h=MH)
                copy(l_k[:, t, :, 0:MN], kv[:, :, 0:MN]).then_inc(*S(f"l k plain {t}"))
                copy(l_val[:, t, :, :], kv[:, :, MN:MN + MV]).then_inc(*S(f"l val {t}"))
            kb = [bank[0], bank[2], bank[4], bank[3]]
            for i, (w, dst) in enumerate((("q", l_qT), ("k", l_kT))):
                for t in range(TT):
                    act.wait_ge(*after(f"l {w}T {t}"))
                    copy(dst[:, :, tokens(t)], kb[2 * i + t][0:MD, :].rearrange("p (h n) -> p h n", h=MH))\
                        .then_inc(*S(f"l {w}T in place {t}"))
            act.wait_ge(*after("l minus max 0"))
            act.wait_ge(*after("l minus max 1"))
            for t in range(TT):
                for x in range(MH):
                    k = 4 * t + x
                    nc.scalar.activation(l_s[t][:, x, :], l_s[t][:, x, :], ACT.Exp, bias=small[:, 104 + k:105 + k],
                                         accum_out=small[:, 112 + k:113 + k]).then_inc(*S(f"l p {t} {x}"))
            pb = [bank[1], bank[0], bank[2]]
            act.wait_ge(*after("gdn 1"))
            for n in range(3):
                act.wait_ge(*after(f"l pT {n}"))
                copy(l_pT[:, 4 * n:4 * n + 4, :], pb[n][:, :].rearrange("p (b n) -> p b n", b=4))\
                    .then_inc(*S(f"l pT in place {n}"))

        def attention_vector(dve):
            TTn, TS, STT = nc.vector.tensor_tensor, nc.vector.tensor_scalar, nc.vector.scalar_tensor_tensor
            cb = [bank[6], bank[7], bank[5]]
            four = lambda x, n=P: x.unsqueeze(1).to_broadcast([P, 4, n])
            h4 = lambda x: x.rearrange("p (h n) -> p h n", h=4)
            for n in range(3):
                dve.wait_ge(*after(f"sb z {max(n, 1)}"))
                for b in range(2):
                    src = bank[(3, 4, 0, 1)[2 * (n // 2) + b]][:, 256 * (n % 2):256 * (n % 2) + 256]
                    src = src.rearrange("p (h n) -> p h n", h=2)
                    o = h4(sb_z[:, n, :])[:, b::2, :]
                    if n == 1:
                        ins = TS(o, src, SBD ** -0.5, None, ALU.mult)
                    else:
                        ins = STT(o, src, SBD ** -0.5,
                                  tab[:, C_NS:C_NS + P].unsqueeze(1).to_broadcast([P, 2, P]), ALU.mult, ALU.add)
                    ins.then_inc(*V(f"sb zp {n}" if b else f"sb zp even {n}"))
            sq = small[:, 64:68]
            for t in range(TT):
                for b, c, w in ((0, 0, MQ), (1, MQ, MKV)):
                    x = latent[:, t, 16 + c:16 + c + w]
                    nc.vector.tensor_tensor_reduce(l_unit[:, t, c:c + w], x, x, 1.0 / w, 0.0, ALU.mult, ALU.add,
                                                   sq[:, 2 * t + b:2 * t + b + 1]).then_inc(*V(f"l squares {t} {b}"))
            dve.wait_ge(*after("l squares 1 1"))
            lr = small[:, 68:80].rearrange("p (s n) -> p s n", s=3)
            rsqrt(dve, "l rms", lr, sq, RMS_EPS)
            dve.wait_ge(*after("l rms"))
            for t in range(TT):
                for b, c, w in ((0, 0, MQ), (1, MQ, MKV)):
                    STT(l_unit[:, t, c:c + w], latent[:, t, 16 + c:16 + c + w], lr[:, 0, 2 * t + b:2 * t + b + 1],
                        pv_qn[:, c:c + w], ALU.mult, ALU.mult).then_inc(*V(f"l unit {t} {b}"))
            for n in (0, 2, 1):
                dve.wait_ge(*after(f"sb ln {n}"))
                STT(sb_sp[:, n, :], sb_z[:, n, :], 0.0, sb_e[:, n, :], ALU.max, ALU.add).then_inc(*V(f"sb sp {n}"))
            cos, sin = rope1[:, 0, :, :], rope1[:, 1, :, :]
            kr = latent[:, :, 16 + MQ + MKV:16 + MLW]
            hm = MR // 2
            TTn(rotk[:, 0], kr[:, :, 0:hm], cos, ALU.mult).then_inc(*V("rk 0"))
            TTn(rotk[:, 1], kr[:, :, hm:MR], sin, ALU.mult).then_inc(*V("rk 1"))
            TTn(rotk[:, 2], kr[:, :, hm:MR], cos, ALU.mult).then_inc(*V("rk 2"))
            TTn(rotk[:, 3], kr[:, :, 0:hm], sin, ALU.mult).then_inc(*V("rk 3"))
            dve.wait_ge(*after("rk 3"))
            over = lambda x: x.unsqueeze(1).to_broadcast([P, MH, hm])
            dve.wait_ge(*after("v_new 1"))
            for t in range(TT):
                TTn(l_k[:, t, :, MN:MN + hm], over(rotk[:, 0, t]), over(rotk[:, 1, t]), ALU.subtract).then_inc(*V(f"rk a {t}"))
                TTn(l_k[:, t, :, MN + hm:MD], over(rotk[:, 2, t]), over(rotk[:, 3, t]), ALU.add).then_inc(*V(f"rk b {t}"))
            for n in (0, 1, 2):
                dve.wait_ge(*after(f"sb rest {n}"))
                TTn(sb_e[:, n, :], sb_z[:, n, :], cb[n][:, :], ALU.subtract).then_inc(*V(f"sb d {n}"))
            for t in range(TT):
                dve.wait_ge(*after(f"l q in place {t}"))
                x1, x2 = l_q[:, t, :, MN:MN + hm], l_q[:, t, :, MN + hm:MD]
                c, s = over(cos[:, t]), over(sin[:, t])
                TTn(rot[:, 0, t], x1, c, ALU.mult).then_inc(*V(f"rq 0 {t}"))
                TTn(rot[:, 1, t], x2, s, ALU.mult).then_inc(*V(f"rq 1 {t}"))
                TTn(rot[:, 2, t], x2, c, ALU.mult).then_inc(*V(f"rq 2 {t}"))
                TTn(rot[:, 3, t], x1, s, ALU.mult).then_inc(*V(f"rq 3 {t}"))
            dve.wait_ge(*after("rq 3 1"))
            TTn(l_q[:, 0, :, MN:MN + hm], rot[:, 0, 0], rot[:, 1, 0], ALU.subtract).then_inc(*V("rq a 0"))
            TTn(l_q[:, 1, :, MN:MN + hm], rot[:, 0, 1], rot[:, 1, 1], ALU.subtract).then_inc(*V("rq a 1"))
            TTn(l_q[:, 0, :, MN + hm:MD], rot[:, 2, 0], rot[:, 3, 0], ALU.add).then_inc(*V("rq b 0"))
            TTn(l_q[:, 1, :, MN + hm:MD], rot[:, 2, 1], rot[:, 3, 1], ALU.add).then_inc(*V("l q whole"))
            dve.wait_ge(*after("l val 1"))
            dve.wait_ge(*after("rk b 1"))
            nc.vector.tensor_copy(rotk[:, 0, 0, 0:1], rotk[:, 1, 0, 0:1]).then_inc(*V("l k whole"))
            scale = MD ** -0.5
            dve.wait_ge(*after("l s 0"))
            STT(l_s[0], h4(bank[5][:, :]), scale, four(tab[:, C_NC + P:C_NC + 2 * P]), ALU.mult, ALU.add).then_inc(*V("l s masked 0"))
            for b in range(2):
                dve.wait_ge(*after(f"l s {1 + b}"))
                STT(l_s[1][:, 2 * b:2 * b + 2, :], bank[6 + b][:, :].rearrange("p (h n) -> p h n", h=2), scale,
                    tab[:, C_NC:C_NC + 2 * P].unsqueeze(1).to_broadcast([P, 2, 2 * P]), ALU.mult, ALU.add)\
                    .then_inc(*V(f"l s masked {1 + b}"))
            for t in range(TT):
                dve.wait_ge(*after(f"l s masked {2 * t}"))
                nc.vector.tensor_reduce(small[:, 96 + 4 * t:100 + 4 * t], l_s[t], AX.X, ALU.max).then_inc(*V(f"l max {t}"))
                dve.wait_ge(*after(f"l max {t}"))
                TS(small[:, 104 + 4 * t:108 + 4 * t], small[:, 96 + 4 * t:100 + 4 * t], -1.0, None, ALU.mult)\
                    .then_inc(*V(f"l minus max {t}"))
            dve.wait_ge(*after("l p 1 3"))
            nc.vector.reciprocal(small[:, 120:128], small[:, 112:120]).then_inc(*V("l rec"))
            dve.wait_ge(*after("l rec"))
            dve.wait_ge(*after("l out"))
            for t in range(TT):
                TTn(h4(mixed[:, t, GW + SBW:D]), h4(bank[3][:, 256 * t:256 * t + 256]),
                    small[:, 120 + 4 * t:124 + 4 * t].unsqueeze(2).to_broadcast([P, MH, MV]), ALU.mult)\
                    .then_inc(*V(f"mixed {t}"))

        G_MIX = 3 * FF_STEPS
        G_WO = G_MIX + 13
        G_FFB = G_WO + 4
        G_PLE = G_FFB + 3 * FF_STEPS
        G_END = G_PLE + 5

        p_tok = place("p_tok", 2048, TT, PLE)
        p_proj = place("p_proj", 0, TT, D)
        p_gate = place("p_gate", 4096, TT, D)

        def wide_product(pe, g, n, left, name, k_step=2):
            for i in range(n):
                await_slab(pe, g + i)
                wide_slab(g + i, left, k_step * i, i == 0, i == n - 1, name).then_inc(slab_used, 1)

        def acc_ready(name, last):
            return lambda t: after(name) if t == 0 else (slab_used, last + 1)

        with nc.Block() as block:
            st.start("setup")

            @block.sync
            def _(sp):
                nc.sync.dma_start(h[:, :, :], A["x"].rearrange("b (t p) d -> p (b t) d", p=P)).then_inc(stored, 16)
                nc.sync.dma_start(tab[:, :], A["tables"][:, :]).then_inc(params[1], 16)
                nc.sync.dma_start(arena[:, 0:TT].bitcast(I32), A["positions"].rearrange("b (t p) -> p (b t)", p=P),
                                  allow_slow_non_contiguous=True)\
                  .then_inc(params[1], 16)
                sp.wait_ge(stored, 16)

            @block.vector
            def _(dve):
                TS, STT = nc.vector.tensor_scalar, nc.vector.scalar_tensor_tensor
                n = MR // 2
                pos, ang, turns = arena[:, 2:4], place("ang", 8, TT, n), place("turns", 64, 2, TT * n)
                two_pi = 2 * math.pi
                p1 = 6.28125
                p2 = 0.00193500518798828125
                p3 = two_pi - p1 - p2
                k = [0]

                def link(ins):
                    k[0] += 1
                    ins.then_inc(*V(f"angle {k[0]}"))
                    dve.wait_ge(*after(f"angle {k[0]}"))

                dve.wait_ge(params[1], 32)
                link(nc.vector.tensor_copy(pos, arena[:, 0:TT].bitcast(I32)))
                for t in range(TT):
                    link(TS(ang[:, t, :], tab[:, C_INV:C_INV + n], pos[:, t:t + 1], None, ALU.mult))
                a = ang[:, :, :].rearrange("p t n -> p (t n)")
                for which, shift in ((0, 0.25), (1, 0.0)):
                    w = turns[:, which, :]
                    o = rope1[:, which, :, :].rearrange("p t n -> p (t n)")
                    link(TS(w, a, 1 / two_pi, shift, ALU.mult, ALU.add))
                    link(TS(w, w, 12582912.0, None, ALU.add))
                    link(TS(w, w, -12582912.0, None, ALU.add))
                    link(STT(o, w, -p1, a, ALU.mult, ALU.add))
                    link(STT(o, w, -p2, o, ALU.mult, ALU.add))
                    link(STT(o, w, -p3, o, ALU.mult, ALU.add))
                    link(TS(o, o, shift * two_pi, None, ALU.add))
                    link(TS(o, o, 3.1415925, -3.1415925, ALU.min, ALU.max))
                nc.vector.tensor_copy(pos, pos).then_inc(*V("angles"))

            @block.scalar
            def _(act):
                act.wait_ge(*after("angles"))
                o = rope1[:, :, :, :].rearrange("p b t n -> p (b t n)")
                nc.scalar.activation(o, o, ACT.Sin).then_inc(*S("rotary"))
                act.wait_ge(*after("rotary"))

        def clear():
            with nc.Block() as block:
                @block.gpsimd
                def _(pool):
                    for s in every:
                        pool.sem_clear(s)

        clear()
        with nc.Fori(0, DEPTH) as layer:
            with nc.Block() as block:
                st.start("layer")
                flat2 = lambda name: A[name].rearrange("l k n -> (l k) n")
                m0, m4 = G_MIX, G_WO

                def norm_row(which, c):
                    return A[which].rearrange("l c n -> (l c) n")[bass.ds(layer * 3 + c, 1), :].rearrange("a n -> (a n)")

                @block.sync
                def _(sp):
                    def norm(nth, free):
                        load_norm(sp, nth, norm_row("ln_g", nth), norm_row("ln_b", nth), free)

                    norm(0, None)
                    small_loads(sp, layer)
                    ff_load(sp, 0, flat2("ffa_w_in"), layer * D, flat2("ffa_w_out"), layer * D_FF)
                    mixer_load(sp, m0, layer)
                    attention_load(sp, layer)
                    norm(1, "tm turned 3")
                    ff_load(sp, G_FFB, flat2("ffb_w_in"), layer * D, flat2("ffb_w_out"), layer * D_FF)
                    norm(2, "n1 done 1")
                    nc.sync.dma_start(p_tok[:, :, :], A["p"].rearrange("l b (t p) n -> p (l b t) n", p=P)[:, bass.ds(layer * TT, TT), :])\
                      .then_inc(params[4], 16)
                    load_slab(sp, G_PLE, 0, wide_parts(flat2("ple_w_proj"), layer * PLE))
                    for n in range(4):
                        load_slab(sp, G_PLE + 1 + n, 0, wide_parts(flat2("ple_w_gate"), layer * D + 2 * P * n))

                @block.tensor
                def _(pe):
                    turn_tensor(pe, "ta", h, None)
                    pe.wait_ge(*after("ta lo 3"))
                    ff_tensor(pe, 0, 0, "ffa out")
                    turn_tensor(pe, "tb", h, lambda t: after(f"n0 done {t}"))
                    pe.wait_ge(*after("tb lo 3"))
                    mixer_tensor(pe, m0)
                    attention_tensor(pe)
                    for w in ("gdn 0", "gdn 1", "sb out in place", "mixed 0", "l pT in place 2"):
                        pe.wait_ge(*after(w))
                    turn_tensor(pe, "tm", mixed, lambda t: after(f"mixed {t}"))
                    pe.wait_ge(*after("tm lo 3"))
                    wide_product(pe, m4, 4, (xhi, xlo), "wo out")
                    turn_tensor(pe, "tc", h, lambda t: after(f"n1 done {t}"))
                    pe.wait_ge(*after("tc lo 3"))
                    ff_tensor(pe, G_FFB, 1, "ffb out")
                    pe.wait_ge(params[4], 16)
                    pe.wait_ge(ff_lo, 2 * FF_STEPS)
                    for k in range(2):
                        for t in range(TT):
                            m = nc.tensor.transpose(bank[6][:, 256 * k + P * t:256 * k + P * t + P],
                                                    p_tok[:, t, P * k:P * k + P], ident)
                    m.then_inc(*T("p turned"))
                    pe.wait_ge(*after("p lo"))
                    for t in range(TT):
                        pe.wait_ge(*after(f"n2 done {t}"))
                    wide_product(pe, G_PLE, 1, (ahi, alo), "proj out")
                    turn_tensor(pe, "td", h, lambda t: after(f"n2 done {t}"))
                    pe.wait_ge(*after("td lo 3"))
                    pe.wait_ge(*after("proj in place 3"))
                    wide_product(pe, G_PLE + 1, 4, (xhi, xlo), "gate out")

                @block.scalar
                def _(act):
                    for g in range(RING):
                        make_hi(act, g)
                    turn_scalar(act, "ta")
                    ff_scalar(act, 0, 0, True)
                    turn_scalar(act, "tb")
                    mixer_scalar(act, m0)
                    attention_scalar(act)
                    turn_scalar(act, "tm")
                    for n in range(4):
                        make_hi(act, m4 + 3 + n)
                    turn_scalar(act, "tc")
                    ff_scalar(act, G_FFB, 1, True)
                    act.wait_ge(*after("p turned"))
                    nc.scalar.activation(flat(ahi), bank[6][:, :], ACT.Copy).then_inc(*S("p hi"))
                    make_hi(act, G_PLE + 3)
                    for n in range(4):
                        t, b = n // 2, n % 2
                        act.wait_ge(slab_used, G_PLE + 1)
                        nc.scalar.activation(p_proj[:, t, 512 * b:512 * b + 512], acc[t][b][:, :], ACT.Copy)\
                            .then_inc(*S(f"proj in place {n}"))
                    turn_scalar(act, "td")
                    make_hi(act, G_PLE + 4)
                    for n in range(4):
                        t, b = n // 2, n % 2
                        act.wait_ge(*acc_ready("gate out", G_END - 1)(t))
                        nc.scalar.activation(p_gate[:, t, 512 * b:512 * b + 512], acc[t][b][:, :], ACT.Tanh, scale=0.5)\
                            .then_inc(*S(f"gate tanh {n}"))

                @block.vector
                def _(dve):
                    for g in range(RING):
                        make_lo(dve, lo_dve, g)
                    turn_vector(dve, "ta")
                    ff_vector(dve, 0, 0, True)
                    norm_vector(dve, "n0", 0.5 / ALPHA, acc_ready("ffa out", G_MIX - 1), 0)
                    turn_vector(dve, "tb")
                    mixer_vector(dve, m0)
                    attention_vector(dve)
                    turn_vector(dve, "tm")
                    for n in range(4):
                        make_lo(dve, lo_dve, m4 + 3 + n)
                    norm_vector(dve, "n1", 1.0 / ALPHA, acc_ready("wo out", G_FFB - 1), 1)
                    turn_vector(dve, "tc")
                    ff_vector(dve, G_FFB, 1, True)
                    dve.wait_ge(*after("p hi"))
                    nc.vector.tensor_tensor(flat(alo), bank[6][:, :], flat(ahi).bitcast(F32), ALU.subtract).then_inc(*V("p lo"))
                    norm_vector(dve, "n2", 0.5 / ALPHA, acc_ready("ffb out", G_PLE - 1), 2)
                    make_lo(dve, lo_dve, G_PLE + 3)
                    turn_vector(dve, "td")
                    make_lo(dve, lo_dve, G_PLE + 4)
                    for n in range(4):
                        t, c = n // 2, slice(512 * (n % 2), 512 * (n % 2) + 512)
                        dve.wait_ge(*after(f"gate tanh {n}"))
                        dve.wait_ge(*after(f"proj in place {n}"))
                        nc.vector.scalar_tensor_tensor(p_gate[:, t, c], p_gate[:, t, c], 1.0, p_proj[:, t, c],
                                                       ALU.add, ALU.mult).then_inc(*V(f"gated p {n}"))
                        dve.wait_ge(*after(f"gated p {n}"))
                        nc.vector.scalar_tensor_tensor(h[:, t, c], p_gate[:, t, c], 0.5, h[:, t, c],
                                                       ALU.mult, ALU.add).then_inc(*V(f"layer done {n}"))

                @block.gpsimd
                def _(pool):
                    for g in range(RING):
                        make_lo(pool, lo_pool, g)
                    ff_gpsimd(pool, 0, True)
                    mixer_gpsimd(pool, m0)
                    for n in range(4):
                        make_lo(pool, lo_pool, m4 + 3 + n)
                    ff_gpsimd(pool, G_FFB, True)
                    for n in range(2):
                        make_lo(pool, lo_pool, G_PLE + 3 + n)

            clear()

        G_IN = 3 * FF_STEPS
        IN_ORDER = ("x0", "x1", "q0", "q1", "kv", "g0", "g1", "l0", "l1", "a0", "a1")
        IN_COL = {"g0": 0, "g1": 512, "x0": LRU, "x1": LRU + 512, "q0": 2 * LRU, "q1": 2 * LRU + 512,
                  "kv": 2 * LRU + QW, "l0": 3584, "l1": 4096, "a0": 4608, "a1": 5120}
        assert IN_COL["kv"] + 2 * KVW == IN_COL["l0"] and IN_COL["a1"] + 512 == IN2
        G_PL = G_IN + 2 * len(IN_ORDER)
        G_PA, G_OUT2 = G_PL + 4, G_PL + 8
        G_FF2 = G_PL + 12
        first = {c: G_IN + 2 * n for n, c in enumerate(IN_ORDER)}
        ready = {c: (slab_used, first[c] + 2) for c in IN_ORDER}
        pair = {c: (bank[0:2], bank[2:4])[n % 2] for n, c in enumerate(IN_ORDER)}

        x_norm = place("x_norm", 0, TT, D)
        lru_h = place("lru_h", 0, LT, SEQ)
        lru_in = place("lru_in", 2048, LT, SEQ + 4)
        lru_a = place("lru_a", 2048, LT, SEQ)
        lru_x = place("lru_x", 4128, LT, SEQ)
        lru_w = place("lru_w", 6176, 2, LT, P)
        lru_i = place("lru_i", 8224, LT, SEQ)
        lru_m = place("lru_m", 10272, LT, SEQ)
        scores = [place("scores0", 2048, 2, 4, P), place("scores1", 3072, 2, 4, 2 * P)]
        probs_T = place("probs_T", 5120, 12, P)
        gate_l = place("gate_l", 8224, TT, D)
        gate_a = place("gate_a", 10272, TT, D)
        q_rot = place("q_rot", 12320, TT, QH, HD)
        y_attn = place("y_attn", 12320, TT, D)
        k_rot = arena[:, 14368:15392].rearrange("p (t h b n) -> p t h b n", t=TT, h=KVH, b=2)
        v_win = place("v_win", 15392, TT, KVW)
        qT2 = place("qT2", 15904, QH // 2, SEQ)
        kT2 = place("kT2", 17952, KVH, SEQ)
        gelu_g = place("gelu_g", 18976, 2, 2, SEQ)
        merged = place("merged", 2048, TT, D)
        rows64 = arena[0:64, 20000:20000 + P]
        rot_t = gated[:, :, :, :].rearrange("p a b c -> p (a b c)").rearrange("p (m h n) -> p m h n", m=4, h=8)
        pc = pv[:, 0:64]
        half_b = pv[:, 64:80]
        lru_c = pv[:, 80:88]
        lam_t = pv[:, 88:104]
        sinks = pv[:, 104:120]

        pre_gain, post_gain = params[0], params[5]

        def gain_load(sp, side, w, free):
            if free:
                sp.wait_ge(*after(free))
            nc.sync.dma_start(normw[:, side, :], A[w].rearrange("a n -> (a n)").partition_broadcast(P))\
              .then_inc((pre_gain, post_gain)[side], 16)

        def pre_scalar(act, name, src_ready):
            for t in range(TT):
                if src_ready:
                    act.wait_ge(*after(f"{src_ready} {t}"))
                nc.scalar.activation(x_norm[:, t, :], h[:, t, :], ACT.Square, accum_out=small[:, 40 + t:41 + t])\
                    .then_inc(*S(f"{name} squares {t}"))

        def pre_vector(dve, name, nth):
            rs = small[:, 44:50].rearrange("p (s n) -> p s n", s=3)
            dve.wait_ge(*after(f"{name} squares 1"))
            rsqrt(dve, f"{name} rms", rs, small[:, 40:42], RMS_EPS, 1.0 / D)
            dve.wait_ge(*after(f"{name} rms"))
            dve.wait_ge(pre_gain, 16 * (nth + 1))
            for t in range(TT):
                nc.vector.scalar_tensor_tensor(x_norm[:, t, :], h[:, t, :], rs[:, 0, t:t + 1], normw[:, 0, :],
                                               ALU.mult, ALU.mult).then_inc(*V(f"{name} unit {t}"))

        def post_scalar(act, name, done):
            for t in range(TT):
                act.wait_ge(*done(t))
                for b in range(2):
                    nc.scalar.activation(x_norm[:, t, 512 * b:512 * b + 512], acc[t][b][:, :], ACT.Square,
                                         accum_out=small[:, 50 + 2 * t + b:51 + 2 * t + b])\
                        .then_inc(*S(f"{name} squares {t} {b}"))

        def post_vector(dve, name, c, eps, nth):
            for t in range(TT):
                rs = small[:, 54 + 3 * t:57 + 3 * t].rearrange("p (s n) -> p s n", s=3)
                dve.wait_ge(*after(f"{name} squares {t} 1"))
                nc.vector.tensor_tensor(small[:, 60 + t:61 + t], small[:, 50 + 2 * t:51 + 2 * t],
                                        small[:, 51 + 2 * t:52 + 2 * t], ALU.add).then_inc(*V(f"{name} sum {t}"))
                dve.wait_ge(*after(f"{name} sum {t}"))
                rsqrt(dve, f"{name} rms {t}", rs, small[:, 60 + t:61 + t], eps, 1.0 / D)
                dve.wait_ge(*after(f"{name} rms {t}"))
                dve.wait_ge(post_gain, 16 * (nth + 1))
                for b in range(2):
                    k = slice(512 * b, 512 * b + 512)
                    nc.vector.scalar_tensor_tensor(x_norm[:, t, k], acc[t][b][:, :], rs[:, 0, 0:1], normw[:, 1, k],
                                                   ALU.mult, ALU.mult).then_inc(*V(f"{name} unit {t} {b}"))
                    dve.wait_ge(*after(f"{name} unit {t} {b}"))
                    nc.vector.scalar_tensor_tensor(h[:, t, k], x_norm[:, t, k], c, h[:, t, k],
                                                   ALU.mult, ALU.add).then_inc(*V(f"{name} {t}" if b else f"{name} half {t}"))

        def two_load(sp):
            W = lambda n: A[n].rearrange("a k n -> (a k) n")
            gain_load(sp, 0, "ffn1_pre_g_2", None)
            gain_load(sp, 1, "ffn1_post_g_2", None)
            for n, (w, k) in enumerate((("conv_w_2", 32), ("conv_b_2", 8), ("lru_b_a_2", 8), ("lru_b_x_2", 8), ("lru_lambda_2", 8))):
                at0 = (0, 32, 40, 48, 56)[n]
                src = A[w].rearrange("a k (c p) -> (a k c) p", p=P) if n == 0 else A[w].rearrange("a (c p) -> (a c) p", p=P)
                nc.sync.dma_start(rows64[at0:at0 + k, :], src).then_inc(params[1], 16)
            nc.sync.dma_start(sinks, A["attn_sinks_2"].rearrange("a n -> (a n)").partition_broadcast(P)).then_inc(params[1], 16)
            ff_load(sp, 0, W("ffn1_w_gu_2"), 0, W("ffn1_w_down_2"), 0)
            gain_load(sp, 0, "mix_pre_g_2", "p1 unit 1")
            sp.wait_ge(*after("lru zeros"))
            for m, w in enumerate(("lru_w_a_2", "lru_w_x_2")):
                for b in range(2):
                    nc.sync.dma_start(lru_w[64 * b:64 * b + 64, m, :, 64 * b:64 * b + 64],
                                      A[w].rearrange("a (c b) k d -> b k (a c) d", b=2)[b]).then_inc(params[2], 16)
            for c in IN_ORDER:
                for half in range(2):
                    load_slab(sp, first[c] + half, 0, col_parts(W("w_in_2"), 0, 4 * half, 4, [(IN_COL[c], 512)]))
            gain_load(sp, 1, "mix_post_g_2", "f1 1")
            gain_load(sp, 0, "ffn2_pre_g_2", "p2 unit 1")
            for g, w in ((G_PL, "w_proj_lru_2"), (G_PA, "w_proj_attn_2"), (G_OUT2, "w_out_2")):
                for n in range(4):
                    load_slab(sp, g + n, 0, wide_parts(W(w), 2 * P * n))
            ff_load(sp, G_FF2, W("ffn2_w_gu_2"), 0, W("ffn2_w_down_2"), 0)
            gain_load(sp, 1, "ffn2_post_g_2", "mx 1")
            for t in range(TT):
                sp.wait_ge(*after(f"f2 {t}"))
                nc.sync.dma_start(out[0, P * t:P * t + P, :], h[:, t, :]).then_inc(stored, 16)
            sp.wait_ge(stored, 32 + 16)

        def window_tensor(pe, g, stage):
            if stage == 0:
                if g == 0:
                    pe.wait_ge(*after("q turned in place 3"))
                    pe.wait_ge(*after("k turned in place 1"))
                else:
                    pe.wait_ge(*after(f"attn {g - 1} 1"))
                for x in range(4):
                    hh = 4 * g + x
                    u = slice(64 * (x % 2), 64 * (x % 2) + 64)
                    b, c = 4 + 2 * (x % 2), x // 2
                    nc.tensor.matmul(bank[b][:, P * c:P * c + P], qT2[u, hh // 2, 0:P], kT2[u, g, 0:P], start=True, stop=True)
                    m = nc.tensor.matmul(bank[b + 1][:, 256 * c:256 * c + 256], qT2[u, hh // 2, P:2 * P], kT2[u, g, :],
                                         start=True, stop=True)
                m.then_inc(*T(f"scores {g}"))
            if stage == 1:
                for n in range(3):
                    for b in range(4):
                        t, x, kt = (0, b, 0) if n == 0 else (1, 2 * (n - 1) + b // 2, b % 2)
                        pe.wait_ge(*after(f"probs {g} {t} {x}"))
                        m = nc.tensor.transpose(bank[4 + n][:, P * b:P * b + P], scores[t][:, g % 2, x, tokens(kt)], ident)
                    m.then_inc(*T(f"probs turned {g} {n}"))
            if stage == 2:
                for n in range(3):
                    pe.wait_ge(*after(f"probs_T {g} {n}"))
                for t in range(TT):
                    for x in range(4):
                        o = bank[7][:, 256 * t + 64 * x:256 * t + 64 * x + 64]
                        blocks = [(x, 0)] if t == 0 else [(4 + 2 * x, 0), (5 + 2 * x, 1)]
                        for i, (b, kt) in enumerate(blocks):
                            m = nc.tensor.matmul(o, probs_T[:, b, :], v_win[:, kt, 64 * g:64 * g + 64],
                                                 start=i == 0, stop=i == len(blocks) - 1)
                m.then_inc(*T(f"attn out {g}"))

        def two_tensor(pe):
            turn_tensor(pe, "ua", x_norm, lambda t: after(f"p1 unit {t}"))
            pe.wait_ge(*after("ua lo 3"))
            ff_tensor(pe, 0, 0, "f1 out")
            pe.wait_ge(params[1], 96)
            turn_tensor(pe, "ub", x_norm, lambda t: after(f"p2 unit {t}"))
            nc.tensor.transpose(bank[4][:, 0:64], rows64, ident[0:64, 0:64]).then_inc(*T("channel rows"))
            pe.wait_ge(*after("ub lo 3"))

            def half_chunk(c, half, free=None):
                if free:
                    pe.wait_ge(*after(free))
                g = first[c] + half
                await_slab(pe, g)
                if c[0] in "xg":
                    m = channel_slab(g, 4 * half, pair[c])
                else:
                    m = token_slab(g, 4 * half, 4, 512, [b[:, :] for b in pair[c]])
                m.then_inc(slab_used, 1)

            def chunk(c, free):
                half_chunk(c, 0, free)
                half_chunk(c, 1)

            chunk("x0", None)
            chunk("x1", None)
            chunk("q0", "evacuated x0 1")
            chunk("q1", "evacuated x1 1")
            pe.wait_ge(params[2], 64)
            for m in range(2):
                for b in range(4):
                    if m:
                        pe.wait_ge(*after(f"lru tanh 0 {2 * b + 1}"))
                    for x in range(2):
                        c = 2 * b + x
                        pe.wait_ge(*after(f"lru conv {c} 3"))
                        i = nc.tensor.matmul(bank[4 + b][:, 256 * x:256 * x + 256], lru_w[:, m, c, :], lru_x[:, c, :],
                                             start=True, stop=True)
                    i.then_inc(*T(f"lru gates {m} {b}"))
            chunk("kv", "rotated q0 1")
            half_chunk("g0", 0, "rotated q1 1")
            for n in range(4):
                pe.wait_ge(*after("rotated q1 1"))
                pe.wait_ge(*after(f"lru tanh 1 {2 * n + 1}"))
                for x in range(2):
                    for t in range(TT):
                        src = q_rot[:, t, 4 * n + 2 * x:4 * n + 2 * x + 2, :].rearrange("p h n -> p (h n)")
                        m = nc.tensor.transpose(bank[4 + n][:, 256 * x + P * t:256 * x + P * t + P], src, ident)
                m.then_inc(*T(f"q turned {n}"))
            half_chunk("g0", 1)
            pe.wait_ge(*after("k doubled"))
            for n in range(2):
                pe.wait_ge(*after(f"q turned in place {n}"))
                for x in range(2):
                    for t in range(TT):
                        src = k_rot[:, t, 2 * n + x, :, :].rearrange("p b n -> p (b n)")
                        m = nc.tensor.transpose(bank[4 + n][:, 256 * x + P * t:256 * x + P * t + P], src, ident)
                m.then_inc(*T(f"k turned {n}"))
            slabs = [(c, half) for c in IN_ORDER[6:] for half in range(2)]
            free = {"g1": "v in place 1", "l0": "gelu g0 1", "l1": "gelu g1 1", "a0": "gate l0 1", "a1": "gate l1 1"}
            for g in range(KVH):
                for stage in range(3):
                    window_tensor(pe, g, stage)
                    if slabs:
                        c, half = slabs.pop(0)
                        half_chunk(c, half, None if half else free[c])
            assert not slabs
            pe.wait_ge(*after("lru lo"))
            pe.wait_ge(*after("gate a0 1"))
            pe.wait_ge(*after("gate a1 1"))
            wide_product(pe, G_PL, 4, (xhi, xlo), "lru out")
            turn_tensor(pe, "uc", y_attn, lambda t: after(f"attn 3 {t}"), (slab_used, G_PL + 4))
            pe.wait_ge(*after("uc lo 3"))
            pe.wait_ge(*after("merged lru 3"))
            wide_product(pe, G_PA, 4, (xhi, xlo), "attn proj out")
            turn_tensor(pe, "ud", merged, lambda t: after(f"merged {2 * t + 1}"))
            pe.wait_ge(*after("ud lo 3"))
            wide_product(pe, G_OUT2, 4, (xhi, xlo), "mix out")
            turn_tensor(pe, "ue", x_norm, lambda t: after(f"p3 unit {t}"))
            pe.wait_ge(*after("ue lo 3"))
            ff_tensor(pe, G_FF2, 1, "f2 out")

        def two_scalar(act):
            act_ = nc.scalar.activation
            copy = lambda o, i: nc.scalar.activation(o, i, ACT.Copy)
            two = lambda b: b[:, :].rearrange("p (c n) -> p c n", c=2)
            made = [G_IN + 3]

            def hi_to(n):
                while made[0] < n:
                    make_hi(act, made[0])
                    made[0] += 1

            for g in range(RING):
                make_hi(act, g)
            pre_scalar(act, "p1", None)
            turn_scalar(act, "ua")
            ff_scalar(act, 0, 0, True)
            post_scalar(act, "f1", acc_ready("f1 out", G_IN - 1))
            pre_scalar(act, "p2", "f1")
            turn_scalar(act, "ub")
            act.wait_ge(*after("channel rows"))
            copy(pc, bank[4][:, 0:64]).then_inc(*S("channel rows in place"))
            act.wait_ge(*after("channel rows in place"))
            act_(lam_t[:, 0:8], pc[:, 56:64], ACT.Abs).then_inc(*S("lam abs"))
            act.wait_ge(*after("lam abs"))
            act_(lam_t[:, 0:8], lam_t[:, 0:8], ACT.Exp, scale=-1.0).then_inc(*S("lam exp"))
            act.wait_ge(*after("lam exp"))
            act_(lam_t[:, 0:8], lam_t[:, 0:8], ACT.Ln, bias=1.0).then_inc(*S("lam ln"))
            for c, k in (("x0", 0), ("x1", 4)):
                hi_to(first[c] + 4)
                for b in range(2):
                    act.wait_ge(*ready[c])
                    copy(lru_in[:, k + 2 * b:k + 2 * b + 2, 3:3 + SEQ], two(pair[c][b])).then_inc(*S(f"evacuated {c} {b}"))
            hi_to(first["q1"] + 4)
            for m, dst in enumerate((lru_a, lru_i)):
                for c in range(LT):
                    act.wait_ge(*after(f"lru gates {m} {c // 2}"))
                    if m == 0 and c == 0:
                        act.wait_ge(*after("half biases"))
                        act.wait_ge(*after("lru conv 7 3"))
                    act_(dst[:, c, :], bank[4 + c // 2][:, 256 * (c % 2):256 * (c % 2) + 256], ACT.Tanh,
                         bias=half_b[:, 8 * m + c:8 * m + c + 1], scale=0.5).then_inc(*S(f"lru tanh {m} {c}"))
                if m == 0:
                    hi_to(first["kv"] + 3)
            act.wait_ge(*after("lru c"))
            for c in range(LT):
                act_(lru_m[:, c, :], lru_a[:, c, :], ACT.Tanh, bias=lru_c[:, c:c + 1], scale=lru_c[:, c:c + 1])\
                    .then_inc(*S(f"lru tanh log a {c}"))
            hi_to(first["kv"] + 4)
            for c in range(LT):
                act.wait_ge(*after(f"lru tanh log a {c}"))
                act_(lru_a[:, c, :], lru_a[:, c, :], ACT.Exp, bias=lru_c[:, c:c + 1], scale=lru_c[:, c:c + 1])\
                    .then_inc(*S(f"lru a {c}"))
            act.wait_ge(*ready["kv"])
            for t in range(TT):
                copy(v_win[:, t, :], pair["kv"][t][:, KVW:2 * KVW]).then_inc(*S(f"v copied {t}"))
            hi_to(first["g0"] + 3)
            for n in range(4):
                act.wait_ge(*after(f"q turned {n}"))
                copy(qT2[:, 2 * n:2 * n + 2, :], two(bank[4 + n])).then_inc(*S(f"q turned in place {n}"))
            hi_to(first["g0"] + 5)
            for n in range(2):
                act.wait_ge(*after(f"k turned {n}"))
                copy(kT2[:, 2 * n:2 * n + 2, :], two(bank[4 + n])).then_inc(*S(f"k turned in place {n}"))
            act.wait_ge(*after("lru mult squared"))
            act_(lru_m[:, :, :], lru_m[:, :, :], ACT.Sqrt).then_inc(*S("lru mult"))

            def gelu(c, k):
                for b in range(2):
                    act.wait_ge(*ready[c])
                    if k:
                        act.wait_ge(*after(f"lru y {2 * b + 1}"))
                    act_(gelu_g[:, b, :, :], two(pair[c][b]), ACT.Gelu_apprx_tanh).then_inc(*S(f"gelu {c} {b}"))

            def gate(c, dst, k):
                for b in range(2):
                    act.wait_ge(*ready[c])
                    if k == 0 and b == 0 and c[0] in "l":
                        act.wait_ge(*after("lru scanned 7"))
                    act_(dst[:, b, k:k + 512], pair[c][b][:, :], ACT.Tanh, scale=0.5).then_inc(*S(f"gate {c} {b}"))

            gelu("g0", 0)
            for g in range(KVH):
                for t in range(TT):
                    act.wait_ge(*after(f"minus max {g} {t}"))
                    for x in range(4):
                        k = 4 * t + x
                        act_(scores[t][:, g % 2, x, :], scores[t][:, g % 2, x, :], ACT.Exp,
                             bias=small[:, 208 + 8 * (g % 2) + k:209 + 8 * (g % 2) + k],
                             accum_out=small[:, 224 + 8 * (g % 2) + k:225 + 8 * (g % 2) + k]).then_inc(*S(f"probs {g} {t} {x}"))
                act.wait_ge(*after(f"sink less max {g}"))
                act_(small[:, 240 + 8 * (g % 2):248 + 8 * (g % 2)], small[:, 240 + 8 * (g % 2):248 + 8 * (g % 2)], ACT.Exp)\
                    .then_inc(*S(f"sink exp {g}"))
                hi_to(min(first["g1"] + 3 + 3 * g + 1, G_PL + 3))
                if g == 0:
                    gelu("g1", 1)
                if g == 1:
                    gate("l0", gate_l, 0)
                if g == 2:
                    gate("l1", gate_l, 512)
                for n in range(3):
                    act.wait_ge(*after(f"probs turned {g} {n}"))
                    if g and n == 0:
                        act.wait_ge(*after(f"attn out {g - 1}"))
                    copy(probs_T[:, 4 * n:4 * n + 4, :], bank[4 + n][:, :].rearrange("p (b n) -> p b n", b=4))\
                        .then_inc(*S(f"probs_T {g} {n}"))
                hi_to(min(first["g1"] + 3 + 3 * g + 3, G_PL + 3))
            gate("a0", gate_a, 0)
            hi_to(G_PL + 2)
            gate("a1", gate_a, 512)
            act.wait_ge(*after("lru y 7"))
            act.wait_ge(slab_used, G_PL)
            for b in range(4):
                copy(xhi[:, 2 * b:2 * b + 2, :], lru_h[:, 2 * b:2 * b + 2, :]).then_inc(*S(f"lru hi {b}"))
            hi_to(G_PA + 2)
            turn_scalar(act, "uc")
            hi_to(G_OUT2 + 2)
            turn_scalar(act, "ud")
            hi_to(G_FF2 + 2)
            post_scalar(act, "mx", acc_ready("mix out", G_FF2 - 1))
            hi_to(G_FF2 + 3)
            pre_scalar(act, "p3", "mx")
            turn_scalar(act, "ue")
            ff_scalar(act, G_FF2, 1, False)
            post_scalar(act, "f2", acc_ready("f2 out", G_FF2 + 3 * FF_STEPS - 1))

        def two_vector(dve):
            TTn, TS, STT = nc.vector.tensor_tensor, nc.vector.tensor_scalar, nc.vector.scalar_tensor_tensor
            made = [G_IN + 3]

            def lo_to(n):
                while made[0] < n:
                    make_lo(dve, lo_dve, made[0])
                    made[0] += 1

            for g in range(RING):
                make_lo(dve, lo_dve, g)
            pre_vector(dve, "p1", 0)
            turn_vector(dve, "ua")
            ff_vector(dve, 0, 0, True)
            post_vector(dve, "f1", 0.5, RMS_EPS, 0)
            pre_vector(dve, "p2", 1)
            turn_vector(dve, "ub")
            dve.wait_ge(*after("channel rows in place"))
            TS(half_b, pc[:, 40:56], 0.5, None, ALU.mult).then_inc(*V("half biases"))
            TS(lam_t[:, 8:16], pc[:, 56:64], -1.0, 0.0, ALU.mult, ALU.max).then_inc(*V("lam relu"))
            dve.wait_ge(*after("lam relu"))
            dve.wait_ge(*after("lam ln"))
            TTn(lru_c, lam_t[:, 0:8], lam_t[:, 8:16], ALU.add).then_inc(*V("lam softplus"))
            dve.wait_ge(*after("lam softplus"))
            TS(lru_c, lru_c, -LRU_C / 2, None, ALU.mult).then_inc(*V("lru c"))
            dve.wait_ge(*after("lru pads"))
            for n, c in enumerate(("x0", "x1")):
                lo_to(first[c] + 4)
                for b in range(2):
                    dve.wait_ge(*after(f"evacuated {c} {b}"))
                    for k in range(CONV):
                        for x in (4 * n + 2 * b, 4 * n + 2 * b + 1):
                            tap, src = pc[:, 8 * k + x:8 * k + x + 1], lru_in[:, x, k:k + SEQ]
                            if k == 0:
                                i = TS(lru_x[:, x, :], src, tap, pc[:, 32 + x:33 + x], ALU.mult, ALU.add)
                            else:
                                dve.wait_ge(*after(f"lru conv {x} {k - 1}"))
                                i = STT(lru_x[:, x, :], src, tap, lru_x[:, x, :], ALU.mult, ALU.add)
                            i.then_inc(*V(f"lru conv {x} {k}"))

            def rotate(src, heads, out1, out2, cos, sin, name, t, k):
                hf = HD // 2
                c = cos.unsqueeze(1).to_broadcast([P, heads, hf])
                s = sin.unsqueeze(1).to_broadcast([P, heads, hf])
                a, b = rot_t[:, 2 * k, 0:heads, :], rot_t[:, 2 * k + 1, 0:heads, :]
                TTn(out1, src[:, :, 0:hf], c, ALU.mult).then_inc(*V(f"{name} a {t}"))
                TTn(a, src[:, :, hf:HD], s, ALU.mult).then_inc(*V(f"{name} b {t}"))
                TTn(out2, src[:, :, hf:HD], c, ALU.mult).then_inc(*V(f"{name} c {t}"))
                TTn(b, src[:, :, 0:hf], s, ALU.mult).then_inc(*V(f"{name} d {t}"))
                dve.wait_ge(*after(f"{name} b {t}"))
                TTn(out1, out1, a, ALU.subtract).then_inc(*V(f"{name} e {t}"))
                dve.wait_ge(*after(f"{name} d {t}"))
                TTn(out2, out2, b, ALU.add).then_inc(*V(f"rotated {name} {t}"))

            hf = HD // 2
            cs = [tab[:, c:c + TT * hf].rearrange("p (t n) -> p t n", t=TT) for c in (C_COS, C_SIN)]
            for n, c in enumerate(("q0", "q1")):
                lo_to(first[c] + 4)
                dve.wait_ge(*ready[c])
                for t in range(TT):
                    o = q_rot[:, t, 8 * n:8 * n + 8, :]
                    if n or t:
                        dve.wait_ge(*after("rotated q0 0" if n == 0 else f"rotated {('q0 1', 'q1 0')[t]}"))
                    rotate(pair[c][t][:, :].rearrange("p (h n) -> p h n", n=HD), 8, o[:, :, 0:hf], o[:, :, hf:HD],
                           cs[0][:, t, :], cs[1][:, t, :], c, t, t)
            lo_to(first["kv"] + 4)
            for t in range(TT):
                dve.wait_ge(*after(f"v copied {t}"))
                dve.wait_ge(*after("rotated q1 1" if t == 0 else "rotated kv 0"))
                o = k_rot[:, t, :, 0, :]
                rotate(pair["kv"][t][:, 0:KVW].rearrange("p (h n) -> p h n", n=HD), KVH, o[:, :, 0:hf], o[:, :, hf:HD],
                       cs[0][:, t, :], cs[1][:, t, :], "kv", t, t)
            dve.wait_ge(*after("rotated kv 1"))
            nc.vector.tensor_copy(k_rot[:, 0, :, 1, :], k_rot[:, 0, :, 0, :]).then_inc(*V("v in place 1"))
            nc.vector.tensor_copy(k_rot[:, 1, :, 1, :], k_rot[:, 1, :, 0, :]).then_inc(*V("k doubled"))
            lo_to(first["g0"] + 3)
            dve.wait_ge(*after("lru a 7"))
            for b in range(2):
                c = slice(4 * b, 4 * b + 4)
                TTn(lru_h[:, c, :], lru_a[:, c, :], lru_a[:, c, :], ALU.mult).then_inc(*V(f"a squared {b}"))
                STT(lru_i[:, c, :], lru_i[:, c, :], 1.0, lru_x[:, c, :], ALU.add, ALU.mult).then_inc(*V(f"i x {b}"))
                dve.wait_ge(*after(f"a squared {b}"))
                STT(lru_m[:, c, :], lru_h[:, c, :], 1.0, lru_m[:, c, :], ALU.add, ALU.mult).then_inc(*V(f"expm1 {b}"))
                dve.wait_ge(*after(f"expm1 {b}"))
                TS(lru_m[:, c, :], lru_m[:, c, :], -1.0, 0.0, ALU.mult, ALU.max).then_inc(*V("lru mult squared" if b else "lru ms 0"))
            lo_to(first["g0"] + 5)
            dve.wait_ge(*after("lru mult"))
            for c in range(LT):
                STT(lru_i[:, c, :], lru_i[:, c, :], 0.5, lru_m[:, c, :], ALU.mult, ALU.mult).then_inc(*V(f"lru b {c}"))
            for c in range(LT):
                dve.wait_ge(*after(f"lru b {c}"))
                nc.vector.tensor_tensor_scan(lru_h[:, c, :], lru_a[:, c, :], lru_i[:, c, :], 0.0, ALU.mult, ALU.add)\
                    .then_inc(*V(f"lru scanned {c}"))

            def gated_y(c, k):
                for b in range(2):
                    dve.wait_ge(*after(f"gelu {c} {b}"))
                    for x in range(2):
                        j = k + 2 * b + x
                        if x == 0:
                            dve.wait_ge(*after(f"lru scanned {j + 1}"))
                        TTn(lru_h[:, j, :], lru_h[:, j, :], gelu_g[:, b, x, :], ALU.mult).then_inc(*V(f"lru y {j}"))

            def window(g):
                k = 8 * (g % 2)
                mx, nm = small[:, 192 + k:200 + k], small[:, 208 + k:216 + k]
                sm_, sk = small[:, 224 + k:232 + k], small[:, 240 + k:248 + k]
                rec = small[:, 256 + k:264 + k]
                scale = HD ** -0.5
                dve.wait_ge(*after(f"scores {g}"))
                if g == 0:
                    dve.wait_ge(*after("lru scanned 7"))
                for b in range(2):
                    STT(scores[0][:, g % 2, b::2, :], bank[4 + 2 * b][:, 0:256].rearrange("p (h n) -> p h n", h=2), scale,
                        tab[:, C_NC + P:C_NC + 2 * P].unsqueeze(1).to_broadcast([P, 2, P]), ALU.mult, ALU.add)\
                        .then_inc(*V(f"masked {g} 0 {b}"))
                dve.wait_ge(*after(f"masked {g} 0 1"))
                nc.vector.tensor_reduce(mx[:, 0:4], scores[0][:, g % 2], AX.X, ALU.max).then_inc(*V(f"max {g} 0"))
                for b in range(2):
                    STT(scores[1][:, g % 2, b::2, :], bank[5 + 2 * b][:, :].rearrange("p (h n) -> p h n", h=2), scale,
                        tab[:, C_NW:C_NW + 2 * P].unsqueeze(1).to_broadcast([P, 2, 2 * P]), ALU.mult, ALU.add)\
                        .then_inc(*V(f"masked {g} 1 {b}"))
                dve.wait_ge(*after(f"masked {g} 1 1"))
                nc.vector.tensor_reduce(mx[:, 4:8], scores[1][:, g % 2], AX.X, ALU.max).then_inc(*V(f"max {g} 1"))
                sink = sinks[:, 4 * g:4 * g + 4]
                for t in range(TT):
                    u = slice(4 * t, 4 * t + 4)
                    dve.wait_ge(*after(f"max {g} {t}"))
                    TTn(mx[:, u], mx[:, u], sink, ALU.max).then_inc(*V(f"max with sink {g} {t}"))
                    dve.wait_ge(*after(f"max with sink {g} {t}"))
                    TS(nm[:, u], mx[:, u], -1.0, None, ALU.mult).then_inc(*V(f"minus max {g} {t}"))
                    TTn(sk[:, u], sink, mx[:, u], ALU.subtract).then_inc(*V(f"sink less max {g}" if t else f"sink less max {g} 0"))
                return sm_, sk, rec

            def window_end(g, sm_, sk, rec):
                dve.wait_ge(*after(f"sink exp {g}"))
                TTn(sm_, sm_, sk, ALU.add).then_inc(*V(f"den {g}"))
                dve.wait_ge(*after(f"den {g}"))
                nc.vector.reciprocal(rec, sm_).then_inc(*V(f"rec {g}"))
                dve.wait_ge(*after(f"rec {g}"))
                dve.wait_ge(*after(f"attn out {g}"))
                for t in range(TT):
                    TTn(y_attn[:, t, 256 * g:256 * g + 256].rearrange("p (h n) -> p h n", h=4),
                        bank[7][:, 256 * t:256 * t + 256].rearrange("p (h n) -> p h n", h=4),
                        rec[:, 4 * t:4 * t + 4].unsqueeze(2).to_broadcast([P, 4, HD]), ALU.mult)\
                        .then_inc(*V(f"attn {g} {t}"))

            for g in range(KVH):
                w = window(g)
                if g == 0:
                    gated_y("g0", 0)
                lo_to(min(first["g1"] + 3 + 3 * g + 1, G_PL + 3))
                if g == 0:
                    gated_y("g1", 4)
                lo_to(min(first["g1"] + 3 + 3 * g + 2, G_PL + 3))
                window_end(g, *w)
                lo_to(min(first["g1"] + 3 + 3 * g + 3, G_PL + 3))
            lo_to(G_PL + 2)
            for b in range(4):
                dve.wait_ge(*after(f"lru hi {b}"))
                TTn(xlo[:, 2 * b:2 * b + 2, :], lru_h[:, 2 * b:2 * b + 2, :], xhi[:, 2 * b:2 * b + 2, :].bitcast(F32),
                    ALU.subtract).then_inc(*V("lru lo" if b == 3 else f"lru lo {b}"))
            lo_to(G_PA + 2)
            turn_order = acc_ready("lru out", G_PA - 1)
            for n in range(4):
                t, c = n // 2, slice(512 * (n % 2), 512 * (n % 2) + 512)
                dve.wait_ge(*turn_order(t))
                STT(merged[:, t, c], gate_l[:, t, c], 1.0, acc[t][n % 2][:, :], ALU.add, ALU.mult).then_inc(*V(f"merged lru {n}"))
            turn_vector(dve, "uc")
            lo_to(G_OUT2 + 2)
            for n in range(4):
                t, c = n // 2, slice(512 * (n % 2), 512 * (n % 2) + 512)
                dve.wait_ge(*acc_ready("attn proj out", G_OUT2 - 1)(t))
                STT(gate_a[:, t, c], gate_a[:, t, c], 1.0, acc[t][n % 2][:, :], ALU.add, ALU.mult).then_inc(*V(f"gated attn {n}"))
                dve.wait_ge(*after(f"gated attn {n}"))
                TTn(merged[:, t, c], merged[:, t, c], gate_a[:, t, c], ALU.add).then_inc(*V(f"merged {n}"))
            turn_vector(dve, "ud")
            lo_to(G_FF2 + 3)
            post_vector(dve, "mx", 1.0, 4 * RMS_EPS, 1)
            pre_vector(dve, "p3", 2)
            turn_vector(dve, "ue")
            ff_vector(dve, G_FF2, 1, False)
            post_vector(dve, "f2", 0.5, RMS_EPS, 2)

        def two_gpsimd(pool):
            for g in range(RING):
                make_lo(pool, lo_pool, g)
            nc.gpsimd.memset(lru_w[:, :, :, :], 0.0).then_inc(*G("lru zeros"))
            nc.gpsimd.memset(lru_in[:, :, 0:3], 0.0).then_inc(*G("lru pads"))
            ff_gpsimd(pool, 0, True)
            for g in range(G_IN + 3, G_FF2 + 3):
                make_lo(pool, lo_pool, g)
            ff_gpsimd(pool, G_FF2, False)

        with nc.Block() as block:
            st.start("two")

            @block.sync
            def _(sp):
                two_load(sp)

            @block.tensor
            def _(pe):
                two_tensor(pe)

            @block.scalar
            def _(act):
                two_scalar(act)

            @block.vector
            def _(dve):
                two_vector(dve)

            @block.gpsimd
            def _(pool):
                two_gpsimd(pool)
        return st.found


_INS = ["x", "p", "positions", "ffa_w_in", "ffa_w_out", "mix_w_in", "gdn_conv_w", "gdn_a_log", "gdn_dt_bias",
        "gdn_norm_w", "mla_q_norm_w", "mla_kv_norm_w", "mla_w_uq", "mla_w_ukv", "mix_w_o", "ffb_w_in", "ffb_w_out",
        "ln_g", "ln_b", "ple_w_gate", "ple_w_proj", "ffn1_pre_g_2", "ffn1_w_gu_2", "ffn1_w_down_2", "ffn1_post_g_2",
        "mix_pre_g_2", "w_in_2", "conv_w_2", "conv_b_2", "lru_w_a_2", "lru_b_a_2", "lru_w_x_2", "lru_b_x_2",
        "lru_lambda_2", "attn_sinks_2", "w_proj_lru_2", "w_proj_attn_2", "w_out_2", "mix_post_g_2",
        "ffn2_pre_g_2", "ffn2_w_gu_2", "ffn2_w_down_2", "ffn2_post_g_2"]


def program(nc, shapes, known):
    A = {n: nc.dram_tensor(f"in_{n}", shape, dtype, kind="ExternalInput").ap() for n, (shape, dtype) in shapes.items()}
    out = nc.dram_tensor("out_0", (1, SEQ, D), F32, kind="ExternalOutput").ap()
    return build_program(nc, A, out, known)


def kernel(**inputs):
    import concourse.bacc as bacc
    from concourse.bass_utils import run_bass_kernel_spmd

    arrays = {n: np.ascontiguousarray(inputs[n]) for n in _INS}
    arrays["tables"] = shape_tables()
    shapes = {n: (a.shape, mybir.dt.from_np(a.dtype)) for n, a in arrays.items()}
    counted = program(bacc.Bacc("TRN2", target_bir_lowering=False, num_devices=1), shapes, {})
    nc = bacc.Bacc("TRN2", target_bir_lowering=False, num_devices=1)
    program(nc, shapes, counted)
    r = run_bass_kernel_spmd(nc, [{f"in_{n}": a for n, a in arrays.items()}], core_ids=[0])
    return r.results[0]["out_0"]
```

```python
import math
from contextlib import ExitStack

import numpy as np

import concourse.bass as bass
from concourse import mybir

ALU = mybir.AluOpType
ACT = mybir.ActivationFunctionType
AX = mybir.AxisListType
F32 = mybir.dt.float32
F32R = mybir.dt.float32r
I32 = mybir.dt.int32

P = 128
SEQ = 256
TT = SEQ // P
D = 1024
KT = D // P
DEPTH = 2
D_FF = 2816
FFC = 256
FF_STEPS = D_FF // FFC
PLE = 256
ALPHA = (2 * DEPTH) ** 0.25
LN_EPS = 1e-5
RMS_EPS = 1e-6
ROPE_BASE = 10000.0

GH, GD = 8, 64
GW = GH * GD
CONV = 4
SBH, SBD = 4, 64
SBW = SBH * SBD
MH, MN, MR, MV = 4, 64, 32, 64
MQ, MKV = 256, 128
MD = MN + MR
IN1 = 4 * GW + 2 * GH + 3 * SBW + MQ + MKV + MR
C_Z = 3 * GW
C_G = 4 * GW
C_SQ = C_G + 2 * GH
C_SV = C_SQ + 2 * SBW
C_MQ = C_SV + SBW
MLW = MQ + MKV + MR
DW = 2 * GH + MLW

LRU = 1024
LT = LRU // P
LRU_C = 8.0
QH, KVH, HD = 16, 4, 64
QW, KVW = QH * HD, KVH * HD
IN2 = 2 * LRU + QW + 2 * KVW + 2 * D

SLAB = 2048
RING = 3
NEG = -1e30

SMALL = [1, 2, 4, 8, 16]
LEVELS = [32, 64]
C_ID, C_UI, C_SL, C_LI, C_ONE = 0, 128, 256, 384, 512
C_LV = 640
C_BD = C_LV + 128 * len(LEVELS)
C_CI = C_BD + 128
C_CM = C_CI + 32
C_NS = C_CM + 32 * len(SMALL)
C_NC = C_NS + 256
C_NW = C_NC + 256
C_INV = C_NW + 256
C_COS = C_INV + MR // 2
C_SIN = C_COS + TT * (HD // 2)
C_TOT = C_SIN + TT * (HD // 2)


def shape_tables():
    t = np.zeros((P, C_TOT), np.float32)
    a, b = np.arange(P)[:, None], np.arange(P)[None, :]
    t[:, C_ID:C_ID + P] = a == b
    t[:, C_UI:C_UI + P] = a <= b
    t[:, C_SL:C_SL + P] = a > b
    t[:, C_LI:C_LI + P] = a >= b
    t[:, C_ONE:C_ONE + P] = 1
    for n, w in enumerate(LEVELS):
        same = a // (2 * w) == b // (2 * w)
        t[:, C_LV + n * P:C_LV + (n + 1) * P] = same & (a // w % 2 == 0) & (b // w % 2 == 1)
    t[:, C_BD:C_BD + P] = a // 32 == b // 32
    r, c = a % 32, np.arange(32)[None, :]
    t[:, C_CI:C_CI + 32] = r == c
    for n, w in enumerate(SMALL):
        row, col = (r, c) if n else (c, r)
        t[:, C_CM + 32 * n:C_CM + 32 * n + 32] = (row // w % 2 == 1) & (col // w == row // w - 1)
    t[:, C_NS:C_NS + P] = np.where(a < b, 0, NEG)
    t[:, C_NC + P:C_NC + 2 * P] = np.where(b <= a, 0, NEG)
    t[:, C_NW:C_NW + P] = np.where(b > a, 0, NEG)
    t[:, C_NW + P:C_NW + 2 * P] = np.where(b <= a, 0, NEG)
    t[:, C_INV:C_INV + MR // 2] = np.float32(1) / np.float32(ROPE_BASE) ** (
        np.arange(0, MR, 2, dtype=np.float32) / np.float32(MR))
    half = HD // 2
    inv = np.float32(ROPE_BASE) ** (-np.arange(half, dtype=np.float32) / np.float32(half))
    ang = np.arange(SEQ, dtype=np.float32)[:, None] * inv[None, :]
    for n, f in ((C_COS, np.cos), (C_SIN, np.sin)):
        t[:, n:n + TT * half] = f(ang).astype(np.float32).reshape(TT, P, half).transpose(1, 0, 2).reshape(P, -1)
    return t


class Steps:

    def __init__(self, known):
        self.known, self.found, self.sems, self.count, self.part = known, {}, {}, {}, ""

    def start(self, part):
        self.part = part
        self.count = dict.fromkeys(self.sems, 0)

    def mark(self, who, name):
        self.count[who] += 1
        assert (self.part, name) not in self.found, name
        self.found[self.part, name] = (who, self.count[who])
        return self.sems[who], 1

    def after(self, name):
        who, value = self.known.get((self.part, name), (None, 1))
        if who is None:
            assert not self.known, (self.part, name)
            who = next(iter(self.sems))
        return self.sems[who], value


def build_program(nc, A, out, known):
    ctx = ExitStack()
    with ctx:
        def sb(name, shape, dt=F32):
            return ctx.enter_context(nc.sbuf_tensor(name, shape, dt))

        def sem(name):
            return ctx.enter_context(nc.semaphore(name))

        raw = sb("raw", [P, RING, SLAB])
        whi = sb("whi", [P, RING, SLAB], F32R)
        wlo = sb("wlo", [P, RING, SLAB], F32R)
        h = sb("h", [P, TT, D])
        xhi = sb("xhi", [P, KT, SEQ], F32R)
        xlo = sb("xlo", [P, KT, SEQ], F32R)
        gated = sb("gated", [P, 2, TT, FFC])
        ahi = sb("ahi", [P, 2, SEQ], F32R)
        alo = sb("alo", [P, 2, SEQ], F32R)
        normw = sb("normw", [P, 2, D])
        tab = sb("tab", [P, C_TOT])
        pv = sb("pv", [P, 512])
        small = sb("small", [P, 512])
        arena = sb("arena", [P, 20992])
        bank = [ctx.enter_context(nc.psum_tensor(f"bank{n}", [P, 512], F32)) for n in range(8)]
        acc = [[bank[2 * t + n] for n in range(2)] for t in range(TT)]

        ident = tab[:, C_ID:C_ID + P]

        silu_gate = gated[:, 0, :, :].rearrange("p a b -> p (a b)")
        gated_up = gated[:, 1, :, :].rearrange("p a b -> p (a b)")

        def flat(x):
            return x[:, :, :].rearrange("p a b -> p (a b)")

        def tokens(t):
            return slice(P * t, P * t + P)

        rope1 = sb("rope1", [P, 2, TT, MR // 2])

        arrived = [sem(f"slab_arrived{n}") for n in range(RING)]
        hi_made = sem("slab_hi_made")
        lo_dve = sem("slab_lo_made_by_vector")
        lo_pool = sem("slab_lo_made_by_gpsimd")
        slab_used = sem("slab_used")
        ff_first = sem("gate_up_products_of_first_tile")
        ff_silu = sem("silu_of_gate")
        ff_gated = sem("gated_ready")
        ff_hi = sem("gated_hi")
        ff_lo = sem("gated_lo")
        st = Steps(known)
        st.sems = {w: sem(f"steps_of_{w}") for w in ("tensor", "vector", "scalar", "gpsimd")}
        params = [sem(f"parameters{n}") for n in range(8)]
        stored = sem("stored")
        every = arrived + [hi_made, lo_dve, lo_pool, slab_used, ff_first, ff_silu, ff_gated,
                           ff_hi, ff_lo, *st.sems.values(), *params]
        after = st.after
        T, V, S, G = (lambda n, w=w: st.mark(w, n) for w in ("tensor", "vector", "scalar", "gpsimd"))

        DVE_PART = 1408

        def load_slab(sp, g, i, parts):
            if not (isinstance(i, int) and g + 3 * i < RING):
                sp.wait_ge(lo_dve, g + 3 * i - RING + 1)
                sp.wait_ge(lo_pool, g + 3 * i - RING + 1)
            for n, (view, src) in enumerate(parts):
                nc.sync.dma_start(view(raw[:, g % RING, :]), src).then_inc(arrived[g % RING], 16)

        def make_hi(act, g, i=0):
            act.wait_ge(arrived[g % RING], 32 * (g // RING + 1 + i))
            if not (isinstance(i, int) and g < RING):
                act.wait_ge(slab_used, g + 3 * i - RING + 1)
            nc.scalar.activation(whi[:, g % RING, :], raw[:, g % RING, :], ACT.Copy).then_inc(hi_made, 1)

        def make_lo(eng, which, g, i=0):
            part = slice(0, DVE_PART) if which is lo_dve else slice(DVE_PART, SLAB)
            eng.wait_ge(hi_made, g + 3 * i + 1)
            eng.tensor_tensor(wlo[:, g % RING, part], raw[:, g % RING, part],
                              whi[:, g % RING, part].bitcast(F32), ALU.subtract).then_inc(which, 1)

        def await_slab(pe, g, i=0):
            pe.wait_ge(hi_made, g + 3 * i + 1)
            pe.wait_ge(lo_dve, g + 3 * i + 1)
            pe.wait_ge(lo_pool, g + 3 * i + 1)

        def product(o, left, right, first, last, skip=False):
            (lh, ll), (rh, rl) = left, right
            nc.tensor.matmul(o, lh, rh, start=first, stop=False, skip_group_check=skip)
            nc.tensor.matmul(o, ll, rh, start=False, stop=False, skip_group_check=skip)
            return nc.tensor.matmul(o, lh, rl, start=False, stop=last, skip_group_check=skip)

        def slab(g, k, w):
            return tuple(x[:, g % RING, :k * w].rearrange("p (k n) -> p k n", k=k) for x in (whi, wlo))

        def wide_slab(g, left, k0, first, last, done=None):
            wh, wl = slab(g, 2, D)
            lh, ll = left
            for t in range(TT):
                for k in range(2):
                    for n in range(2):
                        c = slice(512 * n, 512 * n + 512)
                        u = tokens(t)
                        m = product(acc[t][n][:, :], (lh[:, k0 + k, u], ll[:, k0 + k, u]),
                                    (wh[:, k, c], wl[:, k, c]), first and k == 0, last and k == 1)
                if last and t == 0:
                    m.then_inc(*T(done))
            return m

        def token_slab(g, k0, nk, w, outs, tiles=range(TT)):
            wh, wl = slab(g, nk, w)
            for t in tiles:
                for k in range(nk):
                    u = tokens(t)
                    m = product(outs[t], (xhi[:, k0 + k, u], xlo[:, k0 + k, u]), (wh[:, k, :], wl[:, k, :]),
                                k0 + k == 0, k0 + k == KT - 1)
            return m

        def channel_slab(g, k0, outs, tiles=range(4)):
            wh, wl = slab(g, 4, 512)
            for c in tiles:
                for k in range(4):
                    u = slice(P * c, P * c + P)
                    m = product(outs[c // 2][:, 256 * (c % 2):256 * (c % 2) + 256],
                                (wh[:, k, u], wl[:, k, u]), (xhi[:, k0 + k, :], xlo[:, k0 + k, :]),
                                k0 + k == 0 and c % 2 == 0, k0 + k == KT - 1, skip=True)
            return m

        def in_parts(W, r0, half, j):
            def view(which):
                return lambda x: x.rearrange("p (k b n) -> p k b n", k=4, b=2)[:, :, which, :]
            return [(view(b), W[bass.ds(r0 + 512 * half, 512), bass.ds(b * D_FF + FFC * j, FFC)]
                     .rearrange("(k p) n -> p k n", p=P)) for b in range(2)]

        def wide_parts(W, r):
            return [((lambda x, k=k: x[:, D * k:D * k + D]), W[bass.ds(r + P * k, P), :]) for k in range(2)]

        def col_parts(W, r0, k0, nk, pieces):
            w = sum(n for _, n in pieces)
            if len(pieces) == 1:
                c = pieces[0][0]
                m = nk // 2
                return [((lambda x, b=b: x[:, :nk * w].rearrange("p (k n) -> p k n", k=nk)[:, b * m:b * m + m, :]),
                         W[bass.ds(r0 + P * (k0 + b * m), P * m), c:c + w].rearrange("(k p) n -> p k n", p=P))
                        for b in range(2)]
            out, at = [], 0
            for c, n in pieces:
                out.append(((lambda x, at=at, n=n: x[:, :nk * w].rearrange("p (k n) -> p k n", k=nk)[:, :, at:at + n]),
                            W[bass.ds(r0 + P * k0, P * nk), c:c + n].rearrange("(k p) n -> p k n", p=P)))
                at += n
            return out

        def ff_load(sp, g0, W1, r1, W2, r2, others=None):
            def step(g, i, j):
                load_slab(sp, g, i, in_parts(W1, r1, 0, j))
                load_slab(sp, g + 1, i, in_parts(W1, r1, 1, j))

            def step_and_out(i):
                step(g0 + 2, i, i + 1)
                load_slab(sp, g0 + 4, i, wide_parts(W2, r2 + FFC * i))

            step(g0, 0, 0)
            if others:
                others()
            step_and_out(0)
            with sp.Fori(1, FF_STEPS - 1) as i:
                step_and_out(i)
            load_slab(sp, g0 + 32, 0, wide_parts(W2, r2 + FFC * (FF_STEPS - 1)))

        gate_up_banks = (bank[4], bank[5])
        first_banks = (bank[6], bank[7])

        def ff_tensor(pe, g0, f, name, turn, before_last=None):
            j0 = FF_STEPS * f
            tname, tsource, tready = turn

            def gate_up(g, i, half, banks):
                wh, wl = slab(g, 4, 2 * FFC)
                await_slab(pe, g, i)
                for c in range(4):
                    b = banks[c // 2]
                    for k in range(4):
                        u, kk = slice(P * c, P * c + P), 4 * half + k
                        m = product(b[:, 256 * (c % 2):256 * (c % 2) + 256], (wh[:, k, u], wl[:, k, u]),
                                    (xhi[:, kk, :], xlo[:, kk, :]), kk == 0 and c % 2 == 0, kk == KT - 1, skip=True)
                    if half and c == 1:
                        m.then_inc(ff_first, 1)
                m.then_inc(slab_used, 1)

            def step_in(g, i, j, banks=gate_up_banks):
                if not (isinstance(j, int) and j <= j0 + 1):
                    pe.wait_ge(ff_gated, j)
                gate_up(g, i, 0, banks)
                gate_up(g + 1, i, 1, banks)

            def step_out(g, i, j, first, last):
                await_slab(pe, g, i)
                pe.wait_ge(ff_lo, j + 1)
                wide_slab(g, (xhi, xlo) if last else (ahi, alo), 0, first, last, name).then_inc(slab_used, 1)

            turn_tensor(pe, tname, tsource, tready)
            pe.wait_ge(*after(f"{tname} lo 3"))
            step_in(g0, 0, j0, first_banks)
            step_in(g0 + 2, 0, j0 + 1)
            step_out(g0 + 4, 0, j0, True, False)
            with pe.Fori(1, FF_STEPS - 1) as i:
                step_in(g0 + 2, i, j0 + 1 + i)
                step_out(g0 + 4, i, j0 + i, False, False)
            if before_last:
                before_last()
            step_out(g0 + 32, 0, j0 + FF_STEPS - 1, False, True)

        def ff_scalar(act, g0, f, more):
            j0 = FF_STEPS * f

            def silu(j, banks=gate_up_banks):
                act.wait_ge(ff_first, j + 1)
                if not (isinstance(j, int) and j == 0):
                    act.wait_ge(ff_gated, j)
                nc.scalar.activation(silu_gate, banks[0][:, :], ACT.Silu).then_inc(ff_silu, 1)

            def hi(j, to=ahi):
                act.wait_ge(ff_gated, j + 1)
                nc.scalar.activation(flat(to), gated_up, ACT.Copy).then_inc(ff_hi, 1)

            def step(i, slabs, last=False):
                make_hi(act, g0 + 5, i)
                silu(j0 + 1 + i)
                if slabs > 1:
                    make_hi(act, g0 + 6, i)
                if last:
                    hi(j0 + 1 + i, xhi[:, 0:2, :])
                else:
                    act.wait_ge(slab_used, g0 + 3 * i + 5)
                    hi(j0 + 1 + i)
                if slabs > 1:
                    make_hi(act, g0 + 7, i)

            make_hi(act, g0 + 3)
            silu(j0, first_banks)
            make_hi(act, g0 + 4)
            hi(j0)
            with act.Fori(0, FF_STEPS - 2) as i:
                step(i, 3)
            step(FF_STEPS - 2, 3 if more else 1, True)

        def ff_vector(dve, g0, f, more):
            j0 = FF_STEPS * f

            def gate(j, g, i, banks=gate_up_banks):
                dve.wait_ge(ff_silu, j + 1)
                dve.wait_ge(slab_used, g + 3 * i + 1)
                if not (isinstance(j, int) and j == 0):
                    dve.wait_ge(ff_lo, j)
                nc.vector.tensor_tensor(gated_up, silu_gate, banks[1][:, :], ALU.mult).then_inc(ff_gated, 1)

            def lo(j, to=alo, of=ahi):
                dve.wait_ge(ff_hi, j + 1)
                nc.vector.tensor_tensor(flat(to), gated_up, flat(of).bitcast(F32), ALU.subtract).then_inc(ff_lo, 1)

            def step(i, slabs, last=False):
                make_lo(dve, lo_dve, g0 + 5, i)
                gate(j0 + 1 + i, g0 + 3, i)
                if slabs > 1:
                    make_lo(dve, lo_dve, g0 + 6, i)
                if last:
                    lo(j0 + 1 + i, xlo[:, 0:2, :], xhi[:, 0:2, :])
                else:
                    dve.wait_ge(slab_used, g0 + 3 * i + 5)
                    lo(j0 + 1 + i)
                if slabs > 1:
                    make_lo(dve, lo_dve, g0 + 7, i)

            make_lo(dve, lo_dve, g0 + 3)
            gate(j0, g0 + 1, 0, first_banks)
            make_lo(dve, lo_dve, g0 + 4)
            lo(j0)
            with dve.Fori(0, FF_STEPS - 2) as i:
                step(i, 3)
            step(FF_STEPS - 2, 3 if more else 1, True)

        def ff_gpsimd(pool, g0, more):
            with pool.Fori(0, FF_STEPS - (0 if more else 1)) as i:
                for n in range(3):
                    make_lo(pool, lo_pool, g0 + 3 + n, i)

        def rsqrt(dve, name, y, v, eps, scale=1.0, between=()):
            n = v.shape[-1]
            x, yy, z = y[:, 1, 0:n], y[:, 0, 0:n], y[:, 2, 0:n]
            k = [0]
            others = list(between)

            def link(ins):
                k[0] += 1
                ins.then_inc(*V(f"{name} {k[0]}"))
                if others:
                    others.pop(0)()
                dve.wait_ge(*after(f"{name} {k[0]}"))

            link(nc.vector.tensor_scalar(x, v, scale, eps, ALU.mult, ALU.add))
            link(nc.vector.tensor_scalar(z.bitcast(I32), x.bitcast(I32), 1, None, ALU.logical_shift_right))
            link(nc.vector.tensor_scalar(yy.bitcast(I32), z.bitcast(I32), -1.0, float(0x5F3759DF), ALU.mult, ALU.add))
            for step in range(3):
                link(nc.vector.scalar_tensor_tensor(z, x, -0.5, yy, ALU.mult, ALU.mult))
                link(nc.vector.tensor_tensor(z, z, yy, ALU.mult))
                ins = nc.vector.scalar_tensor_tensor(yy, z, 1.5, yy, ALU.add, ALU.mult)
                if step < 2:
                    link(ins)
            ins.then_inc(*V(name))

        def norm_vector(dve, name, c, ready, nth, turn):
            stats = small[:, 0:24].rearrange("p (t n s) -> p t n s", t=2, n=2)
            mv = small[:, 24:28].rearrange("p (t s) -> p t s", t=2)
            rs = small[:, 28:34].rearrange("p (s n) -> p s n", s=3)
            half = [slice(512 * n, 512 * n + 512) for n in range(2)]
            for t in range(TT):
                dve.wait_ge(*ready(t))
                for n in range(2):
                    nc.vector.scalar_tensor_tensor(h[:, t, half[n]], acc[t][n][:, :], c, h[:, t, half[n]],
                                                   ALU.mult, ALU.add).then_inc(*V(f"{name} sum {t}{n}"))
                for n in range(2):
                    dve.wait_ge(*after(f"{name} sum {t}{n}"))
                    nc.vector.bn_stats(stats[:, t, n, :], h[:, t, half[n]]).then_inc(*V(f"{name} stats {t}{n}"))
                dve.wait_ge(*after(f"{name} stats {t}1"))
                nc.vector.bn_aggr(mv[:, t, :], stats[:, t, :, :].rearrange("p n s -> p (n s)")).then_inc(*V(f"{name} mean {t}"))
            dve.wait_ge(*after(f"{name} mean 1"))
            dve.wait_ge(params[0], 32 * (nth + 1))

            def gained(t, n):
                return lambda: nc.vector.scalar_tensor_tensor(h[:, t, half[n]], h[:, t, half[n]], mv[:, t, 0:1], normw[:, 0, half[n]],
                                                   ALU.subtract, ALU.mult).then_inc(*V(f"{name} gained {t}{n}"))

            rsqrt(dve, f"{name} rstd", rs, mv[:, :, 1:2].rearrange("p t s -> p (t s)"), LN_EPS / ALPHA ** 2,
                  between=[gained(t, n) for t in range(TT) for n in range(2)])
            dve.wait_ge(*after(f"{name} rstd"))

            def done(t, n):
                nc.vector.scalar_tensor_tensor(h[:, t, half[n]], h[:, t, half[n]], rs[:, 0, t:t + 1], normw[:, 1, half[n]],
                                               ALU.mult, ALU.add).then_inc(*V(f"{name} done {t}{n}"))

            turn_behind(dve, done, turn)

        def turn_behind(dve, done, turn):
            done(0, 0)
            done(0, 1)
            done(1, 0)
            turn_rest(dve, turn, 0)
            done(1, 1)
            for n in range(1, 4):
                turn_rest(dve, turn, n)

        def load_norm(sp, nth, g, b, free):
            if free:
                sp.wait_ge(*after(free))
            nc.sync.dma_start(normw[:, 0, :], g.partition_broadcast(P)).then_inc(params[0], 16)
            nc.sync.dma_start(normw[:, 1, :], b.partition_broadcast(P)).then_inc(params[0], 16)

        def turn_tensor(pe, name, src, ready, free=None, tiles=range(TT)):
            if free:
                pe.wait_ge(*free)
            for t in tiles:
                for half in range(2):
                    if ready:
                        pe.wait_ge(*ready(t, half))
                    n = 2 * t + half
                    if n >= 2:
                        pe.wait_ge(*after(f"{name} lo {n - 2}"))
                    for q in range(4):
                        m = nc.tensor.transpose(bank[6 + half][:, P * q:P * q + P],
                                                src[:, t, P * (4 * half + q):P * (4 * half + q) + P], ident)
                    m.then_inc(*T(f"{name} turned {n}"))

        def turn_rounded(act, name, n, b):
            t, half = n // 2, n % 2
            act.wait_ge(*after(f"{name} turned {n}"))
            nc.scalar.activation(xhi[:, 4 * half:4 * half + 4, tokens(t)], b[:, :].rearrange("p (k n) -> p k n", k=4),
                                 ACT.Copy).then_inc(*S(f"{name} hi {n}"))

        def turn_scalar(act, name):
            for n in range(4):
                turn_rounded(act, name, n, bank[6 + n % 2])

        def turn_rest(dve, name, n, b=None):
            t, half = n // 2, n % 2
            b = b or bank[6 + half]
            dve.wait_ge(*after(f"{name} hi {n}"))
            nc.vector.tensor_tensor(xlo[:, 4 * half:4 * half + 4, tokens(t)],
                                    b[:, :].rearrange("p (k n) -> p k n", k=4),
                                    xhi[:, 4 * half:4 * half + 4, tokens(t)].bitcast(F32),
                                    ALU.subtract).then_inc(*V(f"{name} lo {n}"))

        def turn_vector(dve, name):
            for n in range(4):
                turn_rest(dve, name, n)

        def place(name, start, *shape):
            n = int(np.prod(shape))
            v = arena[:, start:start + n]
            if len(shape) == 2:
                v = v.rearrange("p (a b) -> p a b", a=shape[0])
            if len(shape) == 3:
                v = v.rearrange("p (a b c) -> p a b c", a=shape[0], b=shape[1])
            return v

        PR = TT * GH
        conv_in = place("conv_in", 0, 12, SEQ + 4)
        conv_out = place("conv_out", 3120, 12, SEQ)
        A_T = place("A_T", 0, PR, P)
        QK_T = place("QK_T", 2048, PR, P)
        B_T = place("B_T", 4096, 2, 4, P)
        Y_g = place("Y_g", 5120, 2, 4, P)
        T_inv = place("T_inv", 6192, PR, P)
        T_invT = place("T_invT", 8240, PR, P)
        A_Tb = place("A_Tb", 4096, PR, P)
        T_c, TT_c = place("T_c", 15408, PR, 32), place("TT_c", 15920, PR, 32)
        Y_c, D_c = place("Y_c", 16432, PR, 32), place("D_c", 16944, PR, 32)
        q_tok = place("q_tok", 6192, TT, GW)
        kb_tok = place("kb_tok", 7216, TT, GW)
        k_tok = place("k_tok", 10288, TT, GW)
        v_new = place("v_new", 10288, TT, GW)
        vb_tok = place("vb_tok", 11312, TT, GW)
        kT = place("kT", 12336, TT, 4, P)
        qkbT = arena[:, 13360:15408].rearrange("p (t r b n) -> p t r b n", t=TT, r=4, b=2)
        g_upto = place("g_upto", 15408, 2, 4, P)
        decay = place("decay", 16432, 2, 4, P)
        squares = place("squares", 15408, 4, GW)
        o_squares = place("o_squares", 2048, TT, GW)
        k_dec = place("k_dec", 17456, GW)
        state = place("state", 17968, 4, GD)
        silu_z = place("silu_z", 18224, TT, GW)
        sqT = place("sqT", 19248, 2, SEQ)
        skT = place("skT", 19760, 2, SEQ)
        s_val = place("s_val", 20272, TT, SBW)
        conv_rows = arena[0:4 * 12, 6192:6192 + P]
        latent = gated[:, :, :, :].rearrange("p a b c -> p (a b c)")[:, 0:TT * DW].rearrange("p (t n) -> p t n", t=TT)
        mixed = normw
        pv_conv = pv[:, 0:48]
        pv_alog, pv_dt = pv[:, 48:56], pv[:, 56:64]
        pv_gnorm = pv[:, 64:128]
        pv_qn = pv[:, 128:128 + MQ + MKV]

        def halves(x, w, which):
            return x.rearrange("p x (a b w) -> p x a b w", b=2, w=w)[:, :, :, which, :]

        def diagonal(x, c):
            return x[32 * c:32 * c + 32, :, 32 * c:32 * c + 32]

        def sm(start, n):
            return small[:, start:start + n]

        def small_loads(sp, l):
            one = lambda name, n: A[name][bass.ds(l, 1), :].partition_broadcast(P).rearrange("p a n -> p (a n)")
            nc.sync.dma_start(conv_rows, A["gdn_conv_w"].rearrange("l k (c p) -> (l k c) p", p=P)[bass.ds(l * 48, 48), :])\
              .then_inc(params[1], 16)
            nc.sync.dma_start(pv_alog, one("gdn_a_log", 8)).then_inc(params[2], 16)
            nc.sync.dma_start(pv_dt, one("gdn_dt_bias", 8)).then_inc(params[2], 16)
            nc.sync.dma_start(pv_gnorm, one("gdn_norm_w", 64)).then_inc(params[2], 16)
            nc.sync.dma_start(pv_qn[:, 0:MQ], one("mla_q_norm_w", MQ)).then_inc(params[2], 16)
            nc.sync.dma_start(pv_qn[:, MQ:MQ + MKV], one("mla_kv_norm_w", MKV)).then_inc(params[2], 16)

        def mixer_load(sp, g0, l):
            W = A["mix_w_in"].rearrange("l k n -> (l k) n")
            r = l * D
            g = g0
            for pieces in ([(0, GW)], [(GW, GW)], [(2 * GW, GW)], [(C_G, 2 * GH), (C_MQ, MLW)], [(C_Z, GW)], [(C_SQ, 2 * SBW)]):
                for half in range(2):
                    load_slab(sp, g, 0, col_parts(W, r, 4 * half, 4, pieces))
                    g += 1
            load_slab(sp, g, 0, col_parts(W, r, 0, 8, [(C_SV, SBW)]))
            wo = A["mix_w_o"].rearrange("l k n -> (l k) n")
            for n in range(4):
                load_slab(sp, g0 + 13 + n, 0, wide_parts(wo, l * D + 2 * P * n))

        def mixer_tensor(pe, g0):
            def used(m):
                m.then_inc(slab_used, 1)

            def chan(g, banks, free=None):
                for half in range(2):
                    if free and half == 0:
                        pe.wait_ge(*after(free))
                    await_slab(pe, g + half)
                    used(channel_slab(g + half, 4 * half, banks))

            def tok(g, nk, w, outs, free=None):
                for half in range(KT // nk):
                    if free and half == 0:
                        pe.wait_ge(*after(free))
                    await_slab(pe, g + half)
                    used(token_slab(g + half, nk * half, nk, w, outs))

            def to_tokens(grp, t, b):
                for c in range(4):
                    m = nc.tensor.transpose(b[:, P * c:P * c + P], conv_out[:, 4 * grp + c, tokens(t)], ident)
                return m

            pe.wait_ge(params[1], 16)
            nc.tensor.transpose(bank[5][:, 0:48], conv_rows, ident[0:48, 0:48]).then_inc(*T("taps"))
            chan(g0, bank[0:2])
            chan(g0 + 2, bank[2:4])
            chan(g0 + 4, bank[0:2], "evacuated 0 1")
            await_slab(pe, g0 + 6)
            pe.wait_ge(*after("evacuated 1 1"))
            used(token_slab(g0 + 6, 0, 4, DW, [bank[2][:, 0:DW], bank[3][:, 0:DW]]))
            for grp in range(2):
                pe.wait_ge(*after(f"conv silu {grp} 1"))
                for t in range(TT):
                    to_tokens(grp, t, bank[4 + 2 * grp + t]).then_inc(*T(f"qk tokens {grp} {t}"))
            await_slab(pe, g0 + 7)
            used(token_slab(g0 + 7, 4, 4, DW, [bank[2][:, 0:DW], bank[3][:, 0:DW]]))
            await_slab(pe, g0 + 8)
            pe.wait_ge(*after("evacuated 2 1"))
            z_banks = [bank[0][:, :], bank[1][:, :]]
            used(token_slab(g0 + 8, 0, 4, GW, z_banks))
            pe.wait_ge(*after("conv silu 2 1"))
            pe.wait_ge(*after("latent 1"))
            for t in range(TT):
                to_tokens(2, t, bank[2 + t]).then_inc(*T(f"v tokens {t}"))
            srcs = [("k", 0), ("q", 0), ("k", 1), ("q", 1), ("kb", 0), ("kb", 1)]
            for n, (what, t) in enumerate(srcs):
                if n == 4:
                    await_slab(pe, g0 + 9)
                    token_slab(g0 + 9, 4, 4, GW, z_banks, [0])
                src = {"k": k_tok, "q": q_tok, "kb": kb_tok}[what]
                pe.wait_ge(*after(f"{what} tok {t}"))
                if n == 0:
                    pe.wait_ge(*after("q tok 1"))
                    pe.wait_ge(*after("k tok 1"))
                if n >= 4:
                    pe.wait_ge(*after(f"turned in place {n - 4}"))
                for r in range(4):
                    m = nc.tensor.transpose(bank[4 + n % 4][:, P * r:P * r + P], src[:, t, P * r:P * r + P], ident)
                m.then_inc(*T(f"turned {n}"))
            pe.wait_ge(*after("g"))
            pe.wait_ge(*after("turned in place 2"))
            nc.tensor.matmul(bank[6][:, 0:16], tab[:, C_UI:C_UI + P], sm(304, 16), start=True, stop=True)
            nc.tensor.matmul(bank[6][:, 16:32], tab[:, C_SL:C_SL + P], sm(304, 16), start=True, stop=True)\
                .then_inc(*T("g sums"))
            for q in range(4):
                pe.wait_ge(*after(f"g upto {q}"))
                if q == 0:
                    pe.wait_ge(*after("turned in place 3"))
                if q == 1:
                    pe.wait_ge(*after("eg"))
                if q >= 2:
                    pe.wait_ge(*after(f"decay exp {q - 2}"))
                nc.tensor.matmul(bank[7 - q % 2][:, :], tab[:, C_SL:C_SL + P], g_upto[:, q % 2, :, :],
                                 start=True, stop=True).then_inc(*T(f"decay sums {q}"))
                pe.wait_ge(*after("turned in place 5"))
                if q >= 1:
                    pe.wait_ge(*after(f"A_T {q - 1} 1"))
                t = q // 2
                for b in range(2):
                    for x in range(2):
                        hh = 4 * (q % 2) + 2 * x + b
                        u = slice(64 * (hh % 2), 64 * (hh % 2) + 64)
                        m = nc.tensor.matmul(bank[4 + b][:, 256 * x:256 * x + 256], kT[u, t, hh // 2, :],
                                             qkbT[u, t, hh // 2, :, :], start=True, stop=True)
                    m.then_inc(*T(f"kk {q} {b}"))
            used(token_slab(g0 + 9, 4, 4, GW, z_banks, [1]))
            pe.wait_ge(*after("A_T 3 1"))
            pe.wait_ge(*after("decay exp 3"))
            pe.wait_ge(*after("A_Tb 3"))
            for n in range(1, len(SMALL)):
                for g in range(2):
                    pe.wait_ge(*after("T_c 0" if n == 1 else f"T_c {n - 1} {g}"))
                    for x in range(8):
                        m = nc.tensor.matmul(bank[4 + g][:, 32 * x:32 * x + 32], A_Tb[:, 8 * g + x, :], T_c[:, 8 * g + x, :],
                                             start=True, stop=True)
                    m.then_inc(*T(f"small Y {n} {g}"))
                if n == 1:
                    pe.wait_ge(*after("silu z 1"))
                if n < 4:
                    await_slab(pe, g0 + 9 + n)
                if n < 3:
                    channel_slab(g0 + 9 + n, 4 * (n - 1), bank[0:2], (0, 1))
                elif n == 3:
                    pe.wait_ge(*after("vb tok 1"))
                    token_slab(g0 + 12, 0, 8, SBW, [bank[2][:, 0:SBW], bank[3][:, 0:SBW]], [0])
                for g in range(2):
                    for c in range(4):
                        pe.wait_ge(*after(f"T_invT block {n - 1} {g} {c}"))
                    pe.wait_ge(*after(f"Y_c {n} {g}"))
                    for x in range(8):
                        m = nc.tensor.matmul(bank[6 + g][:, 32 * x:32 * x + 32], T_invT[:, 8 * g + x, :], Y_c[:, 8 * g + x, :],
                                             start=True, stop=True)
                    m.then_inc(*T(f"small dT {n} {g}"))
                if n < 3:
                    used(channel_slab(g0 + 9 + n, 4 * (n - 1), bank[0:2], (2, 3)))
                elif n == 3:
                    used(token_slab(g0 + 12, 0, 8, SBW, [bank[2][:, 0:SBW], bank[3][:, 0:SBW]], [1]))
            def wide_Y(n, q):
                pe.wait_ge(*after(f"B_T {n} {q}"))
                if n == 0 and q == 0:
                    for g in range(2):
                        for c in range(4):
                            pe.wait_ge(*after(f"T_invT block {len(SMALL) - 1} {g} {c}"))
                    for c in range(4):
                        pe.wait_ge(*after(f"T_inv block {c}"))
                if n > 0:
                    pe.wait_ge(*after(f"T_invT {n - 1} {q}"))
                for x in range(4):
                    m = nc.tensor.matmul(bank[4 + q][:, P * x:P * x + P], B_T[:, q % 2, x, :], T_inv[:, 4 * q + x, :],
                                         start=True, stop=True)
                m.then_inc(*T(f"Y {n} {q}"))

            def wide_dT(n, q):
                y, w = bank[4 + q], LEVELS[n]
                pe.wait_ge(*after(f"Y_g {n} {q}"))
                if n < len(LEVELS) - 1:
                    for x in range(4):
                        m = nc.tensor.matmul(y[:, 64 * x:64 * x + 64], T_invT[:, 4 * q + x, :],
                                             halves(Y_g[:, q % 2, :, :], w, 0)[:, x], start=True, stop=True)
                    m.then_inc(*T(f"dT {n} {q}"))
                if n == 0 and q == 0:
                    pe.wait_ge(*after("sk"))
                    pe.wait_ge(*after("s_val"))
                for x in range(4):
                    m = nc.tensor.matmul(bank[q][:, 64 * x:64 * x + 64], Y_g[:, q % 2, x, :],
                                         halves(T_invT[:, 4 * q:4 * q + 4, :], w, 1)[:, x], start=True, stop=True)
                m.then_inc(*T(f"dTT {n} {q}"))

            wide = [(n, q) for n in range(len(LEVELS)) for q in range(4)]
            wide_Y(*wide[0])
            for now, then in zip(wide, wide[1:] + [None]):
                if then:
                    wide_Y(*then)
                wide_dT(*now)
            last = len(LEVELS) - 1

            def heads(o, left, right, name, pairs=False):
                for hh in range(GH):
                    m = nc.tensor.matmul(o(hh), left(hh), right(hh), start=True, stop=True)
                m.then_inc(*T(name))

            half = lambda hh: slice(64 * (hh % 2), 64 * (hh % 2) + 64)
            col = lambda hh: slice(64 * hh, 64 * hh + 64)
            pe.wait_ge(*after(f"T_invT {last} 3"))
            stick_scores(pe)
            heads(lambda x: bank[2][:, col(x)], lambda x: T_invT[:, x, :], lambda x: vb_tok[:, 0, col(x)], "v_new 0")
            pe.wait_ge(*after("v_new in place 0"))
            pe.wait_ge(*after("k_dec"))
            heads(lambda x: bank[6][half(x), col(x // 2)], lambda x: k_dec[:, col(x)],
                  lambda x: v_new[:, 0, col(x)], "state")
            heads(lambda x: bank[5][:, col(x)], lambda x: QK_T[:, x, :], lambda x: v_new[:, 0, col(x)], "o 0")
            pe.wait_ge(*after("state in place"))
            pe.wait_ge(*after("sb zp 2"))
            heads(lambda x: bank[3 if x % 2 else 0][:, col(x // 2)], lambda x: kT[half(x), 1, x // 2, :],
                  lambda x: state[half(x), x // 2, :], "k state")
            heads(lambda x: bank[4 if x % 2 else 7][:, col(x // 2)], lambda x: qkbT[half(x), 1, x // 2, 0, :],
                  lambda x: state[half(x), x // 2, :], "q state")
            pe.wait_ge(*after("rhs 1"))
            heads(lambda x: bank[1][:, col(x)], lambda x: T_invT[:, GH + x, :], lambda x: vb_tok[:, 1, col(x)], "v_new 1")
            pe.wait_ge(*after("v_new in place 1"))
            heads(lambda x: bank[2][:, col(x)], lambda x: QK_T[:, GH + x, :], lambda x: v_new[:, 1, col(x)], "o 1")

        def mixer_scalar(act, g0):
            copy = lambda o, i: nc.scalar.activation(o, i, ACT.Copy)
            two = lambda b: b[:, :].rearrange("p (c n) -> p c n", c=2)

            def evacuate(grp, banks):
                for b in range(2):
                    act.wait_ge(slab_used, g0 + 2 * grp + 2)
                    c = 4 * grp + 2 * b
                    copy(conv_in[:, c:c + 2, 3:3 + SEQ], two(banks[b])).then_inc(*S(f"evacuated {grp} {b}"))

            def silu(grp):
                for b in range(2):
                    c = 4 * grp + 2 * b
                    act.wait_ge(*after(f"conv {c + 1} 3"))
                    nc.scalar.activation(conv_out[:, c:c + 2, :], conv_out[:, c:c + 2, :], ACT.Silu)\
                        .then_inc(*S(f"conv silu {grp} {b}"))

            act.wait_ge(*after("taps"))
            copy(pv_conv, bank[5][:, 0:48]).then_inc(*S("taps in place"))
            make_hi(act, g0 + 3)
            evacuate(0, bank[0:2])
            make_hi(act, g0 + 4)
            make_hi(act, g0 + 5)
            evacuate(1, bank[2:4])
            make_hi(act, g0 + 6)
            silu(0)
            make_hi(act, g0 + 7)
            evacuate(2, bank[0:2])
            make_hi(act, g0 + 8)
            silu(1)
            for n in range(4):
                act.wait_ge(*after(f"qk tokens {n // 2} {n % 2}"))
                nc.scalar.activation(squares[:, n, :], bank[4 + n][:, :], ACT.Square).then_inc(*S(f"squares {n}"))
            make_hi(act, g0 + 9)
            silu(2)
            for t in range(TT):
                act.wait_ge(slab_used, g0 + 8)
                copy(latent[:, t, :], bank[2 + t][:, 0:DW]).then_inc(*S(f"latent {t}"))
            make_hi(act, g0 + 10)
            act.wait_ge(params[2], 80)
            nc.scalar.activation(sm(352, 8), pv_alog, ACT.Exp).then_inc(*S("exp a"))
            act.wait_ge(*after("x gates"))
            nc.scalar.activation(sm(256, 32), sm(192, 32), ACT.Abs).then_inc(*S("abs gates"))
            act.wait_ge(*after("abs gates"))
            nc.scalar.activation(sm(224, 32), sm(256, 32), ACT.Exp, scale=-1.0).then_inc(*S("exp gates"))
            act.wait_ge(*after("exp gates"))
            nc.scalar.activation(sm(288, 16), sm(224, 16), ACT.Ln, bias=1.0).then_inc(*S("ln gates"))
            for n in range(6):
                act.wait_ge(*after(f"turned {n}"))
                src = bank[4 + n % 4][:, :].rearrange("p (r n) -> p r n", r=4)
                dst = (kT[:, 0], qkbT[:, 0, :, 0, :], kT[:, 1], qkbT[:, 1, :, 0, :], qkbT[:, 0, :, 1, :], qkbT[:, 1, :, 1, :])[n]
                copy(dst, src).then_inc(*S(f"turned in place {n}"))
            act.wait_ge(*after("g sums"))
            nc.scalar.activation(sm(368, 32), bank[6][:, 0:32], ACT.Exp).then_inc(*S("eg"))
            for q in range(4):
                act.wait_ge(*after(f"decay sums {q}"))
                if q >= 2:
                    act.wait_ge(*after(f"A_T {q - 2} 1"))
                nc.scalar.activation(decay[:, q % 2, :, :], bank[7 - q % 2][:, :].rearrange("p (x n) -> p x n", x=4),
                                     ACT.Exp).then_inc(*S(f"decay exp {q}"))
            for c in (2, 3):
                if c == 2:
                    act.wait_ge(*after("A_T 3 1"))
                copy(D_c[32 * c:32 * c + 32, :, :], diagonal(A_T, c)).then_inc(*S(f"A_T block {c}"))

            def blocks(n, g):
                act.wait_ge(*after("TT_c 0" if n == 0 else f"TT_c {n} {g}"))
                if n == 0:
                    act.wait_ge(*after("T_invT zero"))
                k = slice(8 * g, 8 * g + 8)
                for c in (2, 3):
                    copy(diagonal(T_invT[:, k, :], c), TT_c[32 * c:32 * c + 32, k, :]).then_inc(*S(f"T_invT block {n} {g} {c}"))

            blocks(0, 0)
            blocks(0, 1)
            for t in range(TT):
                act.wait_ge(slab_used, g0 + 10)
                nc.scalar.activation(silu_z[:, t, :], bank[t][:, :], ACT.Silu).then_inc(*S(f"silu z {t}"))
            for n in range(1, len(SMALL)):
                for g in range(2):
                    act.wait_ge(*after(f"small Y {n} {g}"))
                    copy(Y_c[:, 8 * g:8 * g + 8, :], bank[4 + g][:, 0:256].rearrange("p (x n) -> p x n", x=8))\
                        .then_inc(*S(f"Y_c {n} {g}"))
                if n == 1:
                    make_hi(act, g0 + 11)
                for g in range(2):
                    blocks(n, g)
                if n == 1:
                    make_hi(act, g0 + 12)
                if n == 2:
                    for w, o in (("sq", sqT), ("sk", skT)):
                        b = bank[0 if w == "sq" else 1]
                        act.wait_ge(slab_used, g0 + 12)
                        copy(o[:, :, :], two(b)).then_inc(*S(w))
                    make_hi(act, g0 + 13)
                    make_hi(act, g0 + 14)
                if n == 3:
                    for t in range(TT):
                        act.wait_ge(slab_used, g0 + 13)
                        copy(s_val[:, t, :], bank[2 + t][:, 0:SBW]).then_inc(*S("s_val" if t else "s_val 0"))
                    make_hi(act, g0 + 15)
            act.wait_ge(*after("T_inv zero"))
            for c in (2, 3):
                copy(diagonal(T_inv, c), T_c[32 * c:32 * c + 32, :, :]).then_inc(*S(f"T_inv block {c}"))
            for n in range(len(LEVELS)):
                for q in range(4):
                    act.wait_ge(*after(f"Y {n} {q}"))
                    if q >= 2:
                        act.wait_ge(*after(f"dTT {n} {q - 2}"))
                    elif n >= 1:
                        act.wait_ge(*after(f"dTT {n - 1} {q + 2}"))
                    copy(Y_g[:, q % 2, :, :], bank[4 + q][:, :].rearrange("p (x n) -> p x n", x=4))\
                        .then_inc(*S(f"Y_g {n} {q}"))
            act.wait_ge(*after("v_new 0"))
            act.wait_ge(*after("k_dec"))
            copy(v_new[:, 0, :], bank[2][:, :]).then_inc(*S("v_new in place 0"))
            act.wait_ge(*after("state"))
            copy(state, bank[6][:, 0:256].rearrange("p (r n) -> p r n", r=4)).then_inc(*S("state in place"))
            stick_scalar(act)
            act.wait_ge(*after("v_new 1"))
            copy(v_new[:, 1, :], bank[1][:, :]).then_inc(*S("v_new in place 1"))

        def mixer_vector(dve, g0):
            TTn, TS, STT = nc.vector.tensor_tensor, nc.vector.tensor_scalar, nc.vector.scalar_tensor_tensor
            lo = lambda n: make_lo(dve, lo_dve, g0 + n)
            per_head = lambda x: x.rearrange("p (h n) -> p h n", n=GD)

            def spread(x, n=GD):
                return x.unsqueeze(2).to_broadcast([P, x.shape[1], n])

            def conv(grp):
                for b in range(2):
                    dve.wait_ge(*after(f"evacuated {grp} {b}"))
                    for k in range(CONV):
                        for c in (4 * grp + 2 * b, 4 * grp + 2 * b + 1):
                            tap = pv_conv[:, 12 * k + c:12 * k + c + 1]
                            src = conv_in[:, c, k:k + SEQ]
                            if k == 0:
                                ins = TS(conv_out[:, c, :], src, tap, None, ALU.mult)
                            else:
                                dve.wait_ge(*after(f"conv {c} {k - 1}"))
                                ins = STT(conv_out[:, c, :], src, tap, conv_out[:, c, :], ALU.mult, ALU.add)
                            ins.then_inc(*V(f"conv {c} {k}"))

            dve.wait_ge(*after("pads"))
            dve.wait_ge(*after("taps in place"))
            lo(3)
            lo(4)
            conv(0)
            lo(5)
            lo(6)
            conv(1)
            lo(7)
            lo(8)
            conv(2)
            lo(9)
            x, e, l, g, be, den, ea = sm(192, 32), sm(224, 32), sm(288, 16), sm(304, 16), sm(320, 16), sm(336, 16), sm(352, 8)
            th = lambda v: v.rearrange("p (t h) -> p t h", t=TT)
            over_t = lambda v: v.unsqueeze(1).to_broadcast([P, TT, GH])
            dve.wait_ge(params[2], 80)
            dve.wait_ge(*after("latent 1"))
            TTn(th(x[:, 0:16]), latent[:, :, 0:8], over_t(pv_dt), ALU.add).then_inc(*V("x decay"))
            nc.vector.tensor_copy(th(x[:, 16:32]), latent[:, :, 8:16]).then_inc(*V("x gates"))
            for n in range(4):
                dve.wait_ge(*after(f"squares {n}"))
                nc.vector.tensor_reduce(sm(64 + 8 * n, 8), per_head(squares[:, n, :]), AX.X, ALU.add)\
                    .then_inc(*V(f"square sums {n}"))
            dve.wait_ge(*after("square sums 3"))
            rn = small[:, 96:192].rearrange("p (s n) -> p s n", s=3)
            rsqrt(dve, "unit", rn, sm(64, 32), RMS_EPS)
            dve.wait_ge(*after("unit"))
            TS(rn[:, 0, 0:16], rn[:, 0, 0:16], GD ** -0.5, None, ALU.mult).then_inc(*V("unit q"))
            dve.wait_ge(*after("unit q"))
            for t in range(TT):
                TTn(per_head(q_tok[:, t, :]), per_head(bank[4 + t][:, :]), spread(rn[:, 0, 8 * t:8 * t + 8]), ALU.mult)\
                    .then_inc(*V(f"q tok {t}"))
                TTn(per_head(k_tok[:, t, :]), per_head(bank[6 + t][:, :]), spread(rn[:, 0, 16 + 8 * t:24 + 8 * t]),
                    ALU.mult).then_inc(*V(f"k tok {t}"))
            lo(10)
            dve.wait_ge(*after("exp gates"))
            TS(den, e[:, 16:32], 1.0, None, ALU.add).then_inc(*V("beta den"))
            STT(be, x[:, 16:32], 0.0, e[:, 16:32], ALU.is_ge, ALU.max).then_inc(*V("beta num"))
            dve.wait_ge(*after("beta den"))
            nc.vector.reciprocal(den, den).then_inc(*V("beta rec"))
            dve.wait_ge(*after("beta rec"))
            dve.wait_ge(*after("beta num"))
            TTn(be, be, den, ALU.mult).then_inc(*V("beta"))
            dve.wait_ge(*after("ln gates"))
            STT(l, x[:, 0:16], 0.0, l, ALU.max, ALU.add).then_inc(*V("softplus"))
            dve.wait_ge(*after("softplus"))
            dve.wait_ge(*after("exp a"))
            STT(th(g), th(l), -1.0, over_t(ea), ALU.mult, ALU.mult).then_inc(*V("g"))
            dve.wait_ge(*after("beta"))
            for t in range(TT):
                dve.wait_ge(*after(f"v tokens {t}"))
                TTn(per_head(vb_tok[:, t, :]), per_head(bank[2 + t][:, :]), spread(be[:, 8 * t:8 * t + 8]), ALU.mult)\
                    .then_inc(*V(f"vb tok {t}"))
            four = lambda c: tab[:, c:c + P].unsqueeze(1).to_broadcast([P, 4, P])

            for q in range(4):
                dve.wait_ge(*after(f"decay exp {q}"))
                TTn(decay[:, q % 2, :, :], decay[:, q % 2, :, :], four(C_UI), ALU.mult).then_inc(*V(f"decay {q}"))
                dve.wait_ge(*after(f"decay {q}"))
                for b in range(2):
                    dve.wait_ge(*after(f"kk {q} {b}"))
                    src = bank[4 + b][:, :].rearrange("p (x w n) -> p x w n", x=2, w=2)
                    pr = slice(4 * q + b, 4 * q + 4, 2)
                    TTn(QK_T[:, pr, :], src[:, :, 0, :], decay[:, q % 2, b::2, :], ALU.mult)\
                        .then_inc(*V(f"QK_T {q} {b}"))
                    TTn(A_T[:, pr, :], src[:, :, 1, :], decay[:, q % 2, b::2, :], ALU.mult)\
                        .then_inc(*V(f"A_T {q} {b}"))
            dve.wait_ge(*after("eg"))
            TTn(sm(400, 16), be, sm(368, 16), ALU.mult).then_inc(*V("beta eg"))
            TTn(per_head(k_dec), per_head(k_tok[:, 0, :]), spread(sm(384, 8)), ALU.mult).then_inc(*V("k_dec"))
            blk = lambda c: slice(32 * c, 32 * c + 32)
            over = lambda at: tab[:, at:at + 32].unsqueeze(1).to_broadcast([P, PR, 32])
            dve.wait_ge(*after("A_T 3 1"))
            for c in (0, 1):
                nc.vector.tensor_copy(D_c[blk(c), :, :], diagonal(A_T, c)).then_inc(*V(f"A_T block {c}"))
            for c in range(4):
                dve.wait_ge(*after(f"A_T block {c}"))
            TTn(TT_c[:, :, :], D_c[:, :, :], over(C_CM), ALU.mult).then_inc(*V("D_c 0"))
            dve.wait_ge(*after("D_c 0"))
            TTn(TT_c[:, :, :], over(C_CI), TT_c[:, :, :], ALU.subtract).then_inc(*V("TT_c 0"))
            dve.wait_ge(*after("TT_c 0"))
            nc.vector.transpose(T_c.rearrange("p x n -> p (x n)"), TT_c.rearrange("p x n -> p (x n)")).then_inc(*V("T_c 0"))

            def blocks(n, g):
                if n == 0:
                    dve.wait_ge(*after("T_invT zero"))
                k = slice(8 * g, 8 * g + 8)
                for c in (0, 1):
                    nc.vector.tensor_copy(diagonal(T_invT[:, k, :], c), TT_c[blk(c), k, :])\
                        .then_inc(*V(f"T_invT block {n} {g} {c}"))

            blocks(0, 0)
            blocks(0, 1)
            lo(11)
            for n in range(1, len(SMALL)):
                for g in range(2):
                    k = slice(8 * g, 8 * g + 8)
                    dve.wait_ge(*after(f"small dT {n} {g}"))
                    TTn(D_c[:, k, :], bank[6 + g][:, 0:256].rearrange("p (x n) -> p x n", x=8),
                        tab[:, C_CM + 32 * n:C_CM + 32 * n + 32].unsqueeze(1).to_broadcast([P, 8, 32]), ALU.mult)\
                        .then_inc(*V(f"D_c {n} {g}"))
                    dve.wait_ge(*after(f"D_c {n} {g}"))
                    TTn(T_c[:, k, :], T_c[:, k, :], D_c[:, k, :], ALU.subtract).then_inc(*V(f"T_c {n} {g}"))
                    dve.wait_ge(*after(f"T_c {n} {g}"))
                    nc.vector.transpose(TT_c[:, k, :].rearrange("p x n -> p (x n)"), T_c[:, k, :].rearrange("p x n -> p (x n)"))\
                        .then_inc(*V(f"TT_c {n} {g}"))
                    dve.wait_ge(*after(f"TT_c {n} {g}"))
                    blocks(n, g)
                if n < 4:
                    for m in ((12,), (13, 14), (15,))[n - 1]:
                        lo(m)
            dve.wait_ge(*after("T_inv zero"))
            for c in (0, 1):
                nc.vector.tensor_copy(diagonal(T_inv, c), T_c[blk(c), :, :]).then_inc(*V(f"T_inv block {c}"))
            for n, w in enumerate(LEVELS):
                for q in range(4):
                    pr = slice(4 * q, 4 * q + 4)
                    part = lambda b: b[:, 0:256].rearrange("p (x a n) -> p x a n", x=4, n=w)
                    if n < len(LEVELS) - 1:
                        dve.wait_ge(*after(f"dT {n} {q}"))
                        e = halves(T_inv[:, pr, :], w, 0)
                        TTn(e, e, part(bank[4 + q]), ALU.subtract).then_inc(*V(f"T_inv {n} {q}"))
                    dve.wait_ge(*after(f"dTT {n} {q}"))
                    e = halves(T_invT[:, pr, :], w, 1)
                    TTn(e, e, part(bank[q]), ALU.subtract).then_inc(*V(f"T_invT {n} {q}"))
            stick_masks(dve)
            dve.wait_ge(*after("k state"))
            for b in range(2):
                TTn(per_head(k_dec)[:, b::2, :], per_head(bank[3 if b else 0][:, 0:256]), spread(sm(408, 8)[:, b::2]),
                    ALU.mult).then_inc(*V("k state beta" if b else "k state beta 0"))
            dve.wait_ge(*after("k state beta"))
            TTn(vb_tok[:, 1, :], vb_tok[:, 1, :], k_dec, ALU.subtract).then_inc(*V("rhs 1"))
            o0, o1 = mixed[:, 0, 0:GW], mixed[:, 1, 0:GW]
            dve.wait_ge(*after("o 0"))
            nc.vector.tensor_copy(o0, bank[5][:, :]).then_inc(*V("o in place 0"))
            dve.wait_ge(*after("q state"))
            for b in range(2):
                TTn(per_head(o1)[:, b::2, :], per_head(bank[4 if b else 7][:, 0:256]), spread(sm(376, 8)[:, b::2]),
                    ALU.mult).then_inc(*V("o old 1" if b else "o old even"))
            latent_units(dve)
            stick_rests(dve)
            rotary_keys(dve)
            dve.wait_ge(*after("o 1"))
            dve.wait_ge(*after("o old 1"))
            TTn(o1, o1, bank[2][:, :], ALU.add).then_inc(*V("o in place 1"))
            stick_exponents(dve)
            for t in range(TT):
                dve.wait_ge(*after(f"o in place {t}"))
                TTn(o_squares[:, t, :], mixed[:, t, 0:GW], mixed[:, t, 0:GW], ALU.mult).then_inc(*V(f"o squares {t}"))
                dve.wait_ge(*after(f"o squares {t}"))
                nc.vector.tensor_reduce(sm(416 + 8 * t, 8), per_head(o_squares[:, t, :]), AX.X, ALU.add)\
                    .then_inc(*V(f"o square sums {t}"))
            rn2 = small[:, 432:480].rearrange("p (s n) -> p s n", s=3)
            dve.wait_ge(*after("o square sums 1"))
            rsqrt(dve, "o unit", rn2, sm(416, 16), RMS_EPS, 1.0 / GD)
            dve.wait_ge(*after("o unit"))
            rotary_queries(dve)
            for t in range(TT):
                o = per_head(mixed[:, t, 0:GW])
                TTn(o, o, spread(rn2[:, 0, 8 * t:8 * t + 8]), ALU.mult).then_inc(*V(f"o a {t}"))
                dve.wait_ge(*after(f"o a {t}"))
                TTn(o, o, pv_gnorm.unsqueeze(1).to_broadcast([P, GH, GD]), ALU.mult).then_inc(*V(f"o b {t}"))
                dve.wait_ge(*after(f"o b {t}"))
                TTn(mixed[:, t, 0:GW], mixed[:, t, 0:GW], silu_z[:, t, :], ALU.mult).then_inc(*V(f"gdn {t}"))

        def mixer_gpsimd(pool, g0):
            lo = lambda n: make_lo(pool, lo_pool, g0 + n)
            nc.gpsimd.memset(conv_in[:, :, 0:3], 0.0).then_inc(*G("pads"))
            for n in range(3, 10):
                lo(n)
            nc.gpsimd.memset(T_invT[:, :, :], 0.0).then_inc(*G("T_invT zero"))
            lo(10)
            per_head = lambda x: x.rearrange("p (h n) -> p h n", n=GD)
            pool.wait_ge(*after("beta"))
            for t in range(TT):
                pool.wait_ge(*after(f"k tok {t}"))
                nc.gpsimd.tensor_tensor(per_head(kb_tok[:, t, :]), per_head(k_tok[:, t, :]),
                                        sm(320 + 8 * t, 8).unsqueeze(2).to_broadcast([P, GH, GD]), ALU.mult)\
                    .then_inc(*G(f"kb tok {t}"))

            def g_upto_of(q):
                if q >= 2:
                    pool.wait_ge(*after(f"decay sums {q - 2}"))
                nc.gpsimd.tensor_tensor(g_upto[:, q % 2, :, :], four(C_UI),
                                        sm(304 + 4 * q, 4).unsqueeze(2).to_broadcast([P, 4, P]), ALU.mult)\
                    .then_inc(*G(f"g upto {q}"))

            four = lambda at: tab[:, at:at + P].unsqueeze(1).to_broadcast([P, 4, P])
            pool.wait_ge(*after("g"))
            g_upto_of(0)
            g_upto_of(1)
            pool.wait_ge(*after("turned 5"))
            nc.gpsimd.memset(T_inv[:, :, :], 0.0).then_inc(*G("T_inv zero"))
            g_upto_of(2)
            g_upto_of(3)
            for q in range(4):
                pool.wait_ge(*after(f"A_T {q} 1"))
                nc.gpsimd.tensor_tensor(A_Tb[:, 4 * q:4 * q + 4, :], A_T[:, 4 * q:4 * q + 4, :], four(C_BD), ALU.mult)\
                    .then_inc(*G(f"A_Tb {q}"))
            lo(11)
            lo(12)
            for n in range(13, 16):
                lo(n)
            for n in range(len(LEVELS)):
                for q in range(4):
                    if n == 0 and q == 0:
                        pool.wait_ge(*after(f"small Y {len(SMALL) - 1} 1"))
                    if q >= 2:
                        pool.wait_ge(*after(f"Y {n} {q - 2}"))
                    elif n >= 1:
                        pool.wait_ge(*after(f"Y {n - 1} {q + 2}"))
                    nc.gpsimd.tensor_tensor(B_T[:, q % 2, :, :], A_T[:, 4 * q:4 * q + 4, :], four(C_LV + P * n), ALU.mult)\
                        .then_inc(*G(f"B_T {n} {q}"))

        sb_z = place("sb_z", 0, 3, 512)
        sb_e = place("sb_e", 4096, 3, 512)
        sb_sp = place("sb_sp", 6192, 3, 512)
        SB_GROUPS = [(0, 0), (0, 1), (1, 1)]
        w_uq = place("w_uq", 13360, 2, MH * MD)
        w_ukv = arena[:, 14128:14128 + MH * (MN + MV)]
        l_unit = place("l_unit", 15408, TT, MQ + MKV)
        l_T = place("l_T", 16176, 3, SEQ)
        l_val = place("l_val", 3584, TT, MH, MV)
        l_q = place("l_q", 8240, TT, MH, MD)
        l_k = place("l_k", 9008, TT, MH, MD)
        rot = arena[:, 9776:10288].rearrange("p (m t h n) -> p m t h n", m=4, t=TT, h=MH)
        rotk = arena[:, 12848:12976].rearrange("p (m t n) -> p m t n", m=4, t=TT)
        l_qT = arena[0:MD, 10288:11312].rearrange("p (h n) -> p h n", h=MH)
        l_kT = arena[0:MD, 11312:12336].rearrange("p (h n) -> p h n", h=MH)
        l_s = [place("l_s0", 12336, MH, P), place("l_s1", 16432, MH, SEQ)]
        l_pT = place("l_pT", 17456, 12, P)

        def head_half(x):
            return slice(64 * (x % 2), 64 * (x % 2) + 64)

        def sb_bank(n, x):
            b = bank[(3, 4, 0, 1)[2 * (n // 2) + x % 2]]
            c = 256 * (n % 2) + P * (x // 2)
            return b[:, c:c + P]

        def attention_load(sp, l):
            sp.wait_ge(*after("q state"))
            nc.sync.dma_start(w_uq[:, :, :], A["mla_w_uq"].rearrange("l (k p) n -> p (l k) n", p=P)[:, bass.ds(l * 2, 2), :])\
              .then_inc(params[3], 16)
            nc.sync.dma_start(w_ukv, A["mla_w_ukv"].rearrange("l k n -> (l k) n")[bass.ds(l * MKV, MKV), :])\
              .then_inc(params[3], 16)

        def stick_scores(pe):
            for n, (kt, qt) in enumerate(SB_GROUPS):
                for x in range(SBH):
                    m = nc.tensor.matmul(sb_bank(n, x), skT[head_half(x), x // 2, tokens(kt)],
                                         sqT[head_half(x), x // 2, tokens(qt)], start=True, stop=True)
                m.then_inc(*T(f"sb z {n}"))

        def stick_scalar(act):
            for n in range(3):
                act.wait_ge(*after(f"sb zp {n}"))
                nc.scalar.activation(sb_e[:, n, :], sb_z[:, n, :], ACT.Abs).then_inc(*S(f"sb abs {n}"))
                act.wait_ge(*after(f"sb abs {n}"))
                nc.scalar.activation(sb_e[:, n, :], sb_e[:, n, :], ACT.Exp, scale=-1.0).then_inc(*S(f"sb exp {n}"))
            for n in (0, 2, 1):
                act.wait_ge(*after(f"sb exp {n}"))
                nc.scalar.activation(sb_e[:, n, :], sb_e[:, n, :], ACT.Ln, bias=1.0).then_inc(*S(f"sb ln {n}"))

        def stick_masks(dve):
            TTn, TS, STT = nc.vector.tensor_tensor, nc.vector.tensor_scalar, nc.vector.scalar_tensor_tensor
            h4 = lambda x: x.rearrange("p (h n) -> p h n", h=4)
            dve.wait_ge(*after(f"B_T {len(LEVELS) - 1} 3"))
            for n in range(3):
                dve.wait_ge(*after(f"sb z {max(n, 1)}"))
                for b in range(2):
                    src = bank[(3, 4, 0, 1)[2 * (n // 2) + b]][:, 256 * (n % 2):256 * (n % 2) + 256]
                    src = src.rearrange("p (h n) -> p h n", h=2)
                    o = h4(sb_z[:, n, :])[:, b::2, :]
                    if n == 1:
                        ins = TS(o, src, SBD ** -0.5, None, ALU.mult)
                    else:
                        ins = STT(o, src, SBD ** -0.5,
                                  tab[:, C_NS:C_NS + P].unsqueeze(1).to_broadcast([P, 2, P]), ALU.mult, ALU.add)
                    ins.then_inc(*V(f"sb zp {n}" if b else f"sb zp even {n}"))

        def latent_units(dve):
            TTn, TS, STT = nc.vector.tensor_tensor, nc.vector.tensor_scalar, nc.vector.scalar_tensor_tensor
            sq = small[:, 64:68]
            for t in range(TT):
                for b, c, w in ((0, 0, MQ), (1, MQ, MKV)):
                    x = latent[:, t, 16 + c:16 + c + w]
                    nc.vector.tensor_tensor_reduce(l_unit[:, t, c:c + w], x, x, 1.0 / w, 0.0, ALU.mult, ALU.add,
                                                   sq[:, 2 * t + b:2 * t + b + 1]).then_inc(*V(f"l squares {t} {b}"))
            dve.wait_ge(*after("l squares 1 1"))
            lr = small[:, 68:80].rearrange("p (s n) -> p s n", s=3)
            rsqrt(dve, "l rms", lr, sq, RMS_EPS)
            dve.wait_ge(*after("l rms"))
            for t in range(TT):
                for b, c, w in ((0, 0, MQ), (1, MQ, MKV)):
                    STT(l_unit[:, t, c:c + w], latent[:, t, 16 + c:16 + c + w], lr[:, 0, 2 * t + b:2 * t + b + 1],
                        pv_qn[:, c:c + w], ALU.mult, ALU.mult).then_inc(*V(f"l unit {t} {b}"))

        def stick_rests(dve):
            TTn, TS, STT = nc.vector.tensor_tensor, nc.vector.tensor_scalar, nc.vector.scalar_tensor_tensor
            for n in (0, 2, 1):
                dve.wait_ge(*after(f"sb ln {n}"))
                STT(sb_sp[:, n, :], sb_z[:, n, :], 0.0, sb_e[:, n, :], ALU.max, ALU.add).then_inc(*V(f"sb sp {n}"))

        def stick_exponents(dve):
            TTn, TS, STT = nc.vector.tensor_tensor, nc.vector.tensor_scalar, nc.vector.scalar_tensor_tensor
            cb = [bank[6], bank[7], bank[5]]
            for n in (0, 1, 2):
                dve.wait_ge(*after(f"sb rest {n}"))
                TTn(sb_e[:, n, :], sb_z[:, n, :], cb[n][:, :], ALU.subtract).then_inc(*V(f"sb d {n}"))

        def rotary_keys(dve):
            TTn = nc.vector.tensor_tensor
            cos, sin = rope1[:, 0, :, :], rope1[:, 1, :, :]
            kr = latent[:, :, 16 + MQ + MKV:16 + MLW]
            hm = MR // 2
            TTn(rotk[:, 0], kr[:, :, 0:hm], cos, ALU.mult).then_inc(*V("rk 0"))
            TTn(rotk[:, 1], kr[:, :, hm:MR], sin, ALU.mult).then_inc(*V("rk 1"))
            TTn(rotk[:, 2], kr[:, :, hm:MR], cos, ALU.mult).then_inc(*V("rk 2"))
            TTn(rotk[:, 3], kr[:, :, 0:hm], sin, ALU.mult).then_inc(*V("rk 3"))
            dve.wait_ge(*after("rk 3"))
            over = lambda x: x.unsqueeze(1).to_broadcast([P, MH, hm])
            dve.wait_ge(*after("v_new 1"))
            for t in range(TT):
                TTn(l_k[:, t, :, MN:MN + hm], over(rotk[:, 0, t]), over(rotk[:, 1, t]), ALU.subtract).then_inc(*V(f"rk a {t}"))
                TTn(l_k[:, t, :, MN + hm:MD], over(rotk[:, 2, t]), over(rotk[:, 3, t]), ALU.add).then_inc(*V(f"rk b {t}"))

        def rotary_queries(dve):
            TTn = nc.vector.tensor_tensor
            cos, sin = rope1[:, 0, :, :], rope1[:, 1, :, :]
            hm = MR // 2
            over = lambda x: x.unsqueeze(1).to_broadcast([P, MH, hm])
            for t in range(TT):
                dve.wait_ge(*after(f"l q in place {t}"))
                x1, x2 = l_q[:, t, :, MN:MN + hm], l_q[:, t, :, MN + hm:MD]
                c, s = over(cos[:, t]), over(sin[:, t])
                TTn(rot[:, 0, t], x1, c, ALU.mult).then_inc(*V(f"rq 0 {t}"))
                TTn(rot[:, 1, t], x2, s, ALU.mult).then_inc(*V(f"rq 1 {t}"))
                TTn(rot[:, 2, t], x2, c, ALU.mult).then_inc(*V(f"rq 2 {t}"))
                TTn(rot[:, 3, t], x1, s, ALU.mult).then_inc(*V(f"rq 3 {t}"))
            dve.wait_ge(*after("rq 3 1"))
            TTn(l_q[:, 0, :, MN:MN + hm], rot[:, 0, 0], rot[:, 1, 0], ALU.subtract).then_inc(*V("rq a 0"))
            TTn(l_q[:, 1, :, MN:MN + hm], rot[:, 0, 1], rot[:, 1, 1], ALU.subtract).then_inc(*V("rq a 1"))
            TTn(l_q[:, 0, :, MN + hm:MD], rot[:, 2, 0], rot[:, 3, 0], ALU.add).then_inc(*V("rq b 0"))
            TTn(l_q[:, 1, :, MN + hm:MD], rot[:, 2, 1], rot[:, 3, 1], ALU.add).then_inc(*V("l q whole"))

        def turn_mixed(pe, half):
            for t in range(TT):
                pe.wait_ge(*after(f"gdn {t}" if half == 0 else f"mixed {t}"))
                if half == 0:
                    pe.wait_ge(*after("l val 1"))
                for q in range(4):
                    m = nc.tensor.transpose((bank[4 + t] if half else bank[6 + t])[:, P * q:P * q + P],
                                            mixed[:, t, P * (4 * half + q):P * (4 * half + q) + P], ident)
                m.then_inc(*T(f"tm turned {2 * t + half}"))

        def attention_tensor(pe, m4):
            cb = [bank[6], bank[7], bank[5]]
            pe.wait_ge(*after("o old 1"))
            for n in range(3):
                pe.wait_ge(*after(f"sb sp {n}"))
                if n == 0:
                    pe.wait_ge(*after("o in place 0"))
                if n == 1:
                    pe.wait_ge(*after("sb sp 2"))
                    nc.tensor.matmul(cb[n][:, :], tab[:, C_ONE:C_ONE + P], sb_sp[:, 2, :], start=True, stop=False)
                nc.tensor.matmul(cb[n][:, :], tab[:, C_LI:C_LI + P], sb_sp[:, n, :], start=n != 1, stop=True)\
                    .then_inc(*T(f"sb rest {n}"))
            for k in range(3):
                for t in range(TT):
                    pe.wait_ge(*after(f"l unit {t} {0 if k < 2 else 1}"))
                    if k == 0 and t == 0:
                        pe.wait_ge(*after("o in place 1"))
                        pe.wait_ge(*after("sb zp 2"))
                    o = bank[2 if k < 2 else 4]
                    m = nc.tensor.transpose(o[:, 256 * (k % 2) + P * t:256 * (k % 2) + P * t + P],
                                            l_unit[:, t, P * k:P * k + P], ident)
                if k >= 1:
                    m.then_inc(*T(f"l turned {k - 1}"))
            pe.wait_ge(params[3], 32)
            pe.wait_ge(*after("l T 1"))
            pe.wait_ge(*after("sb d 2"))
            pe.wait_ge(*after("o in place 0"))
            for t in range(TT):
                for k in range(2):
                    m = nc.tensor.matmul(bank[4 + t if t else 1][:, 0:MH * MD], l_T[:, k, tokens(t)], w_uq[:, k, :],
                                         start=k == 0, stop=k == 1)
                m.then_inc(*T(f"l q {t}"))
                nc.tensor.matmul(bank[6 + t][:, :], l_T[:, 2, tokens(t)], w_ukv, start=True, stop=True)\
                    .then_inc(*T(f"l kv {t}"))
            for n in range(3):
                pe.wait_ge(*after(f"sb w {n}"))
            for t in range(TT):
                for x in range(SBH):
                    o = bank[3][:, 256 * t + 64 * x:256 * t + 64 * x + 64]
                    gs = [(0, 0)] if t == 0 else [(1, 0), (2, 1)]
                    for i, (n, kt) in enumerate(gs):
                        m = nc.tensor.matmul(o, sb_e[:, n, P * x:P * x + P], s_val[:, kt, 64 * x:64 * x + 64],
                                             start=i == 0, stop=i == len(gs) - 1)
            m.then_inc(*T("sb out"))
            kb = [bank[0], bank[2], bank[4], bank[3]]
            pe.wait_ge(*after("sb out in place"))
            for i, (w, src) in enumerate((("q", l_q), ("k", l_k))):
                for t in range(TT):
                    if w == "q":
                        pe.wait_ge(*after("l q whole"))
                    else:
                        pe.wait_ge(*after("l k plain 1"))
                        pe.wait_ge(*after("rk b 1"))
                    for x in range(MH):
                        m = nc.tensor.transpose(kb[2 * i + t][0:MD, P * x:P * x + P], src[:, t, x, :], ident)
                    m.then_inc(*T(f"l {w}T {t}"))
            turn_mixed(pe, 0)
            for w in "qk":
                for t in range(TT):
                    pe.wait_ge(*after(f"l {w}T in place {t}"))
            for t in range(TT):
                pe.wait_ge(*after(f"tm lo {2 * t}"))
            sbk = [bank[5], bank[6], bank[7]]
            for x in range(MH):
                m = nc.tensor.matmul(sbk[0][:, P * x:P * x + P], l_qT[:, x, 0:P], l_kT[:, x, 0:P], start=True, stop=True)
            m.then_inc(*T("l s 0"))
            for x in range(MH):
                m = nc.tensor.matmul(sbk[1 + x // 2][:, 256 * (x % 2):256 * (x % 2) + 256], l_qT[:, x, P:2 * P],
                                     l_kT[:, x, :], start=True, stop=True)
                if x % 2:
                    m.then_inc(*T(f"l s {1 + x // 2}"))
            await_slab(pe, m4)
            wide_slab(m4, (xhi, xlo), 0, True, False).then_inc(slab_used, 1)
            pb = [bank[4], bank[5], bank[6]]
            for n in range(3):
                for b in range(4):
                    if n == 0:
                        src = l_s[0][:, b, :]
                    else:
                        x, kt = 2 * (n - 1) + b // 2, b % 2
                        src = l_s[1][:, x, tokens(kt)]
                    pe.wait_ge(*after(f"l p {0 if n == 0 else 1} {b if n == 0 else x}"))
                    m = nc.tensor.transpose(pb[n][:, P * b:P * b + P], src, ident)
                m.then_inc(*T(f"l pT {n}"))
            await_slab(pe, m4 + 1)
            wide_slab(m4 + 1, (xhi, xlo), 2, False, False).then_inc(slab_used, 1)
            for n in range(3):
                pe.wait_ge(*after(f"l pT in place {n}"))
            for t in range(TT):
                for x in range(MH):
                    o = bank[7][:, 256 * t + 64 * x:256 * t + 64 * x + 64]
                    blocks = [(x, 0)] if t == 0 else [(4 + 2 * x, 0), (5 + 2 * x, 1)]
                    for i, (b, kt) in enumerate(blocks):
                        m = nc.tensor.matmul(o, l_pT[:, b, :], l_val[:, kt, x, :], start=i == 0,
                                             stop=i == len(blocks) - 1)
            m.then_inc(*T("l out"))

        def attention_scalar(act):
            copy = lambda o, i: nc.scalar.activation(o, i, ACT.Copy)
            act.wait_ge(*after("l turned 0"))
            copy(l_T[:, 0:2, :], bank[2][:, :].rearrange("p (k n) -> p k n", k=2)).then_inc(*S("l T 0"))
            act.wait_ge(*after("l turned 1"))
            copy(l_T[:, 2, :], bank[4][:, 0:SEQ]).then_inc(*S("l T 1"))
            for n in range(3):
                act.wait_ge(*after(f"sb d {n}"))
                nc.scalar.activation(sb_e[:, n, :], sb_e[:, n, :], ACT.Exp).then_inc(*S(f"sb w {n}"))
            for t in range(TT):
                act.wait_ge(*after(f"l q {t}"))
                copy(l_q[:, t, :, :], bank[4 + t if t else 1][:, 0:MH * MD].rearrange("p (h n) -> p h n", h=MH))\
                    .then_inc(*S(f"l q in place {t}"))
                act.wait_ge(*after(f"l kv {t}"))
                kv = bank[6 + t][:, :].rearrange("p (h n) -> p h n", h=MH)
                copy(l_k[:, t, :, 0:MN], kv[:, :, 0:MN]).then_inc(*S(f"l k plain {t}"))
                copy(l_val[:, t, :, :], kv[:, :, MN:MN + MV]).then_inc(*S(f"l val {t}"))
            act.wait_ge(*after("sb out"))
            copy(mixed[:, :, GW:GW + SBW], bank[3][:, :].rearrange("p (t n) -> p t n", t=TT)).then_inc(*S("sb out in place"))
            kb = [bank[0], bank[2], bank[4], bank[3]]
            for i, (w, dst) in enumerate((("q", l_qT), ("k", l_kT))):
                for t in range(TT):
                    act.wait_ge(*after(f"l {w}T {t}"))
                    copy(dst[:, :, tokens(t)], kb[2 * i + t][0:MD, :].rearrange("p (h n) -> p h n", h=MH))\
                        .then_inc(*S(f"l {w}T in place {t}"))
            for t in range(TT):
                turn_rounded(act, "tm", 2 * t, bank[6 + t])
            act.wait_ge(*after("l minus max 0"))
            act.wait_ge(*after("l minus max 1"))
            for t in range(TT):
                for x in range(MH):
                    k = 4 * t + x
                    nc.scalar.activation(l_s[t][:, x, :], l_s[t][:, x, :], ACT.Exp, bias=small[:, 104 + k:105 + k],
                                         accum_out=small[:, 112 + k:113 + k]).then_inc(*S(f"l p {t} {x}"))
            pb = [bank[4], bank[5], bank[6]]
            act.wait_ge(*after("gdn 1"))
            for n in range(3):
                act.wait_ge(*after(f"l pT {n}"))
                copy(l_pT[:, 4 * n:4 * n + 4, :], pb[n][:, :].rearrange("p (b n) -> p b n", b=4))\
                    .then_inc(*S(f"l pT in place {n}"))

        def attention_vector(dve):
            TTn, TS, STT = nc.vector.tensor_tensor, nc.vector.tensor_scalar, nc.vector.scalar_tensor_tensor
            cb = [bank[6], bank[7], bank[5]]
            four = lambda x, n=P: x.unsqueeze(1).to_broadcast([P, 4, n])
            h4 = lambda x: x.rearrange("p (h n) -> p h n", h=4)
            scale = MD ** -0.5
            for t in range(TT):
                turn_rest(dve, "tm", 2 * t, bank[6 + t])
            dve.wait_ge(*after("l s 0"))
            STT(l_s[0], h4(bank[5][:, :]), scale, four(tab[:, C_NC + P:C_NC + 2 * P]), ALU.mult, ALU.add).then_inc(*V("l s masked 0"))
            for b in range(2):
                dve.wait_ge(*after(f"l s {1 + b}"))
                STT(l_s[1][:, 2 * b:2 * b + 2, :], bank[6 + b][:, :].rearrange("p (h n) -> p h n", h=2), scale,
                    tab[:, C_NC:C_NC + 2 * P].unsqueeze(1).to_broadcast([P, 2, 2 * P]), ALU.mult, ALU.add)\
                    .then_inc(*V(f"l s masked {1 + b}"))
            for t in range(TT):
                dve.wait_ge(*after(f"l s masked {2 * t}"))
                nc.vector.tensor_reduce(small[:, 96 + 4 * t:100 + 4 * t], l_s[t], AX.X, ALU.max).then_inc(*V(f"l max {t}"))
                dve.wait_ge(*after(f"l max {t}"))
                TS(small[:, 104 + 4 * t:108 + 4 * t], small[:, 96 + 4 * t:100 + 4 * t], -1.0, None, ALU.mult)\
                    .then_inc(*V(f"l minus max {t}"))
            dve.wait_ge(*after("l p 1 3"))
            nc.vector.reciprocal(small[:, 120:128], small[:, 112:120]).then_inc(*V("l rec"))
            dve.wait_ge(*after("l rec"))
            dve.wait_ge(*after("l out"))
            for t in range(TT):
                TTn(h4(mixed[:, t, GW + SBW:D]), h4(bank[7][:, 256 * t:256 * t + 256]),
                    small[:, 120 + 4 * t:124 + 4 * t].unsqueeze(2).to_broadcast([P, MH, MV]), ALU.mult)\
                    .then_inc(*V(f"mixed {t}"))

        G_MIX = 3 * FF_STEPS
        G_WO = G_MIX + 13
        G_FFB = G_WO + 4
        G_PLE = G_FFB + 3 * FF_STEPS
        G_END = G_PLE + 5

        p_tok = place("p_tok", 2048, TT, PLE)
        p_proj = place("p_proj", 0, TT, D)
        p_gate = place("p_gate", 4096, TT, D)

        def wide_product(pe, g, n, left, name, k_step=2):
            for i in range(n):
                await_slab(pe, g + i)
                wide_slab(g + i, left, k_step * i, i == 0, i == n - 1, name).then_inc(slab_used, 1)

        def acc_ready(name, last):
            return lambda t: after(name) if t == 0 else (slab_used, last + 1)

        with nc.Block() as block:
            st.start("setup")

            @block.sync
            def _(sp):
                nc.sync.dma_start(h[:, :, :], A["x"].rearrange("b (t p) d -> p (b t) d", p=P)).then_inc(stored, 16)
                nc.sync.dma_start(tab[:, :], A["tables"][:, :]).then_inc(params[1], 16)
                nc.sync.dma_start(arena[:, 0:TT].bitcast(I32), A["positions"].rearrange("b (t p) -> p (b t)", p=P),
                                  allow_slow_non_contiguous=True)\
                  .then_inc(params[1], 16)
                sp.wait_ge(stored, 16)

            @block.vector
            def _(dve):
                TS, STT = nc.vector.tensor_scalar, nc.vector.scalar_tensor_tensor
                n = MR // 2
                pos, ang, turns = arena[:, 2:4], place("ang", 8, TT, n), place("turns", 64, 2, TT * n)
                two_pi = 2 * math.pi
                p1 = 6.28125
                p2 = 0.00193500518798828125
                p3 = two_pi - p1 - p2
                k = [0]

                def link(ins):
                    k[0] += 1
                    ins.then_inc(*V(f"angle {k[0]}"))
                    dve.wait_ge(*after(f"angle {k[0]}"))

                dve.wait_ge(params[1], 32)
                link(nc.vector.tensor_copy(pos, arena[:, 0:TT].bitcast(I32)))
                for t in range(TT):
                    link(TS(ang[:, t, :], tab[:, C_INV:C_INV + n], pos[:, t:t + 1], None, ALU.mult))
                a = ang[:, :, :].rearrange("p t n -> p (t n)")
                for which, shift in ((0, 0.25), (1, 0.0)):
                    w = turns[:, which, :]
                    o = rope1[:, which, :, :].rearrange("p t n -> p (t n)")
                    link(TS(w, a, 1 / two_pi, shift, ALU.mult, ALU.add))
                    link(TS(w, w, 12582912.0, None, ALU.add))
                    link(TS(w, w, -12582912.0, None, ALU.add))
                    link(STT(o, w, -p1, a, ALU.mult, ALU.add))
                    link(STT(o, w, -p2, o, ALU.mult, ALU.add))
                    link(STT(o, w, -p3, o, ALU.mult, ALU.add))
                    link(TS(o, o, shift * two_pi, None, ALU.add))
                    link(TS(o, o, 3.1415925, -3.1415925, ALU.min, ALU.max))
                nc.vector.tensor_copy(pos, pos).then_inc(*V("angles"))

            @block.scalar
            def _(act):
                act.wait_ge(*after("angles"))
                o = rope1[:, :, :, :].rearrange("p b t n -> p (b t n)")
                nc.scalar.activation(o, o, ACT.Sin).then_inc(*S("rotary"))
                act.wait_ge(*after("rotary"))

        def clear():
            with nc.Block() as block:
                @block.gpsimd
                def _(pool):
                    for s in every:
                        pool.sem_clear(s)

        clear()
        with nc.Fori(0, DEPTH) as layer:
            with nc.Block() as block:
                st.start("layer")
                flat2 = lambda name: A[name].rearrange("l k n -> (l k) n")
                m0, m4 = G_MIX, G_WO

                def norm_row(which, c):
                    return A[which].rearrange("l c n -> (l c) n")[bass.ds(layer * 3 + c, 1), :].rearrange("a n -> (a n)")

                @block.sync
                def _(sp):
                    def norm(nth, free):
                        load_norm(sp, nth, norm_row("ln_g", nth), norm_row("ln_b", nth), free)

                    def first_parameters():
                        norm(0, None)
                        small_loads(sp, layer)

                    ff_load(sp, 0, flat2("ffa_w_in"), layer * D, flat2("ffa_w_out"), layer * D_FF, first_parameters)
                    mixer_load(sp, m0, layer)
                    attention_load(sp, layer)
                    norm(1, "tm turned 3")
                    ff_load(sp, G_FFB, flat2("ffb_w_in"), layer * D, flat2("ffb_w_out"), layer * D_FF)
                    norm(2, "n1 done 11")
                    nc.sync.dma_start(p_tok[:, :, :], A["p"].rearrange("l b (t p) n -> p (l b t) n", p=P)[:, bass.ds(layer * TT, TT), :])\
                      .then_inc(params[4], 16)
                    load_slab(sp, G_PLE, 0, wide_parts(flat2("ple_w_proj"), layer * PLE))
                    for n in range(4):
                        load_slab(sp, G_PLE + 1 + n, 0, wide_parts(flat2("ple_w_gate"), layer * D + 2 * P * n))

                @block.tensor
                def _(pe):
                    ff_tensor(pe, 0, 0, "ffa out", ("ta", h, None))
                    turn_tensor(pe, "tb", h, lambda t, n: after(f"n0 done {t}{n}"))
                    pe.wait_ge(*after("tb lo 3"))
                    mixer_tensor(pe, m0)
                    attention_tensor(pe, m4)
                    for w in ("gdn 0", "gdn 1", "sb out in place", "mixed 0", "l pT in place 2"):
                        pe.wait_ge(*after(w))
                    turn_mixed(pe, 1)
                    pe.wait_ge(*after("tm lo 3"))
                    for n in (2, 3):
                        await_slab(pe, m4 + n)
                        wide_slab(m4 + n, (xhi, xlo), 2 * n, False, n == 3, "wo out").then_inc(slab_used, 1)

                    def turn_p():
                        pe.wait_ge(params[4], 16)
                        for k in range(2):
                            for t in range(TT):
                                m = nc.tensor.transpose(bank[6][:, 256 * k + P * t:256 * k + P * t + P],
                                                        p_tok[:, t, P * k:P * k + P], ident)
                        m.then_inc(*T("p turned"))

                    ff_tensor(pe, G_FFB, 1, "ffb out", ("tc", h, lambda t, n: after(f"n1 done {t}{n}")), turn_p)
                    pe.wait_ge(*after("p lo"))
                    pe.wait_ge(*after("n2 sum 11"))
                    wide_product(pe, G_PLE, 1, (ahi, alo), "proj out")
                    turn_tensor(pe, "td", h, lambda t, n: after(f"n2 done {t}{n}"))
                    pe.wait_ge(*after("td lo 3"))
                    pe.wait_ge(*after("proj in place 3"))
                    wide_product(pe, G_PLE + 1, 4, (xhi, xlo), "gate out")

                @block.scalar
                def _(act):
                    turn_scalar(act, "ta")
                    for g in range(RING):
                        make_hi(act, g)
                    ff_scalar(act, 0, 0, True)
                    turn_scalar(act, "tb")
                    make_hi(act, m0 + 2)
                    mixer_scalar(act, m0)
                    attention_scalar(act)
                    for t in range(TT):
                        turn_rounded(act, "tm", 2 * t + 1, bank[4 + t])
                    for n in range(4):
                        if n < 2:
                            make_hi(act, m4 + 3 + n)
                    turn_scalar(act, "tc")
                    make_hi(act, m4 + 5)
                    make_hi(act, m4 + 6)
                    ff_scalar(act, G_FFB, 1, True)
                    act.wait_ge(*after("p turned"))
                    nc.scalar.activation(flat(ahi), bank[6][:, :], ACT.Copy).then_inc(*S("p hi"))
                    make_hi(act, G_PLE + 2)
                    for n in range(4):
                        t, b = n // 2, n % 2
                        act.wait_ge(slab_used, G_PLE + 1)
                        nc.scalar.activation(p_proj[:, t, 512 * b:512 * b + 512], acc[t][b][:, :], ACT.Copy)\
                            .then_inc(*S(f"proj in place {n}"))
                    turn_scalar(act, "td")
                    make_hi(act, G_PLE + 3)
                    make_hi(act, G_PLE + 4)
                    for n in range(4):
                        t, b = n // 2, n % 2
                        act.wait_ge(*acc_ready("gate out", G_END - 1)(t))
                        nc.scalar.activation(p_gate[:, t, 512 * b:512 * b + 512], acc[t][b][:, :], ACT.Tanh, scale=0.5)\
                            .then_inc(*S(f"gate tanh {n}"))

                @block.vector
                def _(dve):
                    turn_vector(dve, "ta")
                    for g in range(RING):
                        make_lo(dve, lo_dve, g)
                    ff_vector(dve, 0, 0, True)
                    norm_vector(dve, "n0", 0.5 / ALPHA, acc_ready("ffa out", G_MIX - 1), 0, "tb")
                    make_lo(dve, lo_dve, m0 + 2)
                    mixer_vector(dve, m0)
                    attention_vector(dve)
                    for t in range(TT):
                        turn_rest(dve, "tm", 2 * t + 1, bank[4 + t])
                    for n in range(2):
                        make_lo(dve, lo_dve, m4 + 3 + n)
                    norm_vector(dve, "n1", 1.0 / ALPHA, acc_ready("wo out", G_FFB - 1), 1, "tc")
                    make_lo(dve, lo_dve, m4 + 5)
                    make_lo(dve, lo_dve, m4 + 6)
                    ff_vector(dve, G_FFB, 1, True)
                    dve.wait_ge(*after("p hi"))
                    nc.vector.tensor_tensor(flat(alo), bank[6][:, :], flat(ahi).bitcast(F32), ALU.subtract).then_inc(*V("p lo"))
                    norm_vector(dve, "n2", 0.5 / ALPHA, acc_ready("ffb out", G_PLE - 1), 2, "td")
                    for n in range(2, 5):
                        make_lo(dve, lo_dve, G_PLE + n)
                    for n in range(4):
                        t, c = n // 2, slice(512 * (n % 2), 512 * (n % 2) + 512)
                        dve.wait_ge(*after(f"gate tanh {n}"))
                        dve.wait_ge(*after(f"proj in place {n}"))
                        nc.vector.scalar_tensor_tensor(p_gate[:, t, c], p_gate[:, t, c], 1.0, p_proj[:, t, c],
                                                       ALU.add, ALU.mult).then_inc(*V(f"gated p {n}"))
                        dve.wait_ge(*after(f"gated p {n}"))
                        nc.vector.scalar_tensor_tensor(h[:, t, c], p_gate[:, t, c], 0.5, h[:, t, c],
                                                       ALU.mult, ALU.add).then_inc(*V(f"layer done {n}"))

                @block.gpsimd
                def _(pool):
                    for g in range(RING):
                        make_lo(pool, lo_pool, g)
                    ff_gpsimd(pool, 0, True)
                    mixer_gpsimd(pool, m0)
                    for n in range(4):
                        make_lo(pool, lo_pool, m4 + 3 + n)
                    ff_gpsimd(pool, G_FFB, True)
                    for n in range(2):
                        make_lo(pool, lo_pool, G_PLE + 3 + n)

            clear()

        G_IN = 3 * FF_STEPS
        IN_ORDER = ("x0", "x1", "q0", "q1", "kv", "g0", "g1", "l0", "l1", "a0", "a1")
        IN_COL = {"g0": 0, "g1": 512, "x0": LRU, "x1": LRU + 512, "q0": 2 * LRU, "q1": 2 * LRU + 512,
                  "kv": 2 * LRU + QW, "l0": 3584, "l1": 4096, "a0": 4608, "a1": 5120}
        assert IN_COL["kv"] + 2 * KVW == IN_COL["l0"] and IN_COL["a1"] + 512 == IN2
        G_PL = G_IN + 2 * len(IN_ORDER)
        G_PA, G_OUT2 = G_PL + 4, G_PL + 8
        G_FF2 = G_PL + 12
        first = {c: G_IN + 2 * n for n, c in enumerate(IN_ORDER)}
        ready = {c: (slab_used, first[c] + 2) for c in IN_ORDER}
        pair = {c: (bank[0:2], bank[2:4])[n % 2] for n, c in enumerate(IN_ORDER)}

        x_norm = place("x_norm", 0, TT, D)
        sq_out = place("sq_out", 12320, TT, D)
        lru_h = place("lru_h", 0, LT, SEQ)
        lru_in = place("lru_in", 2048, LT, SEQ + 4)
        lru_a = place("lru_a", 2048, LT, SEQ)
        lru_x = place("lru_x", 4128, LT, SEQ)
        lru_w = place("lru_w", 6176, 2, LT, P)
        lru_i = place("lru_i", 8224, LT, SEQ)
        lru_m = place("lru_m", 10272, LT, SEQ)
        scores = [place("scores0", 2048, 2, 4, P), place("scores1", 3072, 2, 4, 2 * P)]
        probs_T = place("probs_T", 5120, 12, P)
        gate_l = place("gate_l", 8224, TT, D)
        gate_a = place("gate_a", 10272, TT, D)
        q_rot = place("q_rot", 12320, TT, QH, HD)
        y_attn = place("y_attn", 12320, TT, D)
        k_rot = arena[:, 14368:15392].rearrange("p (t h b n) -> p t h b n", t=TT, h=KVH, b=2)
        v_win = place("v_win", 15392, TT, KVW)
        qT2 = place("qT2", 15904, QH // 2, SEQ)
        kT2 = place("kT2", 17952, KVH, SEQ)
        gelu_g = place("gelu_g", 18976, 2, 2, SEQ)
        merged = place("merged", 2048, TT, D)
        rows64 = arena[0:64, 20000:20000 + P]
        rot_t = gated[:, :, :, :].rearrange("p a b c -> p (a b c)").rearrange("p (m h n) -> p m h n", m=4, h=8)
        pc = pv[:, 0:64]
        half_b = pv[:, 64:80]
        lru_c = pv[:, 80:88]
        lam_t = pv[:, 88:104]
        sinks = pv[:, 104:120]

        pre_gain, post_gain = params[0], params[5]

        def gain_load(sp, side, w, free):
            if free:
                sp.wait_ge(*after(free))
            nc.sync.dma_start(normw[:, side, :], A[w].rearrange("a n -> (a n)").partition_broadcast(P))\
              .then_inc((pre_gain, post_gain)[side], 16)

        def pre_scalar(act, name, source):
            for t in range(TT):
                for n in range(2):
                    if source:
                        act.wait_ge(*after(f"{source} {t}{n}"))
                    k = slice(512 * n, 512 * n + 512)
                    nc.scalar.activation(sq_out[:, t, k], h[:, t, k], ACT.Square,
                                         accum_out=small[:, 40 + 2 * t + n:41 + 2 * t + n]).then_inc(*S(f"{name} squares {t}{n}"))

        def rms_of(dve, name, sums, row, eps, c=1.0, between=()):
            rs = small[:, row:row + 6].rearrange("p (s n) -> p s n", s=3)
            both = sums.rearrange("p (t n) -> p t n", t=TT)
            nc.vector.tensor_tensor(small[:, row + 6:row + 8], both[:, :, 0], both[:, :, 1], ALU.add)\
                .then_inc(*V(f"{name} square sums"))
            dve.wait_ge(*after(f"{name} square sums"))
            rsqrt(dve, f"{name} rms", rs, small[:, row + 6:row + 8], eps / c ** 2, 1.0 / D / c ** 2, between)
            dve.wait_ge(*after(f"{name} rms"))
            return rs

        def pre_vector(dve, name, nth, turn):
            dve.wait_ge(*after(f"{name} squares 11"))
            rs = rms_of(dve, name, small[:, 40:44], 44, RMS_EPS)
            dve.wait_ge(pre_gain, 16 * (nth + 1))

            def unit(t, n):
                k = slice(512 * n, 512 * n + 512)
                nc.vector.scalar_tensor_tensor(x_norm[:, t, k], h[:, t, k], rs[:, 0, t:t + 1], normw[:, 0, k],
                                               ALU.mult, ALU.mult).then_inc(*V(f"{name} unit {t}{n}"))

            turn_behind(dve, unit, turn)

        def post_scalar(act, name, done):
            for t in range(TT):
                act.wait_ge(*done(t))
                for b in range(2):
                    nc.scalar.activation(sq_out[:, t, 512 * b:512 * b + 512], acc[t][b][:, :], ACT.Square,
                                         accum_out=small[:, 52 + 2 * t + b:53 + 2 * t + b])\
                        .then_inc(*S(f"{name} post squares {t}{b}"))

        def post_vector(dve, name, c, eps, nth):
            dve.wait_ge(post_gain, 16 * (nth + 1))

            def gained(t, b):
                k = slice(512 * b, 512 * b + 512)
                nc.vector.tensor_tensor(x_norm[:, t, k], acc[t][b][:, :], normw[:, 1, k], ALU.mult)\
                    .then_inc(*V(f"{name} gained {t}{b}"))

            for b in range(2):
                dve.wait_ge(*after(f"{name} post squares 0{b}"))
                gained(0, b)
            dve.wait_ge(*after(f"{name} post squares 11"))
            rs = rms_of(dve, name, small[:, 52:56], 56, eps, c, [lambda: gained(1, 0), lambda: gained(1, 1)])
            for t in range(TT):
                for b in range(2):
                    k = slice(512 * b, 512 * b + 512)
                    dve.wait_ge(*after(f"{name} gained {t}{b}"))
                    nc.vector.scalar_tensor_tensor(h[:, t, k], x_norm[:, t, k], rs[:, 0, t:t + 1], h[:, t, k],
                                                   ALU.mult, ALU.add).then_inc(*V(f"{name} {t}{b}"))

        def two_load(sp):
            W = lambda n: A[n].rearrange("a k n -> (a k) n")
            gain_load(sp, 0, "ffn1_pre_g_2", None)

            def first_parameters():
                gain_load(sp, 1, "ffn1_post_g_2", None)
                for n, (w, k) in enumerate((("conv_w_2", 32), ("conv_b_2", 8), ("lru_b_a_2", 8), ("lru_b_x_2", 8), ("lru_lambda_2", 8))):
                    at0 = (0, 32, 40, 48, 56)[n]
                    src = A[w].rearrange("a k (c p) -> (a k c) p", p=P) if n == 0 else A[w].rearrange("a (c p) -> (a c) p", p=P)
                    nc.sync.dma_start(rows64[at0:at0 + k, :], src).then_inc(params[1], 16)
                nc.sync.dma_start(sinks, A["attn_sinks_2"].rearrange("a n -> (a n)").partition_broadcast(P)).then_inc(params[1], 16)

            ff_load(sp, 0, W("ffn1_w_gu_2"), 0, W("ffn1_w_down_2"), 0, first_parameters)
            gain_load(sp, 0, "mix_pre_g_2", "p1 unit 11")
            sp.wait_ge(*after("lru zeros"))
            for m, w in enumerate(("lru_w_a_2", "lru_w_x_2")):
                for b in range(2):
                    nc.sync.dma_start(lru_w[64 * b:64 * b + 64, m, :, 64 * b:64 * b + 64],
                                      A[w].rearrange("a (c b) k d -> b k (a c) d", b=2)[b]).then_inc(params[2], 16)
            for c in IN_ORDER:
                for half in range(2):
                    load_slab(sp, first[c] + half, 0, col_parts(W("w_in_2"), 0, 4 * half, 4, [(IN_COL[c], 512)]))
            gain_load(sp, 1, "mix_post_g_2", "f1 gained 11")
            gain_load(sp, 0, "ffn2_pre_g_2", "p2 unit 11")
            for g, w in ((G_PL, "w_proj_lru_2"), (G_PA, "w_proj_attn_2"), (G_OUT2, "w_out_2")):
                for n in range(4):
                    load_slab(sp, g + n, 0, wide_parts(W(w), 2 * P * n))
            ff_load(sp, G_FF2, W("ffn2_w_gu_2"), 0, W("ffn2_w_down_2"), 0)
            gain_load(sp, 1, "ffn2_post_g_2", "mx gained 11")
            for t in range(TT):
                sp.wait_ge(*after(f"f2 {t}1"))
                nc.sync.dma_start(out[0, P * t:P * t + P, :], h[:, t, :]).then_inc(stored, 16)
            sp.wait_ge(stored, 32 + 16)

        def window_tensor(pe, g, stage):
            if stage == 0:
                if g == 0:
                    pe.wait_ge(*after("q turned in place 3"))
                    pe.wait_ge(*after("k turned in place 1"))
                else:
                    pe.wait_ge(*after(f"attn {g - 1} 1"))
                for x in range(4):
                    hh = 4 * g + x
                    u = slice(64 * (x % 2), 64 * (x % 2) + 64)
                    b, c = 4 + 2 * (x % 2), x // 2
                    nc.tensor.matmul(bank[b][:, P * c:P * c + P], qT2[u, hh // 2, 0:P], kT2[u, g, 0:P], start=True, stop=True)
                    m = nc.tensor.matmul(bank[b + 1][:, 256 * c:256 * c + 256], qT2[u, hh // 2, P:2 * P], kT2[u, g, :],
                                         start=True, stop=True)
                m.then_inc(*T(f"scores {g}"))
            if stage == 1:
                for n in range(3):
                    for b in range(4):
                        t, x, kt = (0, b, 0) if n == 0 else (1, 2 * (n - 1) + b // 2, b % 2)
                        pe.wait_ge(*after(f"probs {g} {t} {x}"))
                        m = nc.tensor.transpose(bank[4 + n][:, P * b:P * b + P], scores[t][:, g % 2, x, tokens(kt)], ident)
                    m.then_inc(*T(f"probs turned {g} {n}"))
            if stage == 2:
                for n in range(3):
                    pe.wait_ge(*after(f"probs_T {g} {n}"))
                for t in range(TT):
                    for x in range(4):
                        o = bank[7][:, 256 * t + 64 * x:256 * t + 64 * x + 64]
                        blocks = [(x, 0)] if t == 0 else [(4 + 2 * x, 0), (5 + 2 * x, 1)]
                        for i, (b, kt) in enumerate(blocks):
                            m = nc.tensor.matmul(o, probs_T[:, b, :], v_win[:, kt, 64 * g:64 * g + 64],
                                                 start=i == 0, stop=i == len(blocks) - 1)
                m.then_inc(*T(f"attn out {g}"))

        def two_tensor(pe):
            ff_tensor(pe, 0, 0, "f1 out", ("ua", x_norm, lambda t, n: after(f"p1 unit {t}{n}")))
            pe.wait_ge(params[1], 96)
            turn_tensor(pe, "ub", x_norm, lambda t, n: after(f"p2 unit {t}{n}"))
            nc.tensor.transpose(bank[4][:, 0:64], rows64, ident[0:64, 0:64]).then_inc(*T("channel rows"))
            pe.wait_ge(*after("ub lo 3"))

            def half_chunk(c, half, free=None):
                if free:
                    pe.wait_ge(*after(free))
                g = first[c] + half
                await_slab(pe, g)
                if c[0] in "xg":
                    m = channel_slab(g, 4 * half, pair[c])
                else:
                    m = token_slab(g, 4 * half, 4, 512, [b[:, :] for b in pair[c]])
                m.then_inc(slab_used, 1)

            def chunk(c, free):
                half_chunk(c, 0, free)
                half_chunk(c, 1)

            chunk("x0", None)
            chunk("x1", None)
            chunk("q0", "evacuated x0 1")
            chunk("q1", "evacuated x1 1")
            pe.wait_ge(params[2], 64)
            for m in range(2):
                for b in range(4):
                    if m:
                        pe.wait_ge(*after(f"lru tanh 0 {2 * b + 1}"))
                    for x in range(2):
                        c = 2 * b + x
                        pe.wait_ge(*after(f"lru conv {c} 3"))
                        i = nc.tensor.matmul(bank[4 + b][:, 256 * x:256 * x + 256], lru_w[:, m, c, :], lru_x[:, c, :],
                                             start=True, stop=True)
                    i.then_inc(*T(f"lru gates {m} {b}"))
            chunk("kv", "rotated q0 1")
            half_chunk("g0", 0, "rotated q1 1")
            for n in range(4):
                pe.wait_ge(*after("rotated q1 1"))
                pe.wait_ge(*after(f"lru tanh 1 {2 * n + 1}"))
                for x in range(2):
                    for t in range(TT):
                        src = q_rot[:, t, 4 * n + 2 * x:4 * n + 2 * x + 2, :].rearrange("p h n -> p (h n)")
                        m = nc.tensor.transpose(bank[4 + n][:, 256 * x + P * t:256 * x + P * t + P], src, ident)
                m.then_inc(*T(f"q turned {n}"))
            half_chunk("g0", 1)
            pe.wait_ge(*after("k doubled"))
            for n in range(2):
                pe.wait_ge(*after(f"q turned in place {n}"))
                for x in range(2):
                    for t in range(TT):
                        src = k_rot[:, t, 2 * n + x, :, :].rearrange("p b n -> p (b n)")
                        m = nc.tensor.transpose(bank[4 + n][:, 256 * x + P * t:256 * x + P * t + P], src, ident)
                m.then_inc(*T(f"k turned {n}"))
            slabs = [(c, half) for c in IN_ORDER[6:] for half in range(2)]
            free = {"g1": "v in place 1", "l0": "gelu g0 1", "l1": "gelu g1 1", "a0": "gate l0 1", "a1": "gate l1 1"}
            for g in range(KVH):
                for stage in range(3):
                    window_tensor(pe, g, stage)
                    if slabs:
                        c, half = slabs.pop(0)
                        half_chunk(c, half, None if half else free[c])
            assert not slabs
            pe.wait_ge(*after("lru lo"))
            pe.wait_ge(*after("gate a0 1"))
            pe.wait_ge(*after("gate a1 1"))
            wide_product(pe, G_PL, 4, (xhi, xlo), "lru out")
            turn_tensor(pe, "uc", y_attn, lambda t, n: after(f"attn 3 {t}"), (slab_used, G_PL + 4))
            pe.wait_ge(*after("uc lo 3"))
            pe.wait_ge(*after("merged lru 3"))
            wide_product(pe, G_PA, 4, (xhi, xlo), "attn proj out")
            turn_tensor(pe, "ud", merged, lambda t, n: after(f"merged {2 * t + n}"))
            pe.wait_ge(*after("ud lo 3"))
            wide_product(pe, G_OUT2, 4, (xhi, xlo), "mix out")
            ff_tensor(pe, G_FF2, 1, "f2 out", ("ue", x_norm, lambda t, n: after(f"p3 unit {t}{n}")))

        def two_scalar(act):
            act_ = nc.scalar.activation
            copy = lambda o, i: nc.scalar.activation(o, i, ACT.Copy)
            two = lambda b: b[:, :].rearrange("p (c n) -> p c n", c=2)
            made = [G_IN + 2]

            def hi_to(n):
                while made[0] < n:
                    make_hi(act, made[0])
                    made[0] += 1

            pre_scalar(act, "p1", None)
            turn_scalar(act, "ua")
            make_hi(act, 0)
            make_hi(act, 1)
            make_hi(act, 2)
            ff_scalar(act, 0, 0, True)
            post_scalar(act, "f1", acc_ready("f1 out", G_IN - 1))
            pre_scalar(act, "p2", "f1")
            turn_scalar(act, "ub")
            hi_to(G_IN + 3)
            act.wait_ge(*after("channel rows"))
            copy(pc, bank[4][:, 0:64]).then_inc(*S("channel rows in place"))
            act.wait_ge(*after("channel rows in place"))
            act_(lam_t[:, 0:8], pc[:, 56:64], ACT.Abs).then_inc(*S("lam abs"))
            act.wait_ge(*after("lam abs"))
            act_(lam_t[:, 0:8], lam_t[:, 0:8], ACT.Exp, scale=-1.0).then_inc(*S("lam exp"))
            act.wait_ge(*after("lam exp"))
            act_(lam_t[:, 0:8], lam_t[:, 0:8], ACT.Ln, bias=1.0).then_inc(*S("lam ln"))
            for c, k in (("x0", 0), ("x1", 4)):
                hi_to(first[c] + 4)
                for b in range(2):
                    act.wait_ge(*ready[c])
                    copy(lru_in[:, k + 2 * b:k + 2 * b + 2, 3:3 + SEQ], two(pair[c][b])).then_inc(*S(f"evacuated {c} {b}"))
            hi_to(first["q1"] + 4)
            for m, dst in enumerate((lru_a, lru_i)):
                for c in range(LT):
                    act.wait_ge(*after(f"lru gates {m} {c // 2}"))
                    if m == 0 and c == 0:
                        act.wait_ge(*after("half biases"))
                        act.wait_ge(*after("lru conv 7 3"))
                    act_(dst[:, c, :], bank[4 + c // 2][:, 256 * (c % 2):256 * (c % 2) + 256], ACT.Tanh,
                         bias=half_b[:, 8 * m + c:8 * m + c + 1], scale=0.5).then_inc(*S(f"lru tanh {m} {c}"))
                if m == 0:
                    hi_to(first["kv"] + 3)
            act.wait_ge(*after("lru c"))
            for c in range(LT):
                act_(lru_m[:, c, :], lru_a[:, c, :], ACT.Tanh, bias=lru_c[:, c:c + 1], scale=lru_c[:, c:c + 1])\
                    .then_inc(*S(f"lru tanh log a {c}"))
            hi_to(first["kv"] + 4)
            for c in range(LT):
                act.wait_ge(*after(f"lru tanh log a {c}"))
                act_(lru_a[:, c, :], lru_a[:, c, :], ACT.Exp, bias=lru_c[:, c:c + 1], scale=lru_c[:, c:c + 1])\
                    .then_inc(*S(f"lru a {c}"))
            act.wait_ge(*ready["kv"])
            for t in range(TT):
                copy(v_win[:, t, :], pair["kv"][t][:, KVW:2 * KVW]).then_inc(*S(f"v copied {t}"))
            hi_to(first["g0"] + 3)
            for n in range(4):
                act.wait_ge(*after(f"q turned {n}"))
                copy(qT2[:, 2 * n:2 * n + 2, :], two(bank[4 + n])).then_inc(*S(f"q turned in place {n}"))
            hi_to(first["g0"] + 5)
            for n in range(2):
                act.wait_ge(*after(f"k turned {n}"))
                copy(kT2[:, 2 * n:2 * n + 2, :], two(bank[4 + n])).then_inc(*S(f"k turned in place {n}"))
            act.wait_ge(*after("lru mult squared"))
            act_(lru_m[:, :, :], lru_m[:, :, :], ACT.Sqrt).then_inc(*S("lru mult"))

            def gelu(c, k):
                for b in range(2):
                    act.wait_ge(*ready[c])
                    if k:
                        act.wait_ge(*after(f"lru y {2 * b + 1}"))
                    act_(gelu_g[:, b, :, :], two(pair[c][b]), ACT.Gelu_apprx_tanh).then_inc(*S(f"gelu {c} {b}"))

            def gate(c, dst, k):
                for b in range(2):
                    act.wait_ge(*ready[c])
                    if k == 0 and b == 0 and c[0] in "l":
                        act.wait_ge(*after("lru scanned 7"))
                    act_(dst[:, b, k:k + 512], pair[c][b][:, :], ACT.Tanh, scale=0.5).then_inc(*S(f"gate {c} {b}"))

            gelu("g0", 0)
            for g in range(KVH):
                for t in range(TT):
                    act.wait_ge(*after(f"minus max {g} {t}"))
                    for x in range(4):
                        k = 4 * t + x
                        act_(scores[t][:, g % 2, x, :], scores[t][:, g % 2, x, :], ACT.Exp,
                             bias=small[:, 208 + 8 * (g % 2) + k:209 + 8 * (g % 2) + k],
                             accum_out=small[:, 224 + 8 * (g % 2) + k:225 + 8 * (g % 2) + k]).then_inc(*S(f"probs {g} {t} {x}"))
                act.wait_ge(*after(f"sink less max {g}"))
                act_(small[:, 240 + 8 * (g % 2):248 + 8 * (g % 2)], small[:, 240 + 8 * (g % 2):248 + 8 * (g % 2)], ACT.Exp)\
                    .then_inc(*S(f"sink exp {g}"))
                hi_to(min(first["g1"] + 3 + 3 * g + 1, G_PL + 3))
                for n in range(3):
                    act.wait_ge(*after(f"probs turned {g} {n}"))
                    if g and n == 0:
                        act.wait_ge(*after(f"attn out {g - 1}"))
                    copy(probs_T[:, 4 * n:4 * n + 4, :], bank[4 + n][:, :].rearrange("p (b n) -> p b n", b=4))\
                        .then_inc(*S(f"probs_T {g} {n}"))
                if g == 0:
                    gelu("g1", 1)
                if g == 1:
                    gate("l0", gate_l, 0)
                if g == 2:
                    gate("l1", gate_l, 512)
                hi_to(min(first["g1"] + 3 + 3 * g + 3, G_PL + 3))
            gate("a0", gate_a, 0)
            hi_to(G_PL + 2)
            gate("a1", gate_a, 512)
            act.wait_ge(*after("lru y 7"))
            act.wait_ge(slab_used, G_PL)
            for b in range(4):
                copy(xhi[:, 2 * b:2 * b + 2, :], lru_h[:, 2 * b:2 * b + 2, :]).then_inc(*S(f"lru hi {b}"))
            hi_to(G_PA + 2)
            turn_scalar(act, "uc")
            hi_to(G_OUT2 + 2)
            turn_scalar(act, "ud")
            hi_to(G_FF2 + 2)
            post_scalar(act, "mx", acc_ready("mix out", G_FF2 - 1))
            pre_scalar(act, "p3", "mx")
            turn_scalar(act, "ue")
            hi_to(G_FF2 + 3)
            ff_scalar(act, G_FF2, 1, False)
            post_scalar(act, "f2", acc_ready("f2 out", G_FF2 + 3 * FF_STEPS - 1))

        def two_vector(dve):
            TTn, TS, STT = nc.vector.tensor_tensor, nc.vector.tensor_scalar, nc.vector.scalar_tensor_tensor
            made = [G_IN + 2]

            def lo_to(n):
                while made[0] < n:
                    make_lo(dve, lo_dve, made[0])
                    made[0] += 1

            pre_vector(dve, "p1", 0, "ua")
            for g in range(RING):
                make_lo(dve, lo_dve, g)
            ff_vector(dve, 0, 0, True)
            post_vector(dve, "f1", 0.5, RMS_EPS, 0)
            pre_vector(dve, "p2", 1, "ub")
            lo_to(G_IN + 3)
            dve.wait_ge(*after("channel rows in place"))
            TS(half_b, pc[:, 40:56], 0.5, None, ALU.mult).then_inc(*V("half biases"))
            TS(lam_t[:, 8:16], pc[:, 56:64], -1.0, 0.0, ALU.mult, ALU.max).then_inc(*V("lam relu"))
            dve.wait_ge(*after("lam relu"))
            dve.wait_ge(*after("lam ln"))
            TTn(lru_c, lam_t[:, 0:8], lam_t[:, 8:16], ALU.add).then_inc(*V("lam softplus"))
            dve.wait_ge(*after("lam softplus"))
            TS(lru_c, lru_c, -LRU_C / 2, None, ALU.mult).then_inc(*V("lru c"))
            dve.wait_ge(*after("lru pads"))
            for n, c in enumerate(("x0", "x1")):
                lo_to(first[c] + 4)
                for b in range(2):
                    dve.wait_ge(*after(f"evacuated {c} {b}"))
                    for k in range(CONV):
                        for x in (4 * n + 2 * b, 4 * n + 2 * b + 1):
                            tap, src = pc[:, 8 * k + x:8 * k + x + 1], lru_in[:, x, k:k + SEQ]
                            if k == 0:
                                i = TS(lru_x[:, x, :], src, tap, pc[:, 32 + x:33 + x], ALU.mult, ALU.add)
                            else:
                                dve.wait_ge(*after(f"lru conv {x} {k - 1}"))
                                i = STT(lru_x[:, x, :], src, tap, lru_x[:, x, :], ALU.mult, ALU.add)
                            i.then_inc(*V(f"lru conv {x} {k}"))

            def rotate(src, heads, out1, out2, cos, sin, name, t, k):
                hf = HD // 2
                c = cos.unsqueeze(1).to_broadcast([P, heads, hf])
                s = sin.unsqueeze(1).to_broadcast([P, heads, hf])
                a, b = rot_t[:, 2 * k, 0:heads, :], rot_t[:, 2 * k + 1, 0:heads, :]
                TTn(out1, src[:, :, 0:hf], c, ALU.mult).then_inc(*V(f"{name} a {t}"))
                TTn(a, src[:, :, hf:HD], s, ALU.mult).then_inc(*V(f"{name} b {t}"))
                TTn(out2, src[:, :, hf:HD], c, ALU.mult).then_inc(*V(f"{name} c {t}"))
                TTn(b, src[:, :, 0:hf], s, ALU.mult).then_inc(*V(f"{name} d {t}"))
                dve.wait_ge(*after(f"{name} b {t}"))
                TTn(out1, out1, a, ALU.subtract).then_inc(*V(f"{name} e {t}"))
                dve.wait_ge(*after(f"{name} d {t}"))
                TTn(out2, out2, b, ALU.add).then_inc(*V(f"rotated {name} {t}"))

            hf = HD // 2
            cs = [tab[:, c:c + TT * hf].rearrange("p (t n) -> p t n", t=TT) for c in (C_COS, C_SIN)]
            for n, c in enumerate(("q0", "q1")):
                lo_to(first[c] + 4)
                dve.wait_ge(*ready[c])
                for t in range(TT):
                    o = q_rot[:, t, 8 * n:8 * n + 8, :]
                    if n or t:
                        dve.wait_ge(*after("rotated q0 0" if n == 0 else f"rotated {('q0 1', 'q1 0')[t]}"))
                    rotate(pair[c][t][:, :].rearrange("p (h n) -> p h n", n=HD), 8, o[:, :, 0:hf], o[:, :, hf:HD],
                           cs[0][:, t, :], cs[1][:, t, :], c, t, t)
            lo_to(first["kv"] + 4)
            for t in range(TT):
                dve.wait_ge(*after(f"v copied {t}"))
                dve.wait_ge(*after("rotated q1 1" if t == 0 else "rotated kv 0"))
                o = k_rot[:, t, :, 0, :]
                rotate(pair["kv"][t][:, 0:KVW].rearrange("p (h n) -> p h n", n=HD), KVH, o[:, :, 0:hf], o[:, :, hf:HD],
                       cs[0][:, t, :], cs[1][:, t, :], "kv", t, t)
            dve.wait_ge(*after("rotated kv 1"))
            nc.vector.tensor_copy(k_rot[:, 0, :, 1, :], k_rot[:, 0, :, 0, :]).then_inc(*V("v in place 1"))
            nc.vector.tensor_copy(k_rot[:, 1, :, 1, :], k_rot[:, 1, :, 0, :]).then_inc(*V("k doubled"))
            lo_to(first["g0"] + 3)
            dve.wait_ge(*after("lru a 7"))
            for b in range(2):
                c = slice(4 * b, 4 * b + 4)
                TTn(lru_h[:, c, :], lru_a[:, c, :], lru_a[:, c, :], ALU.mult).then_inc(*V(f"a squared {b}"))
                STT(lru_i[:, c, :], lru_i[:, c, :], 1.0, lru_x[:, c, :], ALU.add, ALU.mult).then_inc(*V(f"i x {b}"))
                dve.wait_ge(*after(f"a squared {b}"))
                STT(lru_m[:, c, :], lru_h[:, c, :], 1.0, lru_m[:, c, :], ALU.add, ALU.mult).then_inc(*V(f"expm1 {b}"))
                dve.wait_ge(*after(f"expm1 {b}"))
                TS(lru_m[:, c, :], lru_m[:, c, :], -1.0, 0.0, ALU.mult, ALU.max).then_inc(*V("lru mult squared" if b else "lru ms 0"))
            lo_to(first["g0"] + 5)
            dve.wait_ge(*after("lru mult"))
            for c in range(LT):
                STT(lru_i[:, c, :], lru_i[:, c, :], 0.5, lru_m[:, c, :], ALU.mult, ALU.mult).then_inc(*V(f"lru b {c}"))
            for c in range(LT):
                dve.wait_ge(*after(f"lru b {c}"))
                nc.vector.tensor_tensor_scan(lru_h[:, c, :], lru_a[:, c, :], lru_i[:, c, :], 0.0, ALU.mult, ALU.add)\
                    .then_inc(*V(f"lru scanned {c}"))

            def gated_y(c, k):
                for b in range(2):
                    dve.wait_ge(*after(f"gelu {c} {b}"))
                    for x in range(2):
                        j = k + 2 * b + x
                        if x == 0:
                            dve.wait_ge(*after(f"lru scanned {j + 1}"))
                        TTn(lru_h[:, j, :], lru_h[:, j, :], gelu_g[:, b, x, :], ALU.mult).then_inc(*V(f"lru y {j}"))

            def window(g):
                k = 8 * (g % 2)
                mx, nm = small[:, 192 + k:200 + k], small[:, 208 + k:216 + k]
                sm_, sk = small[:, 224 + k:232 + k], small[:, 240 + k:248 + k]
                rec = small[:, 256 + k:264 + k]
                scale = HD ** -0.5
                dve.wait_ge(*after(f"scores {g}"))
                if g == 0:
                    dve.wait_ge(*after("lru scanned 7"))
                for b in range(2):
                    STT(scores[0][:, g % 2, b::2, :], bank[4 + 2 * b][:, 0:256].rearrange("p (h n) -> p h n", h=2), scale,
                        tab[:, C_NC + P:C_NC + 2 * P].unsqueeze(1).to_broadcast([P, 2, P]), ALU.mult, ALU.add)\
                        .then_inc(*V(f"masked {g} 0 {b}"))
                dve.wait_ge(*after(f"masked {g} 0 1"))
                nc.vector.tensor_reduce(mx[:, 0:4], scores[0][:, g % 2], AX.X, ALU.max).then_inc(*V(f"max {g} 0"))
                for b in range(2):
                    STT(scores[1][:, g % 2, b::2, :], bank[5 + 2 * b][:, :].rearrange("p (h n) -> p h n", h=2), scale,
                        tab[:, C_NW:C_NW + 2 * P].unsqueeze(1).to_broadcast([P, 2, 2 * P]), ALU.mult, ALU.add)\
                        .then_inc(*V(f"masked {g} 1 {b}"))
                dve.wait_ge(*after(f"masked {g} 1 1"))
                nc.vector.tensor_reduce(mx[:, 4:8], scores[1][:, g % 2], AX.X, ALU.max).then_inc(*V(f"max {g} 1"))
                sink = sinks[:, 4 * g:4 * g + 4]
                for t in range(TT):
                    u = slice(4 * t, 4 * t + 4)
                    dve.wait_ge(*after(f"max {g} {t}"))
                    TTn(mx[:, u], mx[:, u], sink, ALU.max).then_inc(*V(f"max with sink {g} {t}"))
                    dve.wait_ge(*after(f"max with sink {g} {t}"))
                    TS(nm[:, u], mx[:, u], -1.0, None, ALU.mult).then_inc(*V(f"minus max {g} {t}"))
                    TTn(sk[:, u], sink, mx[:, u], ALU.subtract).then_inc(*V(f"sink less max {g}" if t else f"sink less max {g} 0"))
                return sm_, sk, rec

            def window_end(g, sm_, sk, rec):
                dve.wait_ge(*after(f"sink exp {g}"))
                TTn(sm_, sm_, sk, ALU.add).then_inc(*V(f"den {g}"))
                dve.wait_ge(*after(f"den {g}"))
                nc.vector.reciprocal(rec, sm_).then_inc(*V(f"rec {g}"))
                dve.wait_ge(*after(f"rec {g}"))
                dve.wait_ge(*after(f"attn out {g}"))
                for t in range(TT):
                    TTn(y_attn[:, t, 256 * g:256 * g + 256].rearrange("p (h n) -> p h n", h=4),
                        bank[7][:, 256 * t:256 * t + 256].rearrange("p (h n) -> p h n", h=4),
                        rec[:, 4 * t:4 * t + 4].unsqueeze(2).to_broadcast([P, 4, HD]), ALU.mult)\
                        .then_inc(*V(f"attn {g} {t}"))

            for g in range(KVH):
                w = window(g)
                if g == 0:
                    gated_y("g0", 0)
                lo_to(min(first["g1"] + 3 + 3 * g + 1, G_PL + 3))
                if g == 0:
                    gated_y("g1", 4)
                lo_to(min(first["g1"] + 3 + 3 * g + 2, G_PL + 3))
                window_end(g, *w)
                lo_to(min(first["g1"] + 3 + 3 * g + 3, G_PL + 3))
            lo_to(G_PL + 2)
            for b in range(4):
                dve.wait_ge(*after(f"lru hi {b}"))
                TTn(xlo[:, 2 * b:2 * b + 2, :], lru_h[:, 2 * b:2 * b + 2, :], xhi[:, 2 * b:2 * b + 2, :].bitcast(F32),
                    ALU.subtract).then_inc(*V("lru lo" if b == 3 else f"lru lo {b}"))
            lo_to(G_PA + 2)
            turn_order = acc_ready("lru out", G_PA - 1)
            for n in range(4):
                t, c = n // 2, slice(512 * (n % 2), 512 * (n % 2) + 512)
                dve.wait_ge(*turn_order(t))
                STT(merged[:, t, c], gate_l[:, t, c], 1.0, acc[t][n % 2][:, :], ALU.add, ALU.mult).then_inc(*V(f"merged lru {n}"))
            turn_vector(dve, "uc")
            lo_to(G_OUT2 + 2)
            for n in range(4):
                t, c = n // 2, slice(512 * (n % 2), 512 * (n % 2) + 512)
                dve.wait_ge(*acc_ready("attn proj out", G_OUT2 - 1)(t))
                STT(gate_a[:, t, c], gate_a[:, t, c], 1.0, acc[t][n % 2][:, :], ALU.add, ALU.mult).then_inc(*V(f"gated attn {n}"))
                dve.wait_ge(*after(f"gated attn {n}"))
                TTn(merged[:, t, c], merged[:, t, c], gate_a[:, t, c], ALU.add).then_inc(*V(f"merged {n}"))
            turn_vector(dve, "ud")
            lo_to(G_FF2 + 2)
            post_vector(dve, "mx", 1.0, 4 * RMS_EPS, 1)
            pre_vector(dve, "p3", 2, "ue")
            lo_to(G_FF2 + 3)
            ff_vector(dve, G_FF2, 1, False)
            post_vector(dve, "f2", 0.5, RMS_EPS, 2)

        def two_gpsimd(pool):
            for g in range(RING):
                make_lo(pool, lo_pool, g)
            nc.gpsimd.memset(lru_w[:, :, :, :], 0.0).then_inc(*G("lru zeros"))
            nc.gpsimd.memset(lru_in[:, :, 0:3], 0.0).then_inc(*G("lru pads"))
            ff_gpsimd(pool, 0, True)
            for g in range(G_IN + 3, G_FF2 + 3):
                make_lo(pool, lo_pool, g)
            ff_gpsimd(pool, G_FF2, False)

        with nc.Block() as block:
            st.start("two")

            @block.sync
            def _(sp):
                two_load(sp)

            @block.tensor
            def _(pe):
                two_tensor(pe)

            @block.scalar
            def _(act):
                two_scalar(act)

            @block.vector
            def _(dve):
                two_vector(dve)

            @block.gpsimd
            def _(pool):
                two_gpsimd(pool)
        return st.found


_INS = ["x", "p", "positions", "ffa_w_in", "ffa_w_out", "mix_w_in", "gdn_conv_w", "gdn_a_log", "gdn_dt_bias",
        "gdn_norm_w", "mla_q_norm_w", "mla_kv_norm_w", "mla_w_uq", "mla_w_ukv", "mix_w_o", "ffb_w_in", "ffb_w_out",
        "ln_g", "ln_b", "ple_w_gate", "ple_w_proj", "ffn1_pre_g_2", "ffn1_w_gu_2", "ffn1_w_down_2", "ffn1_post_g_2",
        "mix_pre_g_2", "w_in_2", "conv_w_2", "conv_b_2", "lru_w_a_2", "lru_b_a_2", "lru_w_x_2", "lru_b_x_2",
        "lru_lambda_2", "attn_sinks_2", "w_proj_lru_2", "w_proj_attn_2", "w_out_2", "mix_post_g_2",
        "ffn2_pre_g_2", "ffn2_w_gu_2", "ffn2_w_down_2", "ffn2_post_g_2"]


def program(nc, shapes, known):
    A = {n: nc.dram_tensor(f"in_{n}", shape, dtype, kind="ExternalInput").ap() for n, (shape, dtype) in shapes.items()}
    out = nc.dram_tensor("out_0", (1, SEQ, D), F32, kind="ExternalOutput").ap()
    return build_program(nc, A, out, known)


def kernel(**inputs):
    import concourse.bacc as bacc
    from concourse.bass_utils import run_bass_kernel_spmd

    arrays = {n: np.ascontiguousarray(inputs[n]) for n in _INS}
    arrays["tables"] = shape_tables()
    shapes = {n: (a.shape, mybir.dt.from_np(a.dtype)) for n, a in arrays.items()}
    counted = program(bacc.Bacc("TRN2", target_bir_lowering=False, num_devices=1), shapes, {})
    nc = bacc.Bacc("TRN2", target_bir_lowering=False, num_devices=1)
    program(nc, shapes, counted)
    r = run_bass_kernel_spmd(nc, [{f"in_{n}": a for n, a in arrays.items()}], core_ids=[0])
    return r.results[0]["out_0"]
```
